# Optimizing a Trainium2 kernel written in Bass

```python
import math
import jax, jax.numpy as jnp
from jax import lax
import numpy as np

D_MODEL = 1024
BATCH = 1
SEQ = 256
DEPTH = 1

CHUNK = 64
MIX_A_WIDTH = D_MODEL // 2
MIX_B_WIDTH = D_MODEL - MIX_A_WIDTH
A_GROUPS = 8
A_GROUP_DIM = MIX_A_WIDTH // A_GROUPS
A_BLOCK = 128
B_HEADS = 8
B_HEAD_DIM = MIX_B_WIDTH // B_HEADS
B_LEFT_CHUNKS = 8
B_BAND = (B_LEFT_CHUNKS + 1) * CHUNK
REL_CLIP = 128
PEER_HEADS = 8
PEER_NKEYS = 128
PEER_EXPERTS = PEER_NKEYS * PEER_NKEYS
PEER_QDIM = 256
PEER_HALF = PEER_QDIM // 2
PEER_TOPK = 16
PEER_TOKEN_BLOCK = 128
IN_COLS = 2 * MIX_A_WIDTH + 3 * MIX_B_WIDTH
EPS = 1e-6
NEG_INF = -1e30


def rms_norm(x, g):
    xf = x.astype(jnp.float32)
    y = xf * lax.rsqrt(jnp.mean(xf * xf, axis=-1, keepdims=True) + EPS)
    return (y * g.astype(jnp.float32)).astype(x.dtype)

def gmlp_spatial_gating(u, v, norm_g, w_s, b_s):
    bsz, s, _ = u.shape
    u = jax.nn.gelu(u)
    v = rms_norm(jax.nn.gelu(v), norm_g)
    nblk = s // A_BLOCK
    v = v.reshape(bsz, nblk, A_BLOCK, A_GROUPS, A_GROUP_DIM)
    pos = jnp.arange(A_BLOCK)
    mask = (pos[None, :] // CHUNK) <= (pos[:, None] // CHUNK)
    w = jnp.where(mask[None], w_s, jnp.zeros_like(w_s)).astype(v.dtype)
    sp = jnp.einsum('gij,bnjgc->bnigc', w, v) + b_s.T.astype(v.dtype)[None, None, :, :, None]
    return u * sp.reshape(bsz, s, MIX_A_WIDTH)

def banded_chunk_attention(q, k, v, q_g, k_g, rel_bias):
    bsz, s, _ = q.shape
    nc = s // CHUNK
    pad = B_LEFT_CHUNKS * CHUNK
    q = rms_norm(q.reshape(bsz, nc, CHUNK, B_HEADS, B_HEAD_DIM), q_g)
    k = rms_norm(k.reshape(bsz, s, B_HEADS, B_HEAD_DIM), k_g)
    v = v.reshape(bsz, s, B_HEADS, B_HEAD_DIM)
    padw = ((0, 0), (pad, 0), (0, 0), (0, 0))
    kp = jnp.pad(k, padw).reshape(bsz, nc + B_LEFT_CHUNKS, CHUNK, B_HEADS, B_HEAD_DIM)
    vp = jnp.pad(v, padw).reshape(bsz, nc + B_LEFT_CHUNKS, CHUNK, B_HEADS, B_HEAD_DIM)
    band_idx = jnp.arange(nc)[:, None] + jnp.arange(B_LEFT_CHUNKS + 1)[None, :]
    kb = kp[:, band_idx].reshape(bsz, nc, B_BAND, B_HEADS, B_HEAD_DIM)
    vb = vp[:, band_idx].reshape(bsz, nc, B_BAND, B_HEADS, B_HEAD_DIM)
    scores = jnp.einsum('bcihd,bcjhd->bhcij', q, kb).astype(jnp.float32) * (B_HEAD_DIM ** -0.5)
    qi = jnp.arange(CHUNK)[:, None] + pad
    kj = jnp.arange(B_BAND)[None, :]
    rel_idx = jnp.clip(qi - kj, -REL_CLIP, REL_CLIP) + REL_CLIP
    bias = rel_bias.astype(jnp.float32)[:, rel_idx]
    valid = kj >= (pad - jnp.arange(nc)[:, None] * CHUNK)
    scores = scores + bias[None, :, None]
    scores = jnp.where(valid[None, None, :, None, :], scores, NEG_INF)
    p = jax.nn.softmax(scores, axis=-1).astype(v.dtype)
    out = jnp.einsum('bhcij,bcjhd->bcihd', p, vb)
    return out.reshape(bsz, s, MIX_B_WIDTH)

def peer_ffn(x, w_query, sub_keys, expert_u, expert_v):
    bsz, s, d = x.shape
    tokens = x.reshape(-1, PEER_TOKEN_BLOCK, d)

    def block(xb):
        q = (xb @ w_query).reshape(PEER_TOKEN_BLOCK, PEER_HEADS, 2, PEER_HALF)
        sc = jnp.einsum('thpd,hpkd->thpk', q, sub_keys).astype(jnp.float32)
        s_top, i_top = lax.top_k(sc, PEER_TOPK)
        cand = s_top[:, :, 0, :, None] + s_top[:, :, 1, None, :]
        cand_idx = i_top[:, :, 0, :, None] * PEER_NKEYS + i_top[:, :, 1, None, :]
        cand = cand.reshape(PEER_TOKEN_BLOCK, PEER_HEADS, PEER_TOPK * PEER_TOPK)
        cand_idx = cand_idx.reshape(PEER_TOKEN_BLOCK, PEER_HEADS, PEER_TOPK * PEER_TOPK)
        best, pos = lax.top_k(cand, PEER_TOPK)
        eidx = jnp.take_along_axis(cand_idx, pos, axis=-1)
        g = jax.nn.softmax(best, axis=-1)
        u = jnp.take(expert_u, eidx, axis=0)
        h = jax.nn.gelu(jnp.einsum('thkd,td->thk', u, xb))
        vv = jnp.take(expert_v, eidx, axis=0)
        return jnp.einsum('thk,thkd->td', (g * h.astype(jnp.float32)).astype(xb.dtype), vv)

    return lax.map(block, tokens).reshape(bsz, s, d)

def first_inputs(seed: int = 0) -> dict:
    key = jax.random.key(seed)
    ks = jax.random.split(key, 16)
    f32 = jnp.float32
    nrm = lambda k, shape, sc: jax.random.normal(k, shape, f32) * sc
    return {
        "x": nrm(ks[0], (BATCH, SEQ, D_MODEL), 1.0),
        "ln_mix_g": 1.0 + nrm(ks[1], (DEPTH, D_MODEL), 0.02),
        "w_in": nrm(ks[2], (DEPTH, D_MODEL, IN_COLS), D_MODEL ** -0.5),
        "gmlp_norm_g": 1.0 + nrm(ks[3], (DEPTH, MIX_A_WIDTH), 0.02),
        "gmlp_w_s": nrm(ks[4], (DEPTH, A_GROUPS, A_BLOCK, A_BLOCK), A_BLOCK ** -0.5),
        "gmlp_b_s": 1.0 + nrm(ks[5], (DEPTH, A_GROUPS, A_BLOCK), 0.1),
        "q_norm_g": 1.0 + nrm(ks[6], (DEPTH, B_HEAD_DIM), 0.02),
        "k_norm_g": 1.0 + nrm(ks[7], (DEPTH, B_HEAD_DIM), 0.02),
        "rel_bias": nrm(ks[8], (DEPTH, B_HEADS, 2 * REL_CLIP + 1), 0.1),
        "w_out": nrm(ks[9], (DEPTH, D_MODEL, D_MODEL), D_MODEL ** -0.5),
        "ln_ffn_g": 1.0 + nrm(ks[10], (DEPTH, D_MODEL), 0.02),
        "peer_w_query": nrm(ks[11], (DEPTH, D_MODEL, PEER_HEADS * PEER_QDIM), D_MODEL ** -0.5),
        "peer_sub_keys": nrm(ks[12], (DEPTH, PEER_HEADS, 2, PEER_NKEYS, PEER_HALF), PEER_HALF ** -0.5),
        "peer_u": nrm(ks[13], (DEPTH, PEER_EXPERTS, D_MODEL), D_MODEL ** -0.5),
        "peer_v": nrm(ks[14], (DEPTH, PEER_EXPERTS, D_MODEL), 0.1),
    }

def first_block(x, ln_mix_g, w_in, gmlp_norm_g, gmlp_w_s, gmlp_b_s, q_norm_g, k_norm_g, rel_bias,
              w_out, ln_ffn_g, peer_w_query, peer_sub_keys, peer_u, peer_v):
    a0, a1 = MIX_A_WIDTH, 2 * MIX_A_WIDTH
    q0, k0, v0 = a1, a1 + MIX_B_WIDTH, a1 + 2 * MIX_B_WIDTH
    for l in range(DEPTH):
        xn = rms_norm(x, ln_mix_g[l])
        proj = xn @ w_in[l]
        a_out = gmlp_spatial_gating(proj[..., :a0], proj[..., a0:a1],
                                    gmlp_norm_g[l], gmlp_w_s[l], gmlp_b_s[l])
        b_out = banded_chunk_attention(proj[..., q0:k0], proj[..., k0:v0], proj[..., v0:],
                                       q_norm_g[l], k_norm_g[l], rel_bias[l])
        x = x + jnp.concatenate([a_out, b_out], axis=-1) @ w_out[l]
        x = x + peer_ffn(rms_norm(x, ln_ffn_g[l]), peer_w_query[l], peer_sub_keys[l],
                         peer_u[l], peer_v[l])
    return x


POOL_GROUPS = 4
POOL_WINDOWS = (2, 4, 8, 16)
POOL_WIDTH = D_MODEL // 2
POOL_GROUP_DIM = POOL_WIDTH // POOL_GROUPS
SB_HEAD_DIM = 64
SB_HEADS = D_MODEL // 128
SB_WIDTH = SB_HEADS * SB_HEAD_DIM
SB_BLOCK = 128
MEM_LEN = 256
X_HEADS = 4
X_HEAD_DIM = D_MODEL // 16
X_WIDTH = X_HEADS * X_HEAD_DIM
N_BRANCHES = 3
D_FF = -(-8 * D_MODEL // (3 * 256)) * 256
RMS_EPS = 1e-6
IN_WIDTH = POOL_WIDTH + 3 * SB_WIDTH + X_WIDTH + N_BRANCHES * D_MODEL


def rmsnorm(x, g):
    xf = x.astype(jnp.float32)
    y = xf * lax.rsqrt(jnp.mean(xf * xf, axis=-1, keepdims=True) + RMS_EPS) * g.astype(jnp.float32)
    return y.astype(x.dtype)

def pool_mixer(p, w_mix, scale):
    b, s, _ = p.shape
    pg = p.astype(jnp.float32).reshape(b, s, POOL_GROUPS, POOL_GROUP_DIM)
    c = jnp.concatenate([jnp.zeros((b, 1, POOL_GROUPS, POOL_GROUP_DIM), jnp.float32),
                         jnp.cumsum(pg, axis=1)], axis=1)
    windows = jnp.array(POOL_WINDOWS, jnp.int32)
    t1 = jnp.arange(1, s + 1, dtype=jnp.int32)[:, None]
    lo = jnp.maximum(t1 - windows[None, :], 0)
    g_idx = jnp.arange(POOL_GROUPS, dtype=jnp.int32)[None, :]
    c_lo = c[:, lo, g_idx]
    count = jnp.minimum(t1, windows[None, :]).astype(jnp.float32)
    mixed = (c[:, 1:] - c_lo) / count[None, :, :, None] - pg
    mixed = mixed.astype(p.dtype)
    y = jnp.einsum('bsgc,gcd->bsgd', mixed, w_mix)
    return y.reshape(b, s, POOL_WIDTH) * scale

def stick_breaking_attention(q, k, v):
    b, s, h, dh = q.shape
    nb = s // SB_BLOCK
    scale = 1.0 / float(np.sqrt(dh))
    kf = k.astype(jnp.float32).transpose(0, 2, 1, 3)
    vf = v.astype(jnp.float32).transpose(0, 2, 1, 3)
    qb = q.astype(jnp.float32).transpose(0, 2, 1, 3).reshape(b, h, nb, SB_BLOCK, dh)
    qb = qb.transpose(2, 0, 1, 3, 4)
    key_pos = jnp.arange(s, dtype=jnp.int32)[None, :]

    def one_block(args):
        q_blk, bi = args
        z = jnp.einsum('bhqd,bhkd->bhqk', q_blk, kf) * scale
        qpos = bi * SB_BLOCK + jnp.arange(SB_BLOCK, dtype=jnp.int32)[:, None]
        mask = key_pos < qpos
        log1m = jnp.where(mask, jax.nn.log_sigmoid(-z), 0.0)
        excl = lax.cumsum(log1m, axis=3, reverse=True) - log1m
        a = jnp.where(mask, jnp.exp(jax.nn.log_sigmoid(z) + excl), 0.0)
        return jnp.einsum('bhqk,bhkd->bhqd', a, vf)

    out = lax.map(one_block, (qb, jnp.arange(nb, dtype=jnp.int32)))
    out = out.transpose(1, 0, 3, 2, 4).reshape(b, s, h * dh)
    return out.astype(q.dtype)

def memory_cross_attention(q, mem_n, w_mem_kv):
    b, s = q.shape[:2]
    m = mem_n.shape[1]
    kv = (mem_n @ w_mem_kv).reshape(b, m, 2, X_HEADS, X_HEAD_DIM)
    mk, mv = kv[:, :, 0], kv[:, :, 1]
    scores = jnp.einsum('bshd,bmhd->bhsm', q.astype(jnp.float32), mk.astype(jnp.float32))
    p = jax.nn.softmax(scores / float(np.sqrt(X_HEAD_DIM)), axis=-1)
    out = jnp.einsum('bhsm,bmhd->bshd', p, mv.astype(jnp.float32))
    return out.reshape(b, s, X_WIDTH).astype(q.dtype)

def second_inputs(seed: int = 0) -> dict:
    key = jax.random.key(seed)
    ks = jax.random.split(key, 20)
    f32 = jnp.float32

    def nrm(k, shape, fan_in):
        return jax.random.normal(k, shape, f32) * (fan_in ** -0.5)

    def gain(k, shape):
        return 1.0 + 0.02 * jax.random.normal(k, shape, f32)

    L = DEPTH
    return {
        "x": jax.random.normal(ks[0], (BATCH, SEQ, D_MODEL), f32),
        "mem": jax.random.normal(ks[1], (BATCH, MEM_LEN, D_MODEL), f32),
        "norm_mix_pre": gain(ks[2], (L, D_MODEL)),
        "w_in": nrm(ks[3], (L, D_MODEL, IN_WIDTH), D_MODEL),
        "w_pool_mix": nrm(ks[4], (L, POOL_GROUPS, POOL_GROUP_DIM, POOL_GROUP_DIM), POOL_GROUP_DIM),
        "pool_scale": gain(ks[5], (L, POOL_WIDTH)),
        "w_pool_o": nrm(ks[6], (L, POOL_WIDTH, D_MODEL), POOL_WIDTH),
        "w_sb_o": nrm(ks[7], (L, SB_WIDTH, D_MODEL), SB_WIDTH),
        "norm_mem": gain(ks[8], (L, D_MODEL)),
        "w_mem_kv": nrm(ks[9], (L, D_MODEL, 2 * X_WIDTH), D_MODEL),
        "w_x_o": nrm(ks[10], (L, X_WIDTH, D_MODEL), X_WIDTH),
        "w_out": nrm(ks[11], (L, D_MODEL, D_MODEL), D_MODEL),
        "norm_mix_post": gain(ks[12], (L, D_MODEL)),
        "norm_ffn_pre": gain(ks[13], (L, D_MODEL)),
        "w_ffn_in": nrm(ks[14], (L, D_MODEL, 2 * D_FF), D_MODEL),
        "w_ffn_out": nrm(ks[15], (L, D_FF, D_MODEL), D_FF),
        "norm_ffn_post": gain(ks[16], (L, D_MODEL)),
    }

def second_block(x, mem, norm_mix_pre, w_in, w_pool_mix, pool_scale, w_pool_o, w_sb_o,
              norm_mem, w_mem_kv, w_x_o, w_out, norm_mix_post, norm_ffn_pre,
              w_ffn_in, w_ffn_out, norm_ffn_post):
    b, s, d = x.shape
    h = x
    for l in range(DEPTH):
        n = rmsnorm(h, norm_mix_pre[l])
        proj = n @ w_in[l]
        o0 = POOL_WIDTH
        o1 = o0 + 3 * SB_WIDTH
        o2 = o1 + X_WIDTH
        p_in = proj[..., :o0]
        qkv = proj[..., o0:o1].reshape(b, s, 3, SB_HEADS, SB_HEAD_DIM)
        xq = proj[..., o1:o2].reshape(b, s, X_HEADS, X_HEAD_DIM)
        gates = jax.nn.sigmoid(proj[..., o2:].astype(jnp.float32)).reshape(b, s, N_BRANCHES, d)

        y_pool = pool_mixer(p_in, w_pool_mix[l], pool_scale[l]) @ w_pool_o[l]
        y_sb = stick_breaking_attention(qkv[:, :, 0], qkv[:, :, 1], qkv[:, :, 2]) @ w_sb_o[l]
        mem_n = rmsnorm(mem, norm_mem[l])
        y_x = memory_cross_attention(xq, mem_n, w_mem_kv[l]) @ w_x_o[l]

        merged = (gates[:, :, 0] * y_pool.astype(jnp.float32)
                  + gates[:, :, 1] * y_sb.astype(jnp.float32)
                  + gates[:, :, 2] * y_x.astype(jnp.float32)).astype(h.dtype)
        h = h + rmsnorm(merged @ w_out[l], norm_mix_post[l])

        n2 = rmsnorm(h, norm_ffn_pre[l])
        gu = n2 @ w_ffn_in[l]
        ff = (jax.nn.silu(gu[..., :D_FF]) * gu[..., D_FF:]) @ w_ffn_out[l]
        h = h + rmsnorm(ff, norm_ffn_post[l])
    return h


def setup_inputs(seed=0):
    out = dict(first_inputs(seed))
    for name, value in second_inputs(seed + 1).items():
        if name != "x":
            out[name + "_2"] = value
    return out


def reference(
    x, ln_mix_g, w_in, gmlp_norm_g, gmlp_w_s, gmlp_b_s, q_norm_g, k_norm_g, rel_bias, w_out,
    ln_ffn_g, peer_w_query, peer_sub_keys, peer_u, peer_v, mem_2, norm_mix_pre_2, w_in_2,
    w_pool_mix_2, pool_scale_2, w_pool_o_2, w_sb_o_2, norm_mem_2, w_mem_kv_2, w_x_o_2, w_out_2,
    norm_mix_post_2, norm_ffn_pre_2, w_ffn_in_2, w_ffn_out_2, norm_ffn_post_2,
):
    x = first_block(
        x, ln_mix_g, w_in, gmlp_norm_g, gmlp_w_s, gmlp_b_s, q_norm_g, k_norm_g, rel_bias, w_out,
        ln_ffn_g, peer_w_query, peer_sub_keys, peer_u, peer_v,
    )
    return second_block(
        x, mem_2, norm_mix_pre_2, w_in_2, w_pool_mix_2, pool_scale_2, w_pool_o_2, w_sb_o_2,
        norm_mem_2, w_mem_kv_2, w_x_o_2, w_out_2, norm_mix_post_2, norm_ffn_pre_2, w_ffn_in_2,
        w_ffn_out_2, norm_ffn_post_2,
    )


_drawn_inputs = setup_inputs


def setup_inputs(seed=0):
    import zlib

    import numpy as np

    out = dict(_drawn_inputs(seed))
    spreads = {}
    factors = {'ln_mix_g': 3.064,
     'gmlp_norm_g': 6.524,
     'q_norm_g': 8.0,
     'k_norm_g': 8.0,
     'rel_bias': 5.127,
     'ln_ffn_g': 35.59,
     'norm_mix_pre_2': 3.407,
     'pool_scale_2': 36.05,
     'norm_mem_2': 36.877,
     'norm_mix_post_2': 24.869,
     'norm_ffn_pre_2': 15.09,
     'norm_ffn_post_2': 111.714}
    for name, (base, spread) in spreads.items():
        noise = np.random.default_rng([zlib.crc32(name.encode()), seed]).standard_normal(out[name].shape)
        drawn = base * np.exp(spread * noise) if base else spread * noise
        out[name] = __import__('jax').numpy.asarray(drawn.astype(out[name].dtype))
    for name, factor in factors.items():
        out[name] = (out[name] * factor).astype(out[name].dtype)
    return out
```

```python
from contextlib import ExitStack

import concourse.bass as bass
from concourse import mybir

F32 = mybir.dt.float32
BF16 = mybir.dt.bfloat16
U32 = mybir.dt.uint32
ALU = mybir.AluOpType
ACT = mybir.ActivationFunctionType
AX_X = mybir.AxisListType.X

P = 128
D = 1024
S = 256
NT = S // P
KC = D // P
HALF = 512
EPS = 1e-6
NEG = -1e30
CHUNK = 64
GD = 64
HD = 64
HEADS = 8
XHEADS = 4
PEER_HEADS = 8
TOPK = 16
NKEYS = 128
HP = 2 * PEER_HEADS
DFF = 2816
FC = DFF // P
GELU_C = 0.7978845608028654
GELU_A = 0.044715
W_SLOTS = 4
RING = 8
N_GATES = 3 * D // HALF
GATE_UNITS = N_GATES * NT

BLOCKS = ([f"in{n}" for n in range(5)] + ["out0", "out1"] + [f"query{n}" for n in range(4)]
          + ["mem", "mem_kv", "in2_p", "in2_q", "in2_k", "in2_v"] + [f"in2_g{n}" for n in range(N_GATES)]
          + ["in2_x", "pool_o", "sb_o", "x_o", "out2_0", "out2_1"]
          + [f"ff_in{n}" for n in range(FC // 2)] + [f"ff_out{n}" for n in range((FC + 3) // 4)])
BLOCK_AT = {name: n for n, name in enumerate(BLOCKS)}
BLOCK_COLS = {"mem": 2 * D, "in2_x": KC * 256, "x_o": 2 * D, f"ff_out{(FC + 3) // 4 - 1}": (FC % 4 or 4) * D}


def psum_uses():
    u = [("xT", t, h) for t in range(NT) for h in range(2)]
    u += [("proj", n, t) for n in range(5) for t in range(NT)]
    u += [("qT", t) for t in range(NT)] + [("kT", t) for t in range(NT)]
    u += [("score", 0), ("score", 1)]
    for h in range(HEADS):
        if h + 2 < HEADS:
            u.append(("score", h + 2))
        u.append(("pT", h))
        if h % 2 == 0:
            u.append(("oT", h // 2))
        if h in (1, 3):
            u.append(("spatial", h // 2))
        if h in (5, 7):
            u.append(("aT", h // 2 - 2))
    u += [("w_out", n, t) for n in range(2) for t in range(NT)]
    u += [("xbT", t, h) for t in range(NT) for h in range(2)]
    u += [("query", j) for j in range(PEER_HEADS)]
    u += [("route", t, j) for t in range(NT) for j in range(HP // 4)]
    u += [("memT", t, h) for t in range(NT) for h in range(2)] + [("mk",), ("mv",)]
    u += [("expert", t, h) for t in range(NT) for h in range(2)]
    u += [("nT", t, h) for t in range(NT) for h in range(2)]
    u += [("pool_in", t) for t in range(NT)] + [("q2", 0), ("q2", 1), ("k2", 0), ("k2", 1)]
    u += [("v2", t) for t in range(NT)]
    for i in range(GATE_UNITS):
        u.append(("gate", i // NT, i % NT))
        if i < HEADS:
            u.append(("z", i))
        if 2 <= i < HEADS + 2 and i % 2 == 0:
            u.append(("sbT", (i - 2) // 2))
        if i in (8, 9):
            u.append(("mix", i - 8))
        if i in (10, 11):
            u.append(("poolT", i - 10))
    u += [("xq",)] + [("xs", t, j) for t in range(NT) for j in range(2)]
    u += [("y_pool", t, n) for t in range(NT) for n in range(2)]
    u += [("y_sb", t, n) for t in range(NT) for n in range(2)]
    for h in range(XHEADS):
        u.append(("xpT", h))
        if h % 2 == 0:
            u.append(("xoT", h // 2))
    u += [("y_x", t, n) for t in range(NT) for n in range(2)]
    u += [("mergedT", t, h) for t in range(NT) for h in range(2)]
    u += [("w_out2", n, t) for n in range(2) for t in range(NT)]
    u += [("n2T", t, h) for t in range(NT) for h in range(2)]
    u += [("ff", j) for j in range(FC)]
    u += [("ff_out", t, n) for t in range(NT) for n in range(2)]
    return u


def two_block_kernel(nc, io, out):
    use_of = {key: n for n, key in enumerate(psum_uses())}

    def at(*key):
        n = use_of[key]
        return n % 8, n // 8

    with ExitStack() as ctx:
        def sb(name, shape, dt=F32):
            return ctx.enter_context(nc.sbuf_tensor(name, shape, dt))

        def sem(name):
            return ctx.enter_context(nc.semaphore(name))

        bank = [ctx.enter_context(nc.psum_tensor(f"bank{b}", [P, HALF], F32)) for b in range(8)]

        x_sb = sb("x_sb", [P, NT, D])
        xn = sb("xn", [P, NT, D])
        nT = sb("nT", [P, KC, S])
        wring = sb("wring", [P, W_SLOTS, 4096])
        gain = sb("gain", [P, 3, D])
        const = sb("const", [P, 4 * P + 2 * 384])
        cols = sb("cols", [P, 16])
        mkT = sb("mkT", [P, 2, S])
        mv = sb("mv", [P, NT, 256])
        stat = sb("stat", [P, 3, 16])
        junk = sb("junk", [P, D], BF16)
        eps = sb("eps", [P, 1])
        small = sb("small", [P, 256])
        rank = sb("rank", [P, 4, TOPK], U32)
        eidx = sb("eidx", [P, 2, TOPK], U32)
        arena = sb("arena", [P, 2 * RING * D + 6144])

        def view(off, a, b):
            return arena[:, off:off + a * b].rearrange("p (a b) -> p a b", a=a)

        u_sb = view(0, NT, HALF)
        vg = view(1024, NT, HALF)
        q_sb = view(2048, NT, HALF)
        k_sb = view(3072, NT, HALF)
        v_sb = view(4096, NT, HALF)
        w_sT = view(5120, 8, P)
        bias = view(6144, HEADS, 384)
        qT = view(9216, 4, S)
        kT = view(10240, 4, S)
        catT = view(11264, KC, S)
        sq = view(13312, 4, HALF)
        prob = view(13312, 4, 384)
        probT = view(15360, 2, 384)
        q2T = view(0, HP, S)
        u_ring = view(0, RING, D)
        v_ring = view(RING * D, RING, D)
        route = view(2 * RING * D, NT, HP * NKEYS)
        sub_kT = view(2 * RING * D + 4096, HP, NKEYS)
        gmlp_g = arena[:, 2 * RING * D:2 * RING * D + HALF]
        attn_stat = sb("attn_stat", [P, 4, HEADS, 2])
        qk_stat = sb("qk_stat", [P, 3, 4, HEADS])
        diag = sb("diag", [P, RING, P])
        choice = 2 * RING * D + 4096
        head_sc = view(choice, 2, NKEYS)
        head_sc2 = view(choice + 256, 2, NKEYS)
        cand = arena[:, choice + 512:choice + 768]
        cand2 = arena[:, choice + 768:choice + 1024]
        onehot = arena[:, choice + 1024:choice + 1536].rearrange("p (a b c) -> p a b c", a=2, b=TOPK)
        gates = view(0, NT, 3 * D)
        hT = view(0, FC, S)
        p_sb = view(6144, NT, HALF)
        q3T = view(7168, 4, S)
        k3T = view(8192, 4, S)
        mixT = view(7168, 4, S)
        poolT = view(8192, 4, S)
        v3 = view(9216, NT, HALF)
        band = view(10240, 4, 384)
        w_mix = view(11776, 4, P)
        sbT = view(12288, 4, S)
        xqT = view(13312, 2, S)
        xpT = view(13824, 2, HALF)
        xprob = view(14848, 8, S)
        z_sb = view(14848, NT, D)
        xoT = view(16896, 2, S)
        sp_e = view(17408, 2, 384)
        sp_l = view(18176, 2, 384)
        att = view(18944, 4, 384)
        silu = view(20480, 2, S)
        tmp = arena[:, 20992:20992 + HALF]
        xstat = sb("xstat", [P, 4, 8])

        ident = const[:, 0:P]
        negtri = const[:, P:2 * P]
        negones = const[:, 2 * P:3 * P]
        mask01 = const[:, 3 * P:3 * P + 384]
        maskneg = const[:, 3 * P + 384:3 * P + 768]
        iota16 = cols[:, 0:0]
        top = small[:, 0:32].rearrange("p (a b) -> p a b", a=2)
        topi = small[:, 32:64].rearrange("p (a b) -> p a b", a=2)
        best = small[:, 64:80]
        ij = small[:, 80:112]
        picked = small[:, 112:144]
        hdot = small[:, 144:160]
        gexp = small[:, 160:176]
        gq = small[:, 176:192]
        ge = small[:, 192:208]
        wexp = small[:, 208:224]
        nbest = small[:, 224:225]
        gsum = small[:, 225:226]
        rsum = small[:, 226:227]
        iota = small[:, 240:256]

        bank_full = [sem(f"bank_full{b}") for b in range(8)]
        bank_read = [sem(f"bank_read{b}") for b in range(8)]
        w_loaded = [sem(f"w_loaded{i}") for i in range(W_SLOTS)]
        x_loaded = [sem(f"x_loaded{t}") for t in range(NT)]
        const_loaded = sem("const_loaded")
        gain_loaded = [sem(f"gain_loaded{i}") for i in range(3)]
        a_loaded = sem("a_loaded")
        subk_loaded = sem("subk_loaded")
        pool_loaded = sem("pool_loaded")
        u_loaded = [sem(f"u_loaded{i}") for i in range(RING)]
        v_loaded = [sem(f"v_loaded{i}") for i in range(RING)]
        stored = sem("stored")
        dve_step = sem("dve_step")
        dve_passed = sem("dve_passed")
        act_step = sem("act_step")
        eps_set = sem("eps_set")
        rms_ready = sem("rms_ready")
        norm_ready = sem("norm_ready")
        w_masked = sem("w_masked")
        bias_masked = sem("bias_masked")
        iota_ready = sem("iota_ready")
        gelu_v = sem("gelu_v")
        v_rms = sem("v_rms")
        v_normed = sem("v_normed")
        qk_squared = sem("qk_squared")
        qk_summed = sem("qk_summed")
        qk_rms = sem("qk_rms")
        a_ready = sem("a_ready")
        row_max = sem("row_max")
        row_exp = sem("row_exp")
        prob_ready = sem("prob_ready")
        even_o = sem("even_o")
        idx_ready = sem("idx_ready")
        u_used = sem("u_used")
        v_used = sem("v_used")
        best_ready = sem("best_ready")
        gexp_ready = sem("gexp_ready")
        gq_ready = sem("gq_ready")
        ge_ready = sem("ge_ready")
        w_ready = sem("w_ready")
        diag_ready = sem("diag_ready")
        pool_passed = sem("pool_passed")
        x2_ready = sem("x2_ready")
        z_ln = sem("z_ln")
        l_ready = sem("l_ready")
        cumulated = sem("cumulated")
        att_in = sem("att_in")
        att_ready = sem("att_ready")
        even_sb = sem("even_sb")
        gates_exp = sem("gates_exp")
        xmax = sem("xmax")
        xexp = sem("xexp")
        xprob_ready = sem("xprob_ready")
        even_x = sem("even_x")
        merged_ready = sem("merged_ready")
        zcopied = sem("zcopied")
        h_ready = sem("h_ready")
        silu_ready = sem("silu_ready")
        ff_used = sem("ff_used")

        def spread(ap, dims):
            return bass.AP(tensor=ap.tensor, offset=ap.offset, ap=[ap.ap[0]] + dims)

        def tok(t):
            return slice(t * P, (t + 1) * P)

        def half(n):
            return slice(n * HALF, (n + 1) * HALF)

        def block_wait(pe, name):
            b = BLOCK_AT[name]
            pe.wait_ge(w_loaded[b % W_SLOTS], 16 * (b // W_SLOTS + 1))
            return wring[:, b % W_SLOTS, :]

        def wait_full(eng, *key):
            b, u = at(*key)
            eng.wait_ge(bank_full[b], u + 1)
            return bank[b]

        def wait_read(eng, *key):
            b, u = at(*key)
            eng.wait_ge(bank_read[b], u + 1)

        def read_of(*key):
            return bank_read[at(*key)[0]]

        def full_of(*key):
            return bank_full[at(*key)[0]]

        last_use = {}
        for n in range(5):
            last_use[f"in{n}"] = ("proj", n, NT - 1)
        for n in range(2):
            last_use[f"out{n}"] = ("w_out", n, NT - 1)
            last_use[f"out2_{n}"] = ("w_out2", n, NT - 1)
        for n in range(4):
            last_use[f"query{n}"] = ("query", 2 * n + 1)
        last_use |= {"mem": ("memT", 1, 1), "mem_kv": ("mv",), "in2_p": ("pool_in", 1), "in2_q": ("q2", 1),
                     "in2_k": ("k2", 1), "in2_v": ("v2", 1), "in2_x": ("xq",), "pool_o": ("y_pool", 1, 1),
                     "sb_o": ("y_sb", 1, 1), "x_o": ("y_x", 1, 1)}
        for n in range(N_GATES):
            last_use[f"in2_g{n}"] = ("gate", n, NT - 1)
        for n in range(FC // 2):
            last_use[f"ff_in{n}"] = ("ff", 2 * n + 1)

        block = ctx.enter_context(nc.Block())

        @block.sync
        def _(sp):
            def load_block(name):
                b = BLOCK_AT[name]
                if b >= W_SLOTS:
                    freed = BLOCKS[b - W_SLOTS]
                    if freed.startswith("ff_out"):
                        sp.wait_ge(ff_used, 4 * (int(freed[6:]) + 1))
                    else:
                        wait_full(sp, *last_use[freed])
                n = BLOCK_COLS.get(name, 4096)
                sp.dma_start(wring[:, b % W_SLOTS, 0:n], io[name]).then_inc(w_loaded[b % W_SLOTS], 16)

            def load_gain(i, name):
                g = io[name]
                src = bass.AP(tensor=g.tensor, offset=g.offset, ap=[[0, P], [1, D]])
                sp.dma_start(gain[:, i, :], src).then_inc(gain_loaded[i], 16)

            for t in range(NT):
                sp.dma_start(x_sb[:, t, :], io["x"][tok(t), :]).then_inc(x_loaded[t], 16)
            sp.dma_start(const[:, :], io["const"]).then_inc(const_loaded, 16)
            load_gain(0, "ln_mix_g")
            sp.dma_start(cols[:, :], io["cols"]).then_inc(const_loaded, 16)
            for n in range(W_SLOTS):
                load_block(BLOCKS[n])
            g = io["gmlp_norm_g"]
            sp.dma_start(gmlp_g, bass.AP(tensor=g.tensor, offset=g.offset, ap=[[0, P], [1, HALF]])).then_inc(a_loaded, 16)
            sp.dma_start(w_sT, io["w_sT"]).then_inc(a_loaded, 16)
            sp.dma_start(bias[:, :, 0:P], io["rel"][:, :, P:S]).then_inc(a_loaded, 16)
            sp.dma_start(bias[:, :, P:384], io["rel"]).then_inc(a_loaded, 16)
            load_gain(1, "ln_ffn_g")
            load_gain(2, "norm_mem_2")
            sp.dma_start(sub_kT, io["sub_kT"]).then_inc(subk_loaded, 16)
            mem_at = BLOCK_AT["mem"]
            for name in BLOCKS[W_SLOTS:mem_at + W_SLOTS + 2]:
                load_block(name)
            sp.wait_ge(norm_ready, 2)
            load_gain(0, "norm_mix_pre_2")
            sp.wait_ge(norm_ready, 4)
            load_gain(1, "norm_mix_post_2")
            sp.wait_ge(norm_ready, 6)
            load_gain(2, "norm_ffn_pre_2")
            sp.wait_ge(x2_ready, 2 * NT)
            sp.dma_start(band, io["band"]).then_inc(pool_loaded, 16)
            sp.dma_start(w_mix, io["w_mix"]).then_inc(pool_loaded, 16)
            for name in BLOCKS[mem_at + W_SLOTS + 2:BLOCK_AT["ff_in4"]]:
                load_block(name)
            sp.wait_ge(norm_ready, 10)
            load_gain(1, "norm_ffn_post_2")
            for name in BLOCKS[BLOCK_AT["ff_in4"]:]:
                load_block(name)
            for t in range(NT):
                sp.wait_ge(h_ready, NT + t + 1)
                sp.dma_start(out[tok(t), :], x_sb[:, t, :]).then_inc(stored, 16)
            sp.wait_ge(stored, 16 * NT)

        @block.gpsimd
        def _(pool):
            pool.iota(iota, [[1, TOPK]], base=0, channel_multiplier=0,
                      allow_small_or_imprecise_dtypes=True).then_inc(iota_ready, 1)
            for t in range(NT):
                for j in range(HP // 4):
                    wait_read(pool, "route", t, j)
            for t in range(NT):
                with pool.Fori(0, PEER_HEADS // 2) as i:
                    for hh in range(2):
                        head = t * PEER_HEADS + i * 2 + hh
                        pool.wait_ge(idx_ready, head + 1)
                        pool.sem_inc(pool_passed, 1)
                        for table, ring, used, loaded in (("peer_u", u_ring, u_used, u_loaded),
                                                          ("peer_v", v_ring, v_used, v_loaded)):
                            for k in range(TOPK):
                                pool.wait_ge(used, head * TOPK + k + 1)
                                pool.sem_inc(pool_passed, 1)
                                pool.indirect_dma_start(
                                    out=ring[:, k % RING, :], out_offset=None, in_=io[table],
                                    in_offset=bass.IndirectOffsetOnAxis(ap=eidx[:, hh, k:k + 1], axis=0),
                                ).then_inc(loaded[k % RING], 16)

        @block.scalar
        def _(act):
            steps = [0]

            def step(ins):
                steps[0] += 1
                ins.then_inc(act_step, 1)
                act.wait_ge(act_step, steps[0])

            def rms(n, src, width=D):
                step(nc.scalar.activation(junk[:, 0:width], src, ACT.Square, accum_out=stat[:, 0, n:n + 1]))
                step(nc.scalar.activation(stat[:, 1, n:n + 1], stat[:, 0, n:n + 1], ACT.Ln,
                                          bias=eps[:, 0:1], scale=1.0 / width))
                return nc.scalar.activation(stat[:, 2, n:n + 1], stat[:, 1, n:n + 1], ACT.Exp, scale=-0.5)

            def copy_half_T(name, dst, t, h):
                src = wait_full(act, name, t, h)
                nc.scalar.copy(dst[:, 4 * h:4 * h + 4, tok(t)],
                               src[:, :].rearrange("p (c k) -> p c k", c=4)).then_inc(read_of(name, t, h), 1)

            act.wait_ge(eps_set, 1)
            for t in range(NT):
                act.wait_ge(x_loaded[t], 16)
                rms(t, x_sb[:, t, :]).then_inc(rms_ready, 1)
            for t in range(NT):
                copy_half_T("xT", nT, t, 0)
            for n, dst in ((0, u_sb), (1, vg)):
                for t in range(NT):
                    src = wait_full(act, "proj", n, t)
                    nc.scalar.activation(dst[:, t, :], src[:, :], ACT.Gelu_apprx_tanh).then_inc(read_of("proj", n, t), 1)
            for t in range(NT):
                wait_read(act, "proj", 1, t)
                rms(14 + t, vg[:, t, :], HALF).then_inc(v_rms, 1)
            for n in range(2):
                for t in range(NT):
                    src = wait_full(act, "proj", 2 + n, t)
                    nc.scalar.activation(sq[:, 2 * n + t, :], src[:, :], ACT.Square).then_inc(qk_squared, 1)
                    act.wait_ge(qk_summed, 2 * n + t + 1)
                    step(nc.scalar.activation(qk_stat[:, 1, 2 * n + t, :], qk_stat[:, 0, 2 * n + t, :], ACT.Ln,
                                              bias=eps[:, 0:1], scale=1.0 / HD))
                    nc.scalar.activation(qk_stat[:, 2, 2 * n + t, :], qk_stat[:, 1, 2 * n + t, :], ACT.Exp,
                                         scale=-0.5).then_inc(qk_rms, 1)
            for t in range(NT):
                src = wait_full(act, "proj", 4, t)
                nc.scalar.copy(v_sb[:, t, :], src[:, :]).then_inc(read_of("proj", 4, t), 1)
            for h in range(HEADS + 1):
                if h < HEADS:
                    act.wait_ge(row_max, h + 1)
                    nc.scalar.activation(prob[:, h % 4, 0:P], prob[:, h % 4, 0:P], ACT.Exp,
                                         bias=attn_stat[:, 1, h, 0:1],
                                         accum_out=attn_stat[:, 2, h, 0:1]).then_inc(row_exp, 1)
                    nc.scalar.activation(prob[:, h % 4, P:384], prob[:, h % 4, P:384], ACT.Exp,
                                         bias=attn_stat[:, 1, h, 1:2],
                                         accum_out=attn_stat[:, 2, h, 1:2]).then_inc(row_exp, 1)
                if h >= 1:
                    g = h - 1
                    src = wait_full(act, "pT", g)
                    if g >= 2:
                        if g % 2 == 0:
                            act.wait_ge(even_o, (g - 2) // 2 + 1)
                        else:
                            wait_full(act, "oT", (g - 2) // 2)
                    nc.scalar.copy(probT[:, g % 2, :], src[:, 0:384]).then_inc(read_of("pT", g), 1)
            for t in range(NT):
                for n in range(2):
                    wait_read(act, "w_out", n, t)
                rms(2 + t, x_sb[:, t, :]).then_inc(rms_ready, 1)
            for t in range(NT):
                copy_half_T("xbT", nT, t, 0)
            for j in range(0, PEER_HEADS, 2):
                src = wait_full(act, "query", j)
                nc.scalar.copy(q2T[:, 2 * j:2 * j + 2, :],
                               src[:, :].rearrange("p (a b) -> p a b", a=2)).then_inc(read_of("query", j), 1)
            for t in range(NT):
                for j in range(0, HP // 4, 2):
                    src = wait_full(act, "route", t, j)
                    nc.scalar.copy(route[:, t, half(j)], src[:, :]).then_inc(read_of("route", t, j), 1)
            mem_at = BLOCK_AT["mem"]
            act.wait_ge(w_loaded[mem_at % W_SLOTS], 16 * (mem_at // W_SLOTS + 1))
            for t in range(NT):
                rms(4 + t, wring[:, mem_at % W_SLOTS, t * D:(t + 1) * D]).then_inc(rms_ready, 1)
            for t in range(NT):
                for h in range(2):
                    copy_half_T("memT", nT, t, h)
            src = wait_full(act, "mk")
            nc.scalar.copy(mkT[:, :, :], src[:, :].rearrange("p (a b) -> p a b", a=2)).then_inc(read_of("mk"), 1)
            src = wait_full(act, "mv")
            nc.scalar.copy(mv[:, :, :], src[:, :].rearrange("p (a b) -> p a b", a=2)).then_inc(read_of("mv"), 1)

            for t in range(NT):
                with act.Fori(0, PEER_HEADS // 2) as i:
                    for hh in range(2):
                        head = t * PEER_HEADS + i * 2 + hh
                        act.wait_ge(best_ready, head + 1)
                        nc.scalar.activation(gexp, best, ACT.Exp, bias=nbest, accum_out=gsum).then_inc(gexp_ready, 1)
                        act.wait_ge(gq_ready, head + 1)
                        nc.scalar.activation(ge, gq, ACT.Tanh, scale=GELU_C).then_inc(ge_ready, 1)
                        act.wait_ge(w_ready, head + 1)
                        for k in range(TOPK):
                            act.wait_ge(v_used, head * TOPK + k + 1)
                            nc.scalar.activation(diag[:, k % RING, :], ident, ACT.Copy,
                                                 scale=wexp[:, k:k + 1]).then_inc(diag_ready, 1)

            for t in range(NT):
                act.wait_ge(x2_ready, 2 * t + 2)
                rms(6 + t, x_sb[:, t, :]).then_inc(rms_ready, 1)
            for t in range(NT):
                copy_half_T("nT", nT, t, 0)
            for t in range(NT):
                src = wait_full(act, "pool_in", t)
                nc.scalar.copy(p_sb[:, t, :], src[:, :]).then_inc(read_of("pool_in", t), 1)
            for c in range(2):
                src = wait_full(act, "k2", c)
                nc.scalar.copy(k3T[:, 2 * c:2 * c + 2, :],
                               src[:, :].rearrange("p (a b) -> p a b", a=2)).then_inc(read_of("k2", c), 1)
            for t in range(NT):
                src = wait_full(act, "v2", t)
                nc.scalar.copy(v3[:, t, :], src[:, :]).then_inc(read_of("v2", t), 1)
            for i in range(GATE_UNITS):
                n, t = i // NT, i % NT
                src = wait_full(act, "gate", n, t)
                nc.scalar.activation(gates[:, t, half(n)], src[:, :], ACT.Exp, scale=-1.0).then_inc(read_of("gate", n, t), 1)
                if i < HEADS:
                    src = wait_full(act, "z", i)
                    if i >= 2:
                        act.wait_ge(l_ready, i - 1)
                    step(nc.scalar.activation(sp_e[:, i % 2, :], src[:, 0:384], ACT.Abs))
                    step(nc.scalar.activation(sp_e[:, i % 2, :], sp_e[:, i % 2, :], ACT.Exp, scale=-1.0))
                    nc.scalar.activation(sp_e[:, i % 2, :], sp_e[:, i % 2, :], ACT.Ln, bias=1.0).then_inc(z_ln, 1)
                if 1 <= i <= HEADS:
                    g = i - 1
                    act.wait_ge(att_in, g + 1)
                    nc.scalar.activation(att[:, g % 4, :], att[:, g % 4, :], ACT.Exp).then_inc(att_ready, 1)
                if i in (8, 9):
                    c = i - 8
                    src = wait_full(act, "mix", c)
                    nc.scalar.copy(mixT[:, 2 * c:2 * c + 2, :],
                                   src[:, :].rearrange("p (a b) -> p a b", a=2)).then_inc(read_of("mix", c), 1)
            src = wait_full(act, "xq")
            nc.scalar.copy(xqT[:, :, :], src[:, :].rearrange("p (a b) -> p a b", a=2)).then_inc(read_of("xq"), 1)
            for t in range(NT):
                for j in range(2):
                    act.wait_ge(xmax, 2 * t + j + 1)
                    src = bank[at("xs", t, j)[0]]
                    for a in range(2):
                        n = 4 * t + 2 * j + a
                        ins = nc.scalar.activation(xprob[:, n, :], src[:, a * S:(a + 1) * S], ACT.Exp,
                                                   scale=HD ** -0.5, bias=xstat[:, 1, n:n + 1],
                                                   accum_out=xstat[:, 2, n:n + 1])
                        ins.then_inc(read_of("xs", t, j) if a else xexp, 1)
            for h in range(XHEADS):
                src = wait_full(act, "xpT", h)
                if h >= 2:
                    if h % 2 == 0:
                        act.wait_ge(even_x, (h - 2) // 2 + 1)
                    else:
                        wait_full(act, "xoT", (h - 2) // 2)
                nc.scalar.copy(xpT[:, h % 2, :], src[:, :]).then_inc(read_of("xpT", h), 1)
            for t in range(NT):
                copy_half_T("mergedT", nT, t, 0)
            for n in range(2):
                for t in range(NT):
                    src = wait_full(act, "w_out2", n, t)
                    nc.scalar.copy(z_sb[:, t, half(n)], src[:, :]).then_inc(read_of("w_out2", n, t), 1)
            for t in range(NT):
                for n in range(2):
                    wait_read(act, "w_out2", n, t)
                rms(8 + t, z_sb[:, t, :]).then_inc(rms_ready, 1)
            for t in range(NT):
                act.wait_ge(h_ready, t + 1)
                rms(10 + t, x_sb[:, t, :]).then_inc(rms_ready, 1)
            for t in range(NT):
                copy_half_T("n2T", nT, t, 0)
            for j in range(FC):
                src = wait_full(act, "ff", j)
                if j >= 2:
                    wait_read(act, "ff", j - 2)
                nc.scalar.activation(silu[:, j % 2, :], src[:, 0:S], ACT.Silu).then_inc(silu_ready, 1)
            for t in range(NT):
                for n in range(2):
                    src = wait_full(act, "ff_out", t, n)
                    nc.scalar.copy(z_sb[:, t, half(n)], src[:, :]).then_inc(read_of("ff_out", t, n), 1)
                for n in range(2):
                    wait_read(act, "ff_out", t, n)
                rms(12 + t, z_sb[:, t, :]).then_inc(rms_ready, 1)

        @block.vector
        def _(dve):
            steps = [0, 0]

            def step(ins):
                steps[0] += 1
                ins.then_inc(dve_step, 1)
                dve.wait_ge(dve_step, steps[1] + steps[0])

            def step_apart(ins):
                step(ins)
                dve.sem_inc(dve_passed, 1)

            def norm(n, src, dst, g):
                dve.wait_ge(rms_ready, n + 1)
                return nc.vector.scalar_tensor_tensor(out=dst, in0=src, scalar=stat[:, 2, n:n + 1],
                                                      in1=gain[:, g, :], op0=ALU.mult, op1=ALU.mult)

            def copy_half_T(name, dst, t, h):
                src = wait_full(dve, name, t, h)
                nc.vector.tensor_copy(dst[:, 4 * h:4 * h + 4, tok(t)],
                                      src[:, :].rearrange("p (c k) -> p c k", c=4)).then_inc(read_of(name, t, h), 1)

            nc.vector.memset(eps[:, :], EPS).then_inc(eps_set, 1)
            nc.vector.memset(small[:, 227:228], 0.0).then_inc(u_used, RING)
            nc.vector.memset(small[:, 228:229], 0.0).then_inc(v_used, RING)
            dve.wait_ge(gain_loaded[0], 16)
            for t in range(NT):
                norm(t, x_sb[:, t, :], xn[:, t, :], 0).then_inc(norm_ready, 1)
            for t in range(NT):
                copy_half_T("xT", nT, t, 1)
            dve.wait_ge(a_loaded, 64)
            nc.vector.memset(w_sT[CHUNK:P, :, 0:CHUNK], 0.0).then_inc(w_masked, 1)
            step(nc.vector.memset(bias[0:CHUNK, :, CHUNK:P], NEG))
            step(nc.vector.memset(bias[0:CHUNK, :, 384 - CHUNK:384], NEG))
            for t in range(NT):
                dve.wait_ge(v_rms, t + 1)
                nc.vector.scalar_tensor_tensor(out=vg[:, t, :], in0=vg[:, t, :], scalar=stat[:, 2, 14 + t:15 + t],
                                               in1=gmlp_g, op0=ALU.mult, op1=ALU.mult).then_inc(v_normed, 1)
            for n, dst in ((0, q_sb), (1, k_sb)):
                for t in range(NT):
                    c = 2 * n + t
                    dve.wait_ge(qk_squared, c + 1)
                    nc.vector.tensor_reduce(qk_stat[:, 0, c, :], sq[:, c, :].rearrange("p (h d) -> p h d", h=HEADS),
                                            AX_X, ALU.add).then_inc(qk_summed, 1)
                    dve.wait_ge(qk_rms, c + 1)
                    src = bank[at("proj", 2 + n, t)[0]]
                    nc.vector.tensor_tensor(dst[:, t, :].rearrange("p (h d) -> p h d", h=HEADS),
                                            src[:, :].rearrange("p (h d) -> p h d", h=HEADS),
                                            spread(qk_stat[:, 2, c, :], [[1, HEADS], [0, HD]]),
                                            ALU.mult).then_inc(read_of("proj", 2 + n, t), 1)
            for name, dst, col, scale in (("qT", qT, 0, HD ** -0.5), ("kT", kT, 1, 1.0)):
                for t in range(NT):
                    src = wait_full(dve, name, t)
                    nc.vector.tensor_scalar(dst[:, :, tok(t)], src[:, :].rearrange("p (c k) -> p c k", c=4),
                                            cols[:, col:col + 1], scale, ALU.mult, ALU.mult).then_inc(read_of(name, t), 1)

            def scores(h):
                src = wait_full(dve, "score", h)
                if h >= 4:
                    wait_full(dve, "pT", h - 4)
                b = read_of("score", h)
                nc.vector.tensor_tensor(prob[:, h % 4, :], src[:, 0:384], bias[:, h, :], ALU.add).then_inc(b, 1)
                wait_read(dve, "score", h)
                nc.vector.tensor_reduce(attn_stat[:, 0, h, 0:1], prob[:, h % 4, 0:P], AX_X, ALU.max)
                step(nc.vector.tensor_reduce(attn_stat[:, 0, h, 1:2], prob[:, h % 4, P:384], AX_X, ALU.max))
                nc.vector.tensor_scalar(attn_stat[:, 1, h, :], attn_stat[:, 0, h, :], -1.0, None,
                                        ALU.mult).then_inc(row_max, 1)

            def normalise(h):
                dve.wait_ge(row_exp, 2 * h + 2)
                step(nc.vector.reciprocal(attn_stat[:, 3, h, :], attn_stat[:, 2, h, :]))
                nc.vector.tensor_scalar(prob[:, h % 4, 0:P], prob[:, h % 4, 0:P], attn_stat[:, 3, h, 0:1], None,
                                        ALU.mult).then_inc(prob_ready, 1)
                nc.vector.tensor_scalar(prob[:, h % 4, P:384], prob[:, h % 4, P:384], attn_stat[:, 3, h, 1:2], None,
                                        ALU.mult).then_inc(prob_ready, 1)

            def spatial(t):
                src = wait_full(dve, "spatial", t)
                v3d = vg[:, t, :].rearrange("p (g c) -> p g c", g=8)
                step(nc.vector.tensor_tensor(v3d, src[:, :].rearrange("p (g c) -> p g c", g=8),
                                             spread(cols[:, 2:10], [[1, 8], [0, GD]]), ALU.add))
                nc.vector.tensor_tensor(u_sb[:, t, :], u_sb[:, t, :], vg[:, t, :], ALU.mult).then_inc(read_of("spatial", t), 1)

            scores(0)
            scores(1)
            for h in range(HEADS):
                normalise(h)
                if h + 2 < HEADS:
                    scores(h + 2)
                if h % 2 == 1:
                    src = wait_full(dve, "oT", h // 2)
                    nc.vector.tensor_copy(catT[:, 4 + h // 2, :], src[:, 0:S]).then_inc(read_of("oT", h // 2), 1)
                if h in (1, 3):
                    spatial(h // 2)
                if h in (5, 7):
                    t = h // 2 - 2
                    src = wait_full(dve, "aT", t)
                    nc.vector.tensor_copy(catT[:, 0:4, tok(t)],
                                          src[:, :].rearrange("p (c k) -> p c k", c=4)).then_inc(read_of("aT", t), 1)
            for n in range(2):
                for t in range(NT):
                    src = wait_full(dve, "w_out", n, t)
                    nc.vector.tensor_tensor(x_sb[:, t, half(n)], x_sb[:, t, half(n)], src[:, :],
                                            ALU.add).then_inc(read_of("w_out", n, t), 1)
            dve.wait_ge(gain_loaded[1], 16)
            for t in range(NT):
                norm(2 + t, x_sb[:, t, :], xn[:, t, :], 1).then_inc(norm_ready, 1)
            for t in range(NT):
                copy_half_T("xbT", nT, t, 1)
            for j in range(1, PEER_HEADS, 2):
                src = wait_full(dve, "query", j)
                nc.vector.tensor_copy(q2T[:, 2 * j:2 * j + 2, :],
                                      src[:, :].rearrange("p (a b) -> p a b", a=2)).then_inc(read_of("query", j), 1)
            for t in range(NT):
                for j in range(1, HP // 4, 2):
                    src = wait_full(dve, "route", t, j)
                    nc.vector.tensor_copy(route[:, t, half(j)], src[:, :]).then_inc(read_of("route", t, j), 1)
            dve.wait_ge(gain_loaded[2], 16)
            mem_at = BLOCK_AT["mem"]
            for t in range(NT):
                m = wring[:, mem_at % W_SLOTS, t * D:(t + 1) * D]
                norm(4 + t, m, m, 2).then_inc(norm_ready, 1)

            def sixteen(values, spare, out, where):
                step_apart(nc.vector.max(out[:, 0:8], values))
                nc.vector.max_index(where[:, 0:8], out[:, 0:8], values)
                step_apart(nc.vector.match_replace(spare, out[:, 0:8], values, -3.0e38))
                step_apart(nc.vector.max(out[:, 8:16], spare))
                return nc.vector.max_index(where[:, 8:16], out[:, 8:16], spare)

            def choose(t, i, hh):
                step_apart(nc.vector.tensor_copy(head_sc[:, :, :].rearrange("p a b -> p (a b)"),
                                           route[:, t, bass.ds(i * 512 + hh * 256, 256)]))
                for p in range(2):
                    step_apart(sixteen(head_sc[:, p, :], head_sc2[:, p, :], top[:, p, :], rank[:, p, :]))
                nc.vector.tensor_copy(topi, rank[:, 0:2, :])
                step_apart(nc.vector.tensor_tensor(cand[:, :].rearrange("p (a b) -> p a b", a=TOPK),
                                             spread(top[:, 0, :], [[1, TOPK], [0, TOPK]]),
                                             spread(top[:, 1, :], [[0, TOPK], [1, TOPK]]), ALU.add))
                step(sixteen(cand[:, :], cand2[:, :], best, rank[:, 2, :]))
                nc.vector.tensor_scalar(nbest, best[:, 0:1], -1.0, None, ALU.mult).then_inc(best_ready, 1)
                step(nc.vector.tensor_scalar(rank[:, 3, :], rank[:, 2, :], 4, None, ALU.logical_shift_right))
                step(nc.vector.tensor_scalar(rank[:, 2, :], rank[:, 2, :], 15, None, ALU.bitwise_and))
                nc.vector.tensor_copy(ij[:, 0:TOPK], rank[:, 3, :])
                step(nc.vector.tensor_copy(ij[:, TOPK:2 * TOPK], rank[:, 2, :]))
                step(nc.vector.tensor_tensor(onehot[:, :, :, :].rearrange("p a b c -> p (a b) c"),
                                             spread(ij, [[1, 2 * TOPK], [0, TOPK]]),
                                             spread(iota, [[0, 2 * TOPK], [1, TOPK]]), ALU.is_equal))
                step(nc.vector.tensor_tensor(onehot[:, :, :, :], onehot[:, :, :, :],
                                             spread(topi, [[TOPK, 2], [0, TOPK], [1, TOPK]]), ALU.mult))
                step(nc.vector.tensor_reduce(picked, onehot[:, :, :, :].rearrange("p a b c -> p (a b) c"),
                                             AX_X, ALU.add))
                nc.vector.scalar_tensor_tensor(out=eidx[:, hh, :], in0=picked[:, 0:TOPK], scalar=float(NKEYS),
                                               in1=picked[:, TOPK:2 * TOPK], op0=ALU.mult,
                                               op1=ALU.add).then_inc(idx_ready, 1)

            def weigh(t, i, hh):
                head = t * PEER_HEADS + i * 2 + hh
                for k in range(TOPK):
                    dve.wait_ge(u_loaded[k % RING], head * 32 + 16 * (k // RING) + 16)
                    nc.vector.scalar_tensor_tensor(out=u_ring[:, k % RING, :], in0=u_ring[:, k % RING, :], scalar=1.0,
                                                   in1=xn[:, t, :], op0=ALU.mult, op1=ALU.mult,
                                                   accum_out=hdot[:, k:k + 1]).then_inc(u_used, 1)
                dve.wait_ge(u_used, head * TOPK + TOPK + RING)
                step(nc.vector.tensor_tensor(gq, hdot, hdot, ALU.mult))
                step(nc.vector.tensor_scalar(gq, gq, GELU_A, 1.0, ALU.mult, ALU.add))
                nc.vector.tensor_tensor(gq, gq, hdot, ALU.mult).then_inc(gq_ready, 1)
                dve.wait_ge(gexp_ready, head + 1)
                step(nc.vector.reciprocal(rsum, gsum))
                step(nc.vector.scalar_tensor_tensor(out=wexp, in0=hdot, scalar=rsum, in1=gexp,
                                                    op0=ALU.mult, op1=ALU.mult))
                dve.wait_ge(ge_ready, head + 1)
                step(nc.vector.tensor_scalar(ge, ge, 1.0, 0.5, ALU.add, ALU.mult))
                nc.vector.tensor_tensor(wexp, wexp, ge, ALU.mult).then_inc(w_ready, 1)

            dve.wait_ge(iota_ready, 1)
            for t in range(NT):
                before = steps[0]
                with dve.Fori(0, PEER_HEADS // 2) as i:
                    per_turn = LOOP_STEPS
                    steps[1] = i * per_turn
                    for hh in range(2):
                        choose(t, i, hh)
                        weigh(t, i, hh)
                    assert steps[0] - before == per_turn, steps[0] - before
                steps[0] += per_turn * (PEER_HEADS // 2 - 1)
                steps[1] = 0
            for t in range(NT):
                for n in range(2):
                    src = wait_full(dve, "expert", t, n)
                    b = read_of("expert", t, n)
                    nc.vector.tensor_tensor(x_sb[:, t, half(n)], x_sb[:, t, half(n)], src[:, :], ALU.add).then_inc(b, 1)
                    wait_read(dve, "expert", t, n)
                    nc.vector.memset(small[:, 229:230], 0.0).then_inc(x2_ready, 1)

            dve.wait_ge(gain_loaded[0], 32)
            for t in range(NT):
                norm(6 + t, x_sb[:, t, :], xn[:, t, :], 0).then_inc(norm_ready, 1)
            for t in range(NT):
                copy_half_T("nT", nT, t, 1)
            for c in range(2):
                src = wait_full(dve, "q2", c)
                nc.vector.tensor_scalar(q3T[:, 2 * c:2 * c + 2, :], src[:, :].rearrange("p (a b) -> p a b", a=2),
                                        HD ** -0.5, None, ALU.mult).then_inc(read_of("q2", c), 1)

            def z_softplus(h):
                dve.wait_ge(z_ln, h + 1)
                src = bank[at("z", h)[0]]
                step(nc.vector.scalar_tensor_tensor(out=sp_e[:, h % 2, :], in0=src[:, 0:384], scalar=0.0,
                                                    in1=sp_e[:, h % 2, :], op0=ALU.max, op1=ALU.add))
                nc.vector.tensor_tensor(sp_l[:, h % 2, :], sp_e[:, h % 2, :], mask01, ALU.mult).then_inc(l_ready, 1)

            def z_weight(h):
                dve.wait_ge(cumulated, h + 1)
                if h >= 4:
                    if h % 2 == 0:
                        dve.wait_ge(even_sb, (h - 4) // 2 + 1)
                    else:
                        wait_full(dve, "sbT", (h - 4) // 2)
                src = bank[at("z", h)[0]]
                b = read_of("z", h)
                nc.vector.tensor_scalar(att[:, h % 4, :], src[:, 0:384], 0.0, None, ALU.min).then_inc(b, 1)
                wait_read(dve, "z", h)
                nc.vector.tensor_tensor(att[:, h % 4, :], att[:, h % 4, :], maskneg, ALU.add).then_inc(att_in, 1)

            for i in range(GATE_UNITS):
                if 1 <= i <= HEADS:
                    z_weight(i - 1)
                if i < HEADS:
                    z_softplus(i)
                if i >= 3 and i % 2 == 1 and (i - 3) // 2 < HEADS // 2:
                    c = (i - 3) // 2
                    src = wait_full(dve, "sbT", c)
                    nc.vector.tensor_copy(sbT[:, c, :], src[:, 0:S]).then_inc(read_of("sbT", c), 1)
                if i in (10, 11):
                    c = i - 10
                    src = wait_full(dve, "poolT", c)
                    for a in range(2):
                        g = 2 * c + a
                        ins = nc.vector.tensor_scalar(poolT[:, g, :], src[:, a * S:(a + 1) * S],
                                                      cols[:, 10 + g:11 + g], None, ALU.mult)
                        ins.then_inc(read_of("poolT", c) if a else merged_ready, 1)
            for t in range(NT):
                for j in range(2):
                    n = 4 * t + 2 * j
                    src = wait_full(dve, "xs", t, j)
                    step(nc.vector.tensor_reduce(xstat[:, 0, n:n + 2], src[:, :].rearrange("p (a b) -> p a b", a=2),
                                                 AX_X, ALU.max))
                    nc.vector.tensor_scalar(xstat[:, 1, n:n + 2], xstat[:, 0, n:n + 2], -HD ** -0.5, None,
                                            ALU.mult).then_inc(xmax, 1)
            for i in range(GATE_UNITS):
                wait_read(dve, "gate", i // NT, i % NT)
            for t in range(NT):
                step(nc.vector.tensor_scalar(gates[:, t, :], gates[:, t, :], 1.0, None, ALU.add))
                step(nc.vector.reciprocal(gates[:, t, :], gates[:, t, :]))
            for t in range(NT):
                for j in range(2):
                    n = 4 * t + 2 * j
                    wait_read(dve, "xs", t, j)
                    step(nc.vector.reciprocal(xstat[:, 3, n:n + 2], xstat[:, 2, n:n + 2]))
                    for a in range(2):
                        nc.vector.tensor_scalar(xprob[:, n + a, :], xprob[:, n + a, :], xstat[:, 3, n + a:n + a + 1],
                                                None, ALU.mult).then_inc(xprob_ready, 1)
            for t in range(NT):
                for n in range(2):
                    src = wait_full(dve, "y_pool", t, n)
                    nc.vector.tensor_tensor(xn[:, t, half(n)], gates[:, t, half(n)], src[:, :],
                                            ALU.mult).then_inc(read_of("y_pool", t, n), 1)
            for t in range(NT):
                for n in range(2):
                    src = wait_full(dve, "y_sb", t, n)
                    nc.vector.tensor_tensor(tmp, gates[:, t, half(2 + n)], src[:, :],
                                            ALU.mult).then_inc(read_of("y_sb", t, n), 1)
                    wait_read(dve, "y_sb", t, n)
                    step(nc.vector.tensor_tensor(xn[:, t, half(n)], xn[:, t, half(n)], tmp, ALU.add))
            for c in range(2):
                src = wait_full(dve, "xoT", c)
                nc.vector.tensor_copy(xoT[:, c, :], src[:, 0:S]).then_inc(read_of("xoT", c), 1)
            for t in range(NT):
                for n in range(2):
                    src = wait_full(dve, "y_x", t, n)
                    nc.vector.tensor_tensor(tmp, gates[:, t, half(4 + n)], src[:, :],
                                            ALU.mult).then_inc(read_of("y_x", t, n), 1)
                    wait_read(dve, "y_x", t, n)
                    nc.vector.tensor_tensor(xn[:, t, half(n)], xn[:, t, half(n)], tmp, ALU.add).then_inc(merged_ready, 1)
                    dve.wait_ge(merged_ready, 2 + 2 * t + n + 1)
            for t in range(NT):
                copy_half_T("mergedT", nT, t, 1)
            dve.wait_ge(gain_loaded[1], 32)
            for t in range(NT):
                norm(8 + t, z_sb[:, t, :], z_sb[:, t, :], 1).then_inc(norm_ready, 1)
                dve.wait_ge(norm_ready, 9 + t)
                nc.vector.tensor_tensor(x_sb[:, t, :], x_sb[:, t, :], z_sb[:, t, :], ALU.add).then_inc(h_ready, 1)
            dve.wait_ge(gain_loaded[2], 32)
            for t in range(NT):
                norm(10 + t, x_sb[:, t, :], xn[:, t, :], 2).then_inc(norm_ready, 1)
            for t in range(NT):
                copy_half_T("n2T", nT, t, 1)
            for j in range(FC):
                dve.wait_ge(silu_ready, j + 1)
                src = bank[at("ff", j)[0]]
                nc.vector.tensor_tensor(hT[:, j, :], silu[:, j % 2, :], src[:, S:2 * S],
                                        ALU.mult).then_inc(read_of("ff", j), 1)
            dve.wait_ge(gain_loaded[1], 48)
            for t in range(NT):
                norm(12 + t, z_sb[:, t, :], z_sb[:, t, :], 1).then_inc(norm_ready, 1)
                dve.wait_ge(norm_ready, 13 + t)
                nc.vector.tensor_tensor(x_sb[:, t, :], x_sb[:, t, :], z_sb[:, t, :], ALU.add).then_inc(h_ready, 1)

        @block.tensor
        def _(pe):
            def open_bank(*key):
                b, u = at(*key)
                if u:
                    pe.wait_ge(bank_read[b], u)
                return bank[b]

            def transposes(src, *key):
                dst = open_bank(*key)
                n = src.shape[1] // P
                for c in range(n):
                    mm = nc.tensor.transpose(dst[:, c * P:(c + 1) * P], src[:, c * P:(c + 1) * P], ident)
                mm.then_inc(full_of(*key), 1)

            def tokens_out(w, lhsT, t, *key, chunks=KC, off=0, width=HALF, pitch=HALF):
                dst = open_bank(*key)
                for c in range(chunks):
                    mm = nc.tensor.matmul(dst[:, 0:width], lhsT[:, c, tok(t)],
                                          w[:, c * pitch + off:c * pitch + off + width],
                                          start=(c == 0), stop=(c == chunks - 1))
                mm.then_inc(full_of(*key), 1)

            def channels_out(w, dst, off, pitch=HALF):
                for c in range(KC):
                    mm = nc.tensor.matmul(dst, w[:, c * pitch + off:c * pitch + off + P], nT[:, c, :],
                                          start=(c == 0), stop=(c == KC - 1))
                return mm

            def normed_T(n, name, src):
                for t in range(NT):
                    pe.wait_ge(norm_ready, n + t + 1)
                    for h in range(2):
                        transposes(src[:, t, half(h)], name, t, h)

            def T_ready(name):
                for t in range(NT):
                    for h in range(2):
                        wait_read(pe, name, t, h)

            pe.wait_ge(const_loaded, 32)
            normed_T(0, "xT", xn)
            T_ready("xT")
            for n in range(5):
                w = block_wait(pe, f"in{n}")
                for t in range(NT):
                    tokens_out(w, nT, t, "proj", n, t)
            for name, n, src in (("qT", 2, q_sb), ("kT", 3, k_sb)):
                for t in range(NT):
                    wait_read(pe, "proj", n, t)
                    transposes(src[:, t, :], name, t)

            def scores(h):
                dst = open_bank("score", h)
                r, c = slice(HD * (h % 2), HD * (h % 2) + HD), h // 2
                nc.tensor.matmul(dst[:, 0:P], qT[r, c, 0:P], kT[r, c, 0:P], start=True, stop=True)
                nc.tensor.matmul(dst[:, P:384], qT[r, c, P:S], kT[r, c, 0:S], start=True,
                                 stop=True).then_inc(full_of("score", h), 1)

            for name in ("qT", "kT"):
                for t in range(NT):
                    wait_read(pe, name, t)
            scores(0)
            scores(1)
            for t in range(NT):
                wait_read(pe, "proj", 4, t)
            for h in range(HEADS):
                if h + 2 < HEADS:
                    scores(h + 2)
                pe.wait_ge(prob_ready, 2 * h + 2)
                transposes(prob[:, h % 4, :], "pT", h)
                if h % 2 == 0:
                    dst_o = open_bank("oT", h // 2)
                wait_read(pe, "pT", h)
                r = slice(HD * (h % 2), HD * (h % 2) + HD)
                nc.tensor.matmul(dst_o[r, 0:S], v_sb[:, 0, h * HD:(h + 1) * HD], probT[:, h % 2, 0:S],
                                 start=True, stop=False)
                mm = nc.tensor.matmul(dst_o[r, P:S], v_sb[:, 1, h * HD:(h + 1) * HD], probT[:, h % 2, S:384],
                                      start=False, stop=True)
                mm.then_inc(full_of("oT", h // 2) if h % 2 else even_o, 1)
                if h in (1, 3):
                    t = h // 2
                    pe.wait_ge(v_normed, t + 1)
                    pe.wait_ge(w_masked, 1)
                    dst = open_bank("spatial", t)
                    for g in range(8):
                        mm = nc.tensor.matmul(dst[:, g * GD:(g + 1) * GD], w_sT[:, g, :], vg[:, t, g * GD:(g + 1) * GD],
                                              start=True, stop=True)
                    mm.then_inc(full_of("spatial", t), 1)
                if h in (5, 7):
                    t = h // 2 - 2
                    wait_read(pe, "spatial", t)
                    transposes(u_sb[:, t, :], "aT", t)
            for c in range(4):
                wait_read(pe, "oT", c)
            for t in range(NT):
                wait_read(pe, "aT", t)
            for n in range(2):
                w = block_wait(pe, f"out{n}")
                for t in range(NT):
                    tokens_out(w, catT, t, "w_out", n, t)
            normed_T(2, "xbT", xn)
            T_ready("xbT")
            for j in range(PEER_HEADS):
                w = block_wait(pe, f"query{j // 2}")
                dst = open_bank("query", j)
                for a in range(2):
                    mm = channels_out(w, dst[:, a * S:(a + 1) * S], ((2 * j + a) % 4) * P)
                mm.then_inc(full_of("query", j), 1)
            pe.wait_ge(subk_loaded, 16)
            for t in range(NT):
                for j in range(HP // 4):
                    dst = open_bank("route", t, j)
                    wait_read(pe, "query", 2 * j)
                    wait_read(pe, "query", 2 * j + 1)
                    for a in range(4):
                        mm = nc.tensor.matmul(dst[:, a * NKEYS:(a + 1) * NKEYS], q2T[:, 4 * j + a, tok(t)],
                                              sub_kT[:, 4 * j + a, :], start=True, stop=True)
                    mm.then_inc(full_of("route", t, j), 1)
            w = block_wait(pe, "mem")
            normed_T(4, "memT", w[:, 0:NT * D].rearrange("p (t d) -> p t d", t=NT))
            T_ready("memT")
            w = block_wait(pe, "mem_kv")
            dst = open_bank("mk")
            for c in range(2):
                mm = channels_out(w, dst[:, c * S:(c + 1) * S], c * P)
            mm.then_inc(full_of("mk"), 1)
            dst = open_bank("mv")
            for t in range(NT):
                for c in range(KC):
                    mm = nc.tensor.matmul(dst[:, t * 256:(t + 1) * 256], nT[:, c, tok(t)],
                                          w[:, c * HALF + 256:(c + 1) * HALF], start=(c == 0), stop=(c == KC - 1))
            mm.then_inc(full_of("mv"), 1)

            zeros = const[:, 3 * P + 768:3 * P + 768 + P]
            for t in range(NT):
                acc = [open_bank("expert", t, n) for n in range(2)]
                for n in range(2):
                    nc.tensor.matmul(acc[n][:, :], zeros, const[:, 0:HALF], start=True, stop=False)
                with pe.Fori(0, PEER_HEADS // 2) as i:
                    for hh in range(2):
                        head = t * PEER_HEADS + i * 2 + hh
                        for k in range(TOPK):
                            pe.wait_ge(v_loaded[k % RING], head * 32 + 16 * (k // RING) + 16)
                            pe.wait_ge(diag_ready, head * TOPK + k + 1)
                            for n in range(2):
                                mm = nc.tensor.matmul(acc[n][:, :], diag[:, k % RING, :], v_ring[:, k % RING, half(n)],
                                                      start=False, stop=False)
                            mm.then_inc(v_used, 1)
                for n in range(2):
                    nc.tensor.matmul(acc[n][:, :], zeros, const[:, 0:HALF], start=False,
                                     stop=True).then_inc(full_of("expert", t, n), 1)

            normed_T(6, "nT", xn)
            T_ready("nT")
            w = block_wait(pe, "in2_p")
            for t in range(NT):
                tokens_out(w, nT, t, "pool_in", t)
            for name, key in (("in2_q", "q2"), ("in2_k", "k2")):
                w = block_wait(pe, name)
                for c in range(2):
                    dst = open_bank(key, c)
                    for a in range(2):
                        mm = channels_out(w, dst[:, a * S:(a + 1) * S], (2 * c + a) * P)
                    mm.then_inc(full_of(key, c), 1)
            w = block_wait(pe, "in2_v")
            for t in range(NT):
                tokens_out(w, nT, t, "v2", t)
            for c in range(2):
                wait_read(pe, "q2", c)
                wait_read(pe, "k2", c)
            for t in range(NT):
                wait_read(pe, "v2", t)
            for i in range(GATE_UNITS):
                w = block_wait(pe, f"in2_g{i // NT}")
                tokens_out(w, nT, i % NT, "gate", i // NT, i % NT)
                if i < HEADS:
                    dst = open_bank("z", i)
                    r, c = slice(HD * (i % 2), HD * (i % 2) + HD), i // 2
                    nc.tensor.matmul(dst[:, 0:S], k3T[r, c, 0:P], q3T[r, c, 0:S], start=True, stop=False)
                    nc.tensor.matmul(dst[:, S:384], k3T[r, c, P:S], q3T[r, c, P:S], start=False,
                                     stop=True).then_inc(full_of("z", i), 1)
                if 1 <= i <= HEADS:
                    g = i - 1
                    pe.wait_ge(l_ready, g + 1)
                    dst = bank[at("z", g)[0]]
                    nc.tensor.matmul(dst[:, 0:S], negtri, sp_l[:, g % 2, 0:S], start=False, stop=False,
                                     skip_group_check=True)
                    nc.tensor.matmul(dst[:, P:S], negones, sp_l[:, g % 2, S:384], start=False, stop=False,
                                     skip_group_check=True)
                    nc.tensor.matmul(dst[:, S:384], negtri, sp_l[:, g % 2, S:384], start=False, stop=True,
                                     skip_group_check=True).then_inc(cumulated, 1)
                if 2 <= i < HEADS + 2:
                    g = i - 2
                    if g % 2 == 0:
                        dst_s = open_bank("sbT", g // 2)
                    pe.wait_ge(att_ready, g + 1)
                    r = slice(HD * (g % 2), HD * (g % 2) + HD)
                    nc.tensor.matmul(dst_s[r, 0:S], v3[:, 0, g * HD:(g + 1) * HD], att[:, g % 4, 0:S],
                                     start=True, stop=False)
                    mm = nc.tensor.matmul(dst_s[r, P:S], v3[:, 1, g * HD:(g + 1) * HD], att[:, g % 4, S:384],
                                          start=False, stop=True)
                    mm.then_inc(full_of("sbT", g // 2) if g % 2 else even_sb, 1)
                if i in (8, 9):
                    c = i - 8
                    if c == 0:
                        pe.wait_ge(pool_loaded, 32)
                        for t in range(NT):
                            wait_read(pe, "pool_in", t)
                    dst = open_bank("mix", c)
                    for a in range(2):
                        g = 2 * c + a
                        nc.tensor.matmul(dst[:, a * S:(a + 1) * S], p_sb[:, 0, g * P:(g + 1) * P], band[:, g, 0:S],
                                         start=True, stop=False)
                        mm = nc.tensor.matmul(dst[:, a * S + P:(a + 1) * S], p_sb[:, 1, g * P:(g + 1) * P],
                                              band[:, g, S:384], start=False, stop=True)
                    mm.then_inc(full_of("mix", c), 1)
                if i in (10, 11):
                    c = i - 10
                    dst = open_bank("poolT", c)
                    wait_read(pe, "mix", c)
                    for a in range(2):
                        g = 2 * c + a
                        mm = nc.tensor.matmul(dst[:, a * S:(a + 1) * S], w_mix[:, g, :], mixT[:, g, :],
                                              start=True, stop=True)
                    mm.then_inc(full_of("poolT", c), 1)
            w = block_wait(pe, "in2_x")
            dst = open_bank("xq")
            for c in range(2):
                mm = channels_out(w, dst[:, c * S:(c + 1) * S], c * P, pitch=256)
            mm.then_inc(full_of("xq"), 1)
            wait_read(pe, "xq")
            wait_read(pe, "mk")
            for t in range(NT):
                for j in range(2):
                    dst = open_bank("xs", t, j)
                    r = slice(HD * j, HD * j + HD)
                    for a in range(2):
                        mm = nc.tensor.matmul(dst[:, a * S:(a + 1) * S], xqT[r, a, tok(t)], mkT[r, a, :],
                                              start=True, stop=True)
                    mm.then_inc(full_of("xs", t, j), 1)
            for name, key, src, src_key in (("pool_o", "y_pool", poolT, "poolT"), ("sb_o", "y_sb", sbT, "sbT")):
                w = block_wait(pe, name)
                for c in range(2 if key == "y_pool" else 4):
                    wait_read(pe, src_key, c)
                for t in range(NT):
                    for n in range(2):
                        tokens_out(w, src, t, key, t, n, chunks=4, off=n * HALF, pitch=D)
            for h in range(XHEADS):
                if h == 0:
                    pe.wait_ge(xprob_ready, 2 * XHEADS)
                dst = open_bank("xpT", h)
                for c in range(2):
                    for t in range(NT):
                        src = xprob[:, 4 * t + 2 * (h % 2) + h // 2, c * P:(c + 1) * P]
                        mm = nc.tensor.transpose(dst[:, c * S + t * P:c * S + (t + 1) * P], src, ident)
                mm.then_inc(full_of("xpT", h), 1)
                if h % 2 == 0:
                    dst_x = open_bank("xoT", h // 2)
                wait_read(pe, "xpT", h)
                wait_read(pe, "mv")
                r = slice(HD * (h % 2), HD * (h % 2) + HD)
                for c in range(2):
                    mm = nc.tensor.matmul(dst_x[r, 0:S], mv[:, c, h * HD:(h + 1) * HD], xpT[:, h % 2, c * S:(c + 1) * S],
                                          start=(c == 0), stop=(c == 1))
                mm.then_inc(full_of("xoT", h // 2) if h % 2 else even_x, 1)
            w = block_wait(pe, "x_o")
            for c in range(2):
                wait_read(pe, "xoT", c)
            for t in range(NT):
                for n in range(2):
                    tokens_out(w, xoT, t, "y_x", t, n, chunks=2, off=n * HALF, pitch=D)
            for t in range(NT):
                pe.wait_ge(merged_ready, 2 + 2 * t + 2)
                for h in range(2):
                    transposes(xn[:, t, half(h)], "mergedT", t, h)
            T_ready("mergedT")
            for n in range(2):
                w = block_wait(pe, f"out2_{n}")
                for t in range(NT):
                    tokens_out(w, nT, t, "w_out2", n, t)
            normed_T(10, "n2T", xn)
            T_ready("n2T")
            for j in range(FC):
                w = block_wait(pe, f"ff_in{j // 2}")
                dst = open_bank("ff", j)
                for a in range(2):
                    mm = channels_out(w, dst[:, a * S:(a + 1) * S], (j % 2) * 2 * P + a * P)
                mm.then_inc(full_of("ff", j), 1)
            acc = {(t, n): open_bank("ff_out", t, n) for t in range(NT) for n in range(2)}
            for j in range(FC):
                w = block_wait(pe, f"ff_out{j // 4}")
                wait_read(pe, "ff", j)
                for t in range(NT):
                    for n in range(2):
                        mm = nc.tensor.matmul(acc[t, n][:, :], hT[:, j, tok(t)],
                                              w[:, (j % 4) * D + n * HALF:(j % 4) * D + (n + 1) * HALF],
                                              start=(j == 0), stop=(j == FC - 1))
                        if j == FC - 1:
                            mm.then_inc(full_of("ff_out", t, n), 1)
                if j < FC - 1:
                    mm.then_inc(ff_used, 1)


LOOP_STEPS = 50


def position_constants():
    import numpy as np

    key, query = np.arange(P)[:, None], np.arange(P)[None, :]
    before = (key < query).astype(np.float32)
    mask = np.concatenate([before, np.ones((P, P), np.float32), before], 1)
    const = np.concatenate([np.eye(P), -(key >= query).astype(np.float32), -np.ones((P, P)),
                            mask, np.where(mask > 0, 0.0, NEG), np.zeros((P, P))], 1)
    band = np.zeros((2 * P, 4, S), np.float32)
    s, t = np.arange(S)[:, None], np.arange(S)[None, :]
    for g, w in enumerate((2, 4, 8, 16)):
        inside = (s <= t) & (s > t - w)
        band[:, g] = inside / np.minimum(t + 1, w).astype(np.float32) - (s == t)
    band = np.concatenate([band[0:P], band[P:, :, P:]], 2)
    return const.astype(np.float32), band.astype(np.float32)


def lay_out(inputs):
    import numpy as np

    a = {k: np.asarray(v) for k, v in inputs.items()}
    a = {k: (v if k in ("x", "mem_2") else v[0]) for k, v in a.items()}
    io = {}

    def blocks(w, names, width=HALF):
        k = w.shape[0] // P
        for n, name in enumerate(names):
            part = w[:, n * width:(n + 1) * width].reshape(k, P, width)
            io[name] = part.transpose(1, 0, 2).reshape(P, k * width)

    io["x"] = a["x"][0]
    blocks(a["w_in"], [f"in{n}" for n in range(5)])
    blocks(a["w_out"], ["out0", "out1"])
    blocks(a["peer_w_query"], [f"query{n}" for n in range(4)])
    io["mem"] = a["mem_2"][0].reshape(NT, P, D).transpose(1, 0, 2).reshape(P, NT * D)
    blocks(a["w_mem_kv_2"], ["mem_kv"])
    w = a["w_in_2"]
    blocks(w[:, 0:2048], ["in2_p", "in2_q", "in2_k", "in2_v"])
    blocks(w[:, 2048:2304], ["in2_x"], 256)
    blocks(w[:, 2304:], [f"in2_g{n}" for n in range(N_GATES)])
    blocks(a["w_pool_o_2"], ["pool_o"], D)
    blocks(a["w_sb_o_2"], ["sb_o"], D)
    blocks(a["w_x_o_2"], ["x_o"], D)
    blocks(a["w_out_2"], ["out2_0", "out2_1"])
    w = a["w_ffn_in_2"].reshape(D, 2, FC, P).transpose(0, 2, 1, 3).reshape(D, 2 * DFF)
    blocks(w, [f"ff_in{n}" for n in range(FC // 2)])
    w = a["w_ffn_out_2"]
    for n in range((FC + 3) // 4):
        blocks(w[n * HALF:(n + 1) * HALF], [f"ff_out{n}"], D)
    io["w_sT"] = a["gmlp_w_s"].transpose(2, 0, 1)
    rel = np.clip(P + np.arange(P)[:, None] - np.arange(S)[None, :], -P, P) + P
    io["rel"] = a["rel_bias"][:, rel].transpose(1, 0, 2)
    io["sub_kT"] = a["peer_sub_keys"].reshape(HP, NKEYS, P).transpose(2, 0, 1)
    io["w_mix"] = a["w_pool_mix_2"].transpose(1, 0, 2)
    cols = np.zeros((P, 16), np.float32)
    cols[:, 0] = np.tile(a["q_norm_g"], 2)
    cols[:, 1] = np.tile(a["k_norm_g"], 2)
    cols[:, 2:10] = a["gmlp_b_s"].T
    cols[:, 10:14] = a["pool_scale_2"].reshape(4, P).T
    io["cols"] = cols
    for name in ("ln_mix_g", "gmlp_norm_g", "ln_ffn_g", "norm_mix_pre_2", "norm_mem_2", "norm_mix_post_2",
                 "norm_ffn_pre_2", "norm_ffn_post_2", "peer_u", "peer_v"):
        io[name] = a[name]
    io["const"], io["band"] = position_constants()
    return {k: np.ascontiguousarray(v) for k, v in io.items()}


def kernel(**inputs):
    import concourse.bacc as bacc
    from concourse.bass_utils import run_bass_kernel_spmd

    nc = bacc.Bacc("TRN2", target_bir_lowering=False, num_devices=1)
    arrays = lay_out(inputs)
    io = {k: nc.dram_tensor("in_" + k, v.shape, mybir.dt.from_np(v.dtype), kind="ExternalInput").ap() for k, v in arrays.items()}
    out = nc.dram_tensor("out_y", (S, D), F32, kind="ExternalOutput").ap()
    two_block_kernel(nc, io, out)
    r = run_bass_kernel_spmd(nc, [{"in_" + k: v for k, v in arrays.items()}], core_ids=[0])
    return r.results[0]["out_y"].reshape(1, S, D)
```

```python
from contextlib import ExitStack

import concourse.bass as bass
from concourse import mybir

F32 = mybir.dt.float32
F32R = mybir.dt.float32r
BF16 = mybir.dt.bfloat16
U32 = mybir.dt.uint32
ALU = mybir.AluOpType
ACT = mybir.ActivationFunctionType
AX_X = mybir.AxisListType.X

P = 128
D = 1024
S = 256
NT = S // P
KC = D // P
HALF = 512
EPS = 1e-6
NEG = -1e30
CHUNK = 64
GD = 64
HD = 64
HEADS = 8
PAIRS = HEADS // 2
XHEADS = 4
PEER_HEADS = 8
TOPK = 16
NKEYS = 128
HP = 2 * PEER_HEADS
DFF = 2816
FC = DFF // P
GELU_C = 0.7978845608028654
GELU_A = 0.044715
WB = 2048
R_SLOTS = 4
S_SLOTS = 3
RING = 8
N_GATES = 3 * D // HALF
PEELED = 4
LOOP_STEPS = 50
DVE_ROWS = range(RING + 1, TOPK, 2)
PE_ROWS = [k for k in range(TOPK) if k not in DVE_ROWS]

SLOT_BLOCKS = (["in2_va", "in2_vb", "in2_pa", "in2_pb", "in2_x"]
               + [f"in2_g{n}{p}" for n in range(N_GATES) for p in "ab"])
BLOCKS = ([f"in{n}{p}" for n in (1, 2, 3, 4, 0) for p in "ab"]
          + [f"out{n}{p}" for n in range(2) for p in "ab"] + ["mem"] + [f"query{j}" for j in range(PEER_HEADS)]
          + ["mem_k", "mem_v", "in2_q0", "in2_q1", "in2_k0", "in2_k1"] + SLOT_BLOCKS
          + ["x_o", "pool_o0", "pool_o1", "sb_o0", "sb_o1"] + [f"out2_{n}{p}" for n in range(2) for p in "ab"]
          + [f"ff_in{j}" for j in range(FC)] + [f"ff_out{j}" for j in range(FC // 2)])
BLOCK_AT = {name: n for n, name in enumerate(BLOCKS)}
SPLIT = [name for name in BLOCKS if not name.startswith(("query", "mem"))]
SPLIT_AT = {name: n for n, name in enumerate(SPLIT)}
RAW_USE = {f"query{j}": ("query", j) for j in range(PEER_HEADS)} | {"mem_k": ("mk",), "mem_v": ("mv",)}


def last_product(name):
    base, part = name[:-1], name[-1]
    if name in ("in2_x", "x_o"):
        return ("xq",) if name == "in2_x" else ("y_x", NT - 1, 1)
    if name.startswith(("in2_q", "in2_k")):
        return (name[4:5] + "2", int(part))
    if name.startswith("ff_in"):
        return ("ff", int(name[5:]))
    if name.startswith("ff_out"):
        return ("ff_out", NT - 1, 1) if name == f"ff_out{FC // 2 - 1}" else None
    if name.startswith(("pool_o", "sb_o")):
        return ("y_" + base[:-2], NT - 1, 1) if part == "1" else None
    if part == "a":
        return None
    if name.startswith("in2_g"):
        return ("gate", int(name[5:-1]), NT - 1)
    if name in ("in2_vb", "in2_pb"):
        return (("v2", NT - 1) if name == "in2_vb" else ("pool_in", NT - 1))
    if name.startswith("out2_"):
        return ("w_out2", int(name[5:-1]), NT - 1)
    return ("proj" if name.startswith("in") else "w_out", int(name[-2]), NT - 1)


PART_AT = {}
for _name in SPLIT:
    if last_product(_name) is None:
        PART_AT[_name] = len(PART_AT) + 1

UNITS = [(0, (0, 2, 4, 6)), (0, (1, 3, 5, 7)), (1, (0, 2)), (1, (1, 3)), (1, (4, 6)), (1, (5, 7))]
BIAS_HEADS = (0, 2, 4, 6, 1, 3, 5, 7)
HEADS_DONE = (3, 5)

Z_SLOT, CUM_SLOT, ATT_SLOT = 0, 2, 4
MIX_SLOT, POOL_SLOT = (9, 11), (12, 13)
XS_SLOT = (8, 10)
XPT_SLOT, XO_SLOT = 12, 13


def pair_at(i, first):
    p = (i - first) // 2
    return p if (i - first) % 2 == 0 and 0 <= p < PAIRS else None


def psum_uses():
    uses, count, turn, held = {}, [0] * 8, {}, set()

    def use(*key, among=tuple(range(8))):
        free = [b for b in among if b not in held]
        n = turn.get(among, 0)
        while among[n % len(among)] not in free:
            n += 1
        b = among[n % len(among)]
        turn[among] = n + 1
        uses[key] = (b, count[b])
        count[b] += 1
        return b

    def both(name):
        for t in range(NT):
            for h in range(2):
                use(name, t, h)

    both("xT")
    for n in (1, 2, 3, 4):
        for t in range(NT):
            use("proj", n, t)
    for name in ("qT", "kT"):
        for t in range(NT):
            use(name, t)
    use("score", 0)
    use("score", 1)
    for t in range(NT):
        use("proj", 0, t)
    for u in range(len(UNITS)):
        if u + 2 < len(UNITS):
            use("score", u + 2)
        use("pT", u)
        if u == 0:
            held.add(use("oT", 0))
            held.add(use("oT", 1))
        if u in (1, 3):
            use("spatial", u // 2)
        if u in (4, 5):
            use("aT", u - 4)
    held.clear()
    for n in range(2):
        for t in range(NT):
            use("w_out", n, t)
    both("xbT")
    for j in range(4):
        use("query", j)
        use("route", j)
    for n in range(2):
        held.add(use("expert", 0, n))
    for j in range(4, PEER_HEADS):
        use("query", j)
        use("route", j)
    both("memT")
    use("mk")
    use("mv")
    held.clear()
    for n in range(2):
        held.add(use("expert", 1, n))
    both("nT")
    held.clear()
    for key in ("q2", "k2"):
        for c in range(2):
            use(key, c)
    z_banks, sum_banks, one = (0, 1, 2, 3), (4, 5, 6), (7,)
    for i, name in enumerate(SLOT_BLOCKS):
        if pair_at(i, ATT_SLOT) is not None:
            use("sbT", pair_at(i, ATT_SLOT), among=one)
        if pair_at(i, Z_SLOT) is not None:
            for a in range(2):
                use("z", 2 * pair_at(i, Z_SLOT) + a, among=z_banks)
        if i in XS_SLOT:
            for j in range(2):
                use("xs", XS_SLOT.index(i), j, among=z_banks)
        if i in MIX_SLOT:
            use("mix", MIX_SLOT.index(i), among=one)
        if i in POOL_SLOT:
            use("poolT", POOL_SLOT.index(i), among=one)
        if 0 <= i - XPT_SLOT < XHEADS:
            use("xpT", i - XPT_SLOT, among=z_banks)
        if 0 <= i - XO_SLOT < XHEADS and (i - XO_SLOT) % 2 == 0:
            use("xoT", (i - XO_SLOT) // 2, among=z_banks)
        if name == "in2_x":
            use("xq", among=sum_banks)
        elif name[-1] == "a":
            for t in range(NT):
                use(*slot_key(name, t), among=sum_banks)
    for key in ("y_x", "y_pool", "y_sb"):
        for t in range(NT):
            for n in range(2):
                use(key, t, n)
    both("mergedT")
    for n in range(2):
        for t in range(NT):
            use("w_out2", n, t)
    both("n2T")
    for j in range(FC):
        use("ff", j)
    for t in range(NT):
        for n in range(2):
            use("ff_out", t, n)
    return uses


def slot_key(name, t):
    if name.startswith("in2_g"):
        return ("gate", int(name[5:-1]), t)
    return ("v2", t) if name.startswith("in2_v") else ("pool_in", t)


def rounded_order():
    keys = [("xT", t, h) for t in range(NT) for h in range(2)]
    keys += [("oT", 0), ("aT", 0), ("aT", 1), ("oT", 1)]
    keys += [("nT", t, h) for t in range(NT) for h in range(2)]
    for i in range(len(SLOT_BLOCKS)):
        if pair_at(i, ATT_SLOT) is not None:
            keys.append(("sbT", pair_at(i, ATT_SLOT)))
        if i in POOL_SLOT:
            keys.append(("poolT", POOL_SLOT.index(i)))
        if 0 <= i - XO_SLOT < XHEADS and (i - XO_SLOT) % 2 == 1:
            keys.append(("xoT", (i - XO_SLOT) // 2))
    keys += [("mergedT", t, h) for t in range(NT) for h in range(2)]
    keys += [("n2T", t, h) for t in range(NT) for h in range(2)]
    return {key: n for n, key in enumerate(keys)}


def two_block_kernel(nc, io, out):
    bank_use = psum_uses()
    rounded = rounded_order()

    def at(*key):
        return bank_use[key]

    with ExitStack() as ctx:
        def sb(name, shape, dt=F32):
            return ctx.enter_context(nc.sbuf_tensor(name, shape, dt))

        def sem(name):
            return ctx.enter_context(nc.semaphore(name))

        bank = [ctx.enter_context(nc.psum_tensor(f"bank{b}", [P, HALF], F32)) for b in range(8)]

        x_sb = sb("x_sb", [P, NT, D])
        xn = sb("xn", [P, NT, D])
        wraw = sb("wraw", [P, R_SLOTS, WB])
        gain = sb("gain", [P, 2, D])
        const = sb("const", [P, 4 * P + 2 * 384])
        cols = sb("cols", [P, 16])
        mkT = sb("mkT", [P, 2, S])
        mv = sb("mv", [P, NT, 256])
        stat = sb("stat", [P, 3, 16])
        junk = sb("junk", [P, D], BF16)
        eps = sb("eps", [P, 1])
        small = sb("small", [P, 256])
        rank = sb("rank", [P, 4, TOPK], U32)
        eidx = sb("eidx", [P, 2, TOPK], U32)
        attn_stat = sb("attn_stat", [P, 4, len(UNITS), 4])
        qk_stat = sb("qk_stat", [P, 3, 4, HEADS])
        xstat = sb("xstat", [P, 4, 8])

        arena_bytes = 141312
        arena = sb("arena", [P, arena_bytes // 4])
        first_byte = nc.sbuf_base - arena_bytes

        def place(name, off, shape, dt=F32):
            size = 4
            for n in shape[1:]:
                size *= n
            assert off + size <= arena_bytes, name
            return nc.alloc_sbuf_tensor_at(name, shape, dt, offset=first_byte + off)

        KB = 1024
        w_hi = place("w_hi", 0, [P, S_SLOTS, WB], F32R)
        w_lo = place("w_lo", 24 * KB, [P, S_SLOTS, WB], F32R)
        aT_hi = place("aT_hi", 48 * KB, [P, KC, S], F32R)
        aT_lo = place("aT_lo", 56 * KB, [P, KC, S], F32R)
        u_sb = place("u_sb", 64 * KB, [P, NT, HALF])
        vg = place("vg", 68 * KB, [P, NT, HALF])
        q_sb = place("q_sb", 72 * KB, [P, NT, HALF])
        k_sb = place("k_sb", 76 * KB, [P, NT, HALF])
        v_sb = place("v_sb", 80 * KB, [P, NT, HALF])
        w_sT = place("w_sT", 84 * KB, [P, 8, P])
        bias0 = place("bias0", 88 * KB, [P, HEADS, P])
        bias1 = place("bias1", 92 * KB, [P, HEADS, S])
        qT = place("qT", 100 * KB, [P, 4, S])
        kT = place("kT", 104 * KB, [P, 4, S])
        sq = place("sq", 108 * KB, [P, 4, HALF])
        prob = place("prob", 108 * KB, [P, 3, HALF])
        probT = place("probT", 116 * KB, [P, 2, HALF])
        gmlp_g = place("gmlp_g", 120 * KB, [P, HALF])
        mem_n = place("mem_n", 122 * KB, [P, NT, D])
        sub_kT = place("sub_kT", 130 * KB, [P, HP, NKEYS])
        u_ring = place("u_ring", 0, [P, RING, D])
        v_ring = place("v_ring", 32 * KB, [P, RING, D])
        diag = place("diag", 64 * KB, [P, RING, P])
        route = place("route", 68 * KB, [P, NT * PEER_HEADS * 2 * NKEYS])
        head_sc = place("head_sc", 84 * KB, [P, 2, NKEYS])
        head_sc2 = place("head_sc2", 85 * KB, [P, 2, NKEYS])
        cand = place("cand", 86 * KB, [P, TOPK * TOPK])
        cand2 = place("cand2", 87 * KB, [P, TOPK * TOPK])
        onehot = place("onehot", 88 * KB, [P, 2, TOPK, TOPK])
        q2T = place("q2T", 90 * KB, [P, 2, 2, S])
        bT = place("bT", 94 * KB, [P, KC, S])
        nT_hi = place("nT_hi", 102 * KB, [P, KC, S], F32R)
        nT_lo = place("nT_lo", 110 * KB, [P, KC, S], F32R)
        gates = place("gates", 48 * KB, [P, NT, 3 * D])
        xqT = place("xqT", 70 * KB, [P, 2, S])
        sbT_hi = place("sbT_hi", 72 * KB, [P, 4, S], F32R)
        sbT_lo = place("sbT_lo", 76 * KB, [P, 4, S], F32R)
        poolT_hi = place("poolT_hi", 80 * KB, [P, 4, S], F32R)
        poolT_lo = place("poolT_lo", 84 * KB, [P, 4, S], F32R)
        p_sb = place("p_sb", 88 * KB, [P, NT, HALF])
        k3T = place("k3T", 92 * KB, [P, 4, S])
        v3 = place("v3", 96 * KB, [P, NT, HALF])
        w_mix = place("w_mix", 100 * KB, [P, 4, P])
        q3T = place("q3T", 118 * KB, [P, 4, S])
        mixT = place("mixT", 118 * KB, [P, 4, S])
        sp_e = place("sp_e", 122 * KB, [P, 2, 384])
        sp_l = place("sp_l", 125 * KB, [P, 2, 384])
        att = place("att", 128 * KB, [P, 2, 384])
        band = place("band", 131 * KB, [P, 4, 384])
        xprob = place("xprob", 92 * KB, [P, 8, S])
        xpT = place("xpT", 122 * KB, [P, 2, HALF])
        xoT_hi = place("xoT_hi", 128 * KB, [P, 2, S], F32R)
        xoT_lo = place("xoT_lo", 130 * KB, [P, 2, S], F32R)
        tmp = place("tmp", 132 * KB, [P, HALF])
        hT_hi = place("hT_hi", 48 * KB, [P, FC, S], F32R)
        hT_lo = place("hT_lo", 70 * KB, [P, FC, S], F32R)
        z_sb = place("z_sb", 92 * KB, [P, NT, D])
        silu = place("silu", 118 * KB, [P, 2, S])
        h32 = place("h32", 120 * KB, [P, 2, S])

        ident = const[:, 0:P]
        negtri = const[:, P:2 * P]
        negones = const[:, 2 * P:3 * P]
        mask01 = const[:, 3 * P:3 * P + 384]
        maskneg = const[:, 3 * P + 384:3 * P + 768]
        zeros = const[:, 3 * P + 768:4 * P + 768]
        top = small[:, 0:32].rearrange("p (a b) -> p a b", a=2)
        topi = small[:, 32:64].rearrange("p (a b) -> p a b", a=2)
        best = small[:, 64:80]
        ij = small[:, 80:112]
        picked = small[:, 112:144]
        hdot = small[:, 144:160]
        gexp = small[:, 160:176]
        gq = small[:, 176:192]
        ge = small[:, 192:208]
        wexp = small[:, 208:224]
        nbest = small[:, 224:225]
        gsum = small[:, 225:226]
        rsum = small[:, 226:227]
        iota = small[:, 240:256]

        bank_full = [sem(f"bank_full{b}") for b in range(8)]
        bank_read = [sem(f"bank_read{b}") for b in range(8)]
        w_loaded = [sem(f"w_loaded{i}") for i in range(R_SLOTS)]
        w_rounded = sem("w_rounded")
        w_split = sem("w_split")
        w_part = sem("w_part")
        act_rounded = sem("act_rounded")
        x_loaded = [sem(f"x_loaded{t}") for t in range(NT)]
        ident_loaded = sem("ident_loaded")
        const_loaded = sem("const_loaded")
        cols_loaded = sem("cols_loaded")
        gain_loaded = [sem(f"gain_loaded{i}") for i in range(2)]
        a_loaded = sem("a_loaded")
        subk_loaded = sem("subk_loaded")
        pool_loaded = sem("pool_loaded")
        u_loaded = [sem(f"u_loaded{i}") for i in range(RING)]
        v_loaded = [sem(f"v_loaded{i}") for i in range(RING)]
        stored = sem("stored")
        dve_step = sem("dve_step")
        dve_passed = sem("dve_passed")
        act_step = sem("act_step")
        eps_set = sem("eps_set")
        rms_ready = sem("rms_ready")
        norm_ready = sem("norm_ready")
        w_masked = sem("w_masked")
        bias_masked = sem("bias_masked")
        iota_ready = sem("iota_ready")
        v_squared = sem("v_squared")
        v_rms = sem("v_rms")
        v_normed = sem("v_normed")
        qk_squared = sem("qk_squared")
        qk_summed = sem("qk_summed")
        qk_rms = sem("qk_rms")
        row_max = sem("row_max")
        prob_ready = sem("prob_ready")
        unit_part = sem("unit_part")
        route_ready = sem("route_ready")
        idx_ready = sem("idx_ready")
        u_used = sem("u_used")
        v_used = sem("v_used")
        best_ready = sem("best_ready")
        gexp_ready = sem("gexp_ready")
        gq_ready = sem("gq_ready")
        ge_ready = sem("ge_ready")
        w_ready = sem("w_ready")
        diag_ready = sem("diag_ready")
        pool_passed = sem("pool_passed")
        x2_ready = sem("x2_ready")
        z_ln = sem("z_ln")
        l_ready = sem("l_ready")
        cumulated = sem("cumulated")
        att_in = sem("att_in")
        att_ready = sem("att_ready")
        xmax = sem("xmax")
        xexp = sem("xexp")
        xprob_ready = sem("xprob_ready")
        even_x = sem("even_x")
        merged_ready = sem("merged_ready")
        h_ready = sem("h_ready")
        silu_ready = sem("silu_ready")
        product_ready = sem("product_ready")
        product_rounded = sem("product_rounded")
        ffT_ready = sem("ffT_ready")

        def spread(ap, dims):
            return bass.AP(tensor=ap.tensor, offset=ap.offset, ap=[ap.ap[0]] + dims)

        def tok(t):
            return slice(t * P, (t + 1) * P)

        def half(n):
            return slice(n * HALF, (n + 1) * HALF)

        def four(ap):
            return ap.rearrange("p (c k) -> p c k", c=4)

        def two(ap):
            return ap.rearrange("p (c k) -> p c k", c=2)

        def wait_loaded(eng, name):
            b = BLOCK_AT[name]
            eng.wait_ge(w_loaded[b % R_SLOTS], 16 * (b // R_SLOTS + 1))
            return wraw[:, b % R_SLOTS, :]

        def wait_full(eng, *key):
            b, u = at(*key)
            eng.wait_ge(bank_full[b], u + 1)
            return bank[b]

        def wait_read(eng, *key):
            b, u = at(*key)
            eng.wait_ge(bank_read[b], u + 1)

        def read_of(*key):
            return bank_read[at(*key)[0]]

        def full_of(*key):
            return bank_full[at(*key)[0]]

        block = ctx.enter_context(nc.Block())

        @block.sync
        def _(sp):
            def load_block(name):
                b = BLOCK_AT[name]
                if b >= R_SLOTS:
                    freed = BLOCKS[b - R_SLOTS]
                    if freed in SPLIT_AT:
                        sp.wait_ge(w_split, SPLIT_AT[freed] + 1)
                    elif freed == "mem":
                        sp.wait_ge(norm_ready, 2 * NT)
                    else:
                        wait_full(sp, *RAW_USE[freed])
                sp.dma_start(wraw[:, b % R_SLOTS, :], io[name]).then_inc(w_loaded[b % R_SLOTS], 16)

            def load_blocks(first, last):
                for name in BLOCKS[BLOCK_AT[first]:BLOCK_AT[last] + 1]:
                    load_block(name)

            def load_gain(n, name):
                if n >= 2:
                    sp.wait_ge(norm_ready, NT * (n - 1))
                g = io[name]
                src = bass.AP(tensor=g.tensor, offset=g.offset, ap=[[0, P], [1, D]])
                sp.dma_start(gain[:, n % 2, :], src).then_inc(gain_loaded[n % 2], 16)

            for t in range(NT):
                sp.dma_start(x_sb[:, t, :], io["x"][tok(t), :]).then_inc(x_loaded[t], 16)
            sp.dma_start(ident, io["const"][:, 0:P]).then_inc(ident_loaded, 16)
            load_gain(0, "ln_mix_g")
            load_blocks("in1a", "in2b")
            sp.dma_start(const[:, P:4 * P + 768], io["const"][:, P:4 * P + 768]).then_inc(const_loaded, 16)
            sp.dma_start(cols[:, :], io["cols"]).then_inc(cols_loaded, 16)
            g = io["gmlp_norm_g"]
            sp.dma_start(gmlp_g[:, :], bass.AP(tensor=g.tensor, offset=g.offset, ap=[[0, P], [1, HALF]])).then_inc(a_loaded, 16)
            sp.dma_start(w_sT[:, :, :], io["w_sT"]).then_inc(a_loaded, 16)
            sp.dma_start(bias0[:, :, :], io["rel"][:, :, P:S]).then_inc(a_loaded, 16)
            sp.dma_start(bias1[:, :, :], io["rel"]).then_inc(a_loaded, 16)
            load_gain(1, "norm_mem_2")
            load_blocks("in3a", "in0b")
            load_gain(2, "ln_ffn_g")
            sp.dma_start(sub_kT[:, :, :], io["sub_kT"]).then_inc(subk_loaded, 16)
            load_blocks("out0a", "query2")
            load_gain(3, "norm_mix_pre_2")
            load_blocks("query3", "query6")
            load_gain(4, "norm_mix_post_2")
            load_blocks("query7", "in2_k1")
            wait_full(sp, "route", PEER_HEADS - 1)
            wait_full(sp, "mk")
            wait_full(sp, "mv")
            sp.dma_start(band[:, :, :], io["band"]).then_inc(pool_loaded, 16)
            sp.dma_start(w_mix[:, :, :], io["w_mix"]).then_inc(pool_loaded, 16)
            load_blocks("in2_va", "in2_g0a")
            load_gain(5, "norm_ffn_pre_2")
            load_blocks("in2_g0b", "ff_in5")
            load_gain(6, "norm_ffn_post_2")
            load_blocks("ff_in6", BLOCKS[-1])
            for t in range(NT):
                for n in range(2):
                    sp.wait_ge(h_ready, 2 * NT + 2 * t + n + 1)
                    sp.dma_start(out[tok(t), half(n)], x_sb[:, t, half(n)]).then_inc(stored, 16)
            sp.wait_ge(stored, 2 * 16 * NT)

        @block.gpsimd
        def _(pool):
            pool.iota(iota, [[1, TOPK]], base=0, channel_multiplier=0,
                      allow_small_or_imprecise_dtypes=True).then_inc(iota_ready, 1)
            with pool.Fori(0, NT * PEER_HEADS // 2) as i:
                for hh in range(2):
                    head = i * 2 + hh
                    pool.wait_ge(idx_ready, head + 1)
                    pool.sem_inc(pool_passed, 1)
                    for table, ring, used, loaded in (("peer_u", u_ring, u_used, u_loaded),
                                                      ("peer_v", v_ring, v_used, v_loaded)):
                        for k in range(TOPK):
                            pool.wait_ge(used, head * TOPK + k + 1)
                            pool.sem_inc(pool_passed, 1)
                            pool.indirect_dma_start(
                                out=ring[:, k % RING, :], out_offset=None, in_=io[table],
                                in_offset=bass.IndirectOffsetOnAxis(ap=eidx[:, hh, k:k + 1], axis=0),
                            ).then_inc(loaded[k % RING], 16)

        @block.scalar
        def _(act):
            steps = [0]
            split = [0]
            turned = [0]

            def written(ins):
                steps[0] += 1
                return ins.then_inc(act_step, 1)

            def all_written():
                act.wait_ge(act_step, steps[0])

            def square(src, n, t, row=0):
                if steps[0]:
                    all_written()
                written(nc.scalar.activation(junk[:, 0:src.shape[1]], src, ACT.Square,
                                             accum_out=stat[:, row, 2 * n + t:2 * n + t + 1]))

            def inverse_rms(n, first=0, tiles=NT, width=D):
                at_n = slice(2 * n + first, 2 * n + first + tiles)
                all_written()
                written(nc.scalar.activation(stat[:, 1, at_n], stat[:, 0, at_n], ACT.Ln,
                                             bias=eps[:, 0:1], scale=1.0 / width))
                all_written()
                return nc.scalar.activation(stat[:, 2, at_n], stat[:, 1, at_n], ACT.Exp, scale=-0.5)

            def inverse_rms_halves(n):
                all_written()
                for t in range(NT):
                    c = slice(2 * n + t, 2 * n + t + 1)
                    written(nc.scalar.activation(stat[:, 1, c], stat[:, 1, c], ACT.Ln, bias=stat[:, 0, c], scale=1.0 / D))
                all_written()
                at_n = slice(2 * n, 2 * n + NT)
                nc.scalar.activation(stat[:, 2, at_n], stat[:, 1, at_n], ACT.Exp, scale=-0.5).then_inc(rms_ready, NT)

            def split_to(name):
                while split[0] <= SPLIT_AT[name]:
                    s = split[0]
                    raw = wait_loaded(act, SPLIT[s])
                    if s >= S_SLOTS:
                        done = last_product(SPLIT[s - S_SLOTS])
                        if done:
                            wait_full(act, *done)
                        else:
                            act.wait_ge(w_part, PART_AT[SPLIT[s - S_SLOTS]])
                    nc.scalar.copy(w_hi[:, s % S_SLOTS, :], raw).then_inc(w_rounded, 1)
                    split[0] += 1

            def split_ahead(name, ahead=S_SLOTS):
                split_to(SPLIT[min(SPLIT_AT[name] + ahead, len(SPLIT) - 1)])

            def round_use(key, *copies):
                assert rounded[key] == turned[0], key
                turned[0] += 1
                wait_full(act, *key)
                for dst, src, scale in copies:
                    if scale is None:
                        ins = nc.scalar.copy(dst, src)
                    else:
                        ins = nc.scalar.activation(dst, src, ACT.Copy, scale=scale)
                ins.then_inc(act_rounded, 1)

            def round_tile(name, dst, t, h, scale=None):
                round_use((name, t, h), (dst[:, 4 * h:4 * h + 4, tok(t)], four(bank[at(name, t, h)[0]][:, :]), scale))

            def copy_half_T(name, dst, t, h):
                src = wait_full(act, name, t, h)
                nc.scalar.copy(dst[:, 4 * h:4 * h + 4, tok(t)], four(src[:, :])).then_inc(read_of(name, t, h), 1)

            act.wait_ge(eps_set, 1)
            split_to("in1a")
            for t in range(NT):
                for h in range(2):
                    round_tile("xT", aT_hi, t, h)
            split_to("in2a")
            for t in range(NT):
                act.wait_ge(x_loaded[t], 16)
                square(x_sb[:, t, :], 0, t)
            inverse_rms(0).then_inc(rms_ready, NT)
            act.wait_ge(rms_ready, NT)
            row_scale = [stat[:, 2, t:t + 1] for t in range(NT)]
            split_to("in2b")
            for t in range(NT):
                src = wait_full(act, "proj", 1, t)
                nc.scalar.activation(vg[:, t, :], src[:, :], ACT.Gelu_apprx_tanh,
                                     scale=row_scale[t]).then_inc(read_of("proj", 1, t), 1)
            for t in range(NT):
                wait_read(act, "proj", 1, t)
                square(vg[:, t, :], 7, t)
            split_to("in3a")
            for n in (2, 3):
                split_to(f"in{n + 1}b")
                for t in range(NT):
                    src = wait_full(act, "proj", n, t)
                    nc.scalar.activation(sq[:, 2 * (n - 2) + t, :], src[:, :], ACT.Square,
                                         scale=row_scale[t]).then_inc(qk_squared, 1)
                if n == 2:
                    split_to("in4a")
            sums, logs, inverses = (qk_stat[:, n, :, :].rearrange("p a b -> p (a b)") for n in range(3))
            all_written()
            written(nc.scalar.activation(stat[:, 1, 14:16], stat[:, 0, 14:16], ACT.Ln, bias=eps[:, 0:1], scale=1.0 / HALF))
            act.wait_ge(qk_summed, 4)
            written(nc.scalar.activation(logs, sums, ACT.Ln, bias=eps[:, 0:1], scale=1.0 / HD))
            all_written()
            nc.scalar.activation(inverses, logs, ACT.Exp, scale=-0.5).then_inc(qk_rms, 1)
            nc.scalar.activation(stat[:, 2, 14:16], stat[:, 1, 14:16], ACT.Exp, scale=-0.5).then_inc(v_rms, 1)
            split_to("in0b")
            for t in range(NT):
                src = wait_full(act, "proj", 4, t)
                nc.scalar.activation(v_sb[:, t, :], src[:, :], ACT.Copy,
                                     scale=row_scale[t]).then_inc(read_of("proj", 4, t), 1)
            split_to("out0a")

            def exps(u):
                act.wait_ge(row_max, u + 1)
                if u >= 3:
                    wait_full(act, "pT", u - 3)
                src = bank[at("score", u)[0]]
                heads = len(UNITS[u][1])
                w = HALF // heads
                for a in range(heads):
                    ins = nc.scalar.activation(prob[:, u % 3, a * w:(a + 1) * w], src[:, a * w:(a + 1) * w], ACT.Exp,
                                               bias=attn_stat[:, 1, u, a:a + 1], accum_out=attn_stat[:, 2, u, a:a + 1])
                ins.then_inc(read_of("score", u), 1)

            exps(0)
            exps(1)
            split_to("out0b")
            for t in range(NT):
                src = wait_full(act, "proj", 0, t)
                nc.scalar.activation(u_sb[:, t, :], src[:, :], ACT.Gelu_apprx_tanh,
                                     scale=row_scale[t]).then_inc(read_of("proj", 0, t), 1)
            for u in range(len(UNITS)):
                src = wait_full(act, "pT", u)
                if u >= 2:
                    if u - 2 in HEADS_DONE:
                        wait_full(act, "oT", HEADS_DONE.index(u - 2))
                    else:
                        act.wait_ge(unit_part, u - 1)
                nc.scalar.copy(probT[:, u % 2, :], src[:, :]).then_inc(read_of("pT", u), 1)
                if u + 2 < len(UNITS):
                    exps(u + 2)
                if u == 1:
                    split_to("out1a")
                if u == 4:
                    round_use(("oT", 0), (aT_hi[:, 4:6, :], two(bank[at("oT", 0)[0]][:, :]), None))
            for t in range(NT):
                round_use(("aT", t), (aT_hi[:, 0:4, tok(t)], four(bank[at("aT", t)[0]][:, :]), None))
            round_use(("oT", 1), (aT_hi[:, 6:8, :], two(bank[at("oT", 1)[0]][:, :]), None))
            split_to("out1b")
            mem = wait_loaded(act, "mem")
            for t in range(NT):
                square(mem[:, t * D:(t + 1) * D], 1, t)
            inverse_rms(1).then_inc(rms_ready, NT)
            for t in range(NT):
                for n in range(2):
                    wait_read(act, "w_out", n, t)
                square(x_sb[:, t, :], 2, t)
            for t in range(NT):
                copy_half_T("xbT", bT, t, 0)
            inverse_rms(2).then_inc(rms_ready, NT)
            act.wait_ge(rms_ready, 3 * NT)

            def router(j):
                src = wait_full(act, "query", j)
                if j >= 2:
                    wait_full(act, "route", j - 2)
                nc.scalar.copy(q2T[:, j % 2, :, :], two(src[:, :])).then_inc(read_of("query", j), 1)
                src = wait_full(act, "route", j)
                for t in range(NT):
                    ins = nc.scalar.activation(route[:, (t * PEER_HEADS + j) * S:(t * PEER_HEADS + j + 1) * S],
                                               src[:, t * S:(t + 1) * S], ACT.Copy, scale=stat[:, 2, 2 * NT + t:2 * NT + t + 1])
                    if t:
                        ins.then_inc(read_of("route", j), 1)
                    else:
                        ins.then_inc(route_ready, 2 if j == PEER_HEADS - 1 else 1)

            def beside(n):
                if n < PEER_HEADS - 4:
                    router(4 + n)
                if n == 4:
                    for t in range(NT):
                        for h in range(2):
                            copy_half_T("memT", bT, t, h)
                if n == 5:
                    src = wait_full(act, "mk")
                    nc.scalar.copy(mkT[:, :, :], two(src[:, :])).then_inc(read_of("mk"), 1)
                if n == 6:
                    src = wait_full(act, "mv")
                    nc.scalar.copy(mv[:, :, :], two(src[:, :])).then_inc(read_of("mv"), 1)

            for j in range(4):
                router(j)

            def weights(head):
                act.wait_ge(best_ready, head + 1)
                nc.scalar.activation(gexp, best, ACT.Exp, bias=nbest, accum_out=gsum).then_inc(gexp_ready, 1)
                act.wait_ge(gq_ready, head + 1)
                nc.scalar.activation(ge, gq, ACT.Tanh, scale=GELU_C).then_inc(ge_ready, 1)
                act.wait_ge(w_ready, head + 1)

            def diagonals(head, ks):
                for k in ks:
                    act.wait_ge(v_used, head * TOPK + k + 1)
                    nc.scalar.activation(diag[:, k % RING, :], ident, ACT.Copy,
                                         scale=wexp[:, k:k + 1]).then_inc(diag_ready, 1)

            for head in range(PEELED):
                weights(head)
                for n in range(2):
                    diagonals(head, range(n * RING, (n + 1) * RING))
                    beside(2 * head + n)

            def block_2_input(t):
                for n in range(2):
                    wait_read(act, "expert", t, n)
                square(x_sb[:, t, :], 3, t)
                inverse_rms(3, t, 1).then_inc(rms_ready, 1)

            def round_input(t):
                for h in range(2):
                    round_tile("nT", nT_hi, t, h)

            with act.Fori(0, (PEER_HEADS - PEELED) // 2) as i:
                for hh in range(2):
                    head = PEELED + i * 2 + hh
                    weights(head)
                    diagonals(head, range(TOPK))
            block_2_input(0)
            for head in (PEER_HEADS, PEER_HEADS + 1):
                weights(head)
                diagonals(head, range(TOPK))
                if head == PEER_HEADS:
                    round_input(0)
            with act.Fori(0, PEER_HEADS // 2 - 2) as i:
                for hh in range(2):
                    head = PEER_HEADS + 2 + i * 2 + hh
                    weights(head)
                    diagonals(head, range(TOPK))
            for head, rows in ((NT * PEER_HEADS - 2, range(TOPK)), (NT * PEER_HEADS - 1, PE_ROWS)):
                weights(head)
                diagonals(head, rows)
            split_to("in2_q0")
            block_2_input(1)
            split_to("in2_q1")
            round_input(1)

            split_to("in2_k0")
            split_to("in2_k1")
            split_to("in2_va")
            for c in range(2):
                src = wait_full(act, "k2", c)
                nc.scalar.copy(k3T[:, 2 * c:2 * c + 2, :], two(src[:, :])).then_inc(read_of("k2", c), 1)
                split_ahead(f"in2_k{c}")
            e_pair, att_pair = (b[:, :, :].rearrange("p a b -> p (a b)") for b in (sp_e, att))
            for i, name in enumerate(SLOT_BLOCKS):
                z, cum, attend = pair_at(i, Z_SLOT), pair_at(i, CUM_SLOT), pair_at(i, ATT_SLOT)
                if z is not None:
                    for a in range(2):
                        src = wait_full(act, "z", 2 * z + a)
                        if z:
                            act.wait_ge(l_ready, z)
                        written(nc.scalar.activation(sp_e[:, a, :], src[:, 0:384], ACT.Abs))
                    all_written()
                    written(nc.scalar.activation(e_pair, e_pair, ACT.Exp, scale=-1.0))
                if cum is not None:
                    act.wait_ge(att_in, cum + 1)
                    nc.scalar.activation(att_pair, att_pair, ACT.Exp).then_inc(att_ready, 1)
                if z is not None:
                    all_written()
                    nc.scalar.activation(e_pair, e_pair, ACT.Ln, bias=1.0).then_inc(z_ln, 1)
                if attend is not None:
                    round_use(("sbT", attend), (sbT_hi[:, attend, :], bank[at("sbT", attend)[0]][:, 0:S], None))
                if i in XS_SLOT:
                    t = XS_SLOT.index(i)
                    for j in range(2):
                        act.wait_ge(xmax, 2 * t + j + 1)
                        src = bank[at("xs", t, j)[0]]
                        for a in range(2):
                            n = 4 * t + 2 * j + a
                            ins = nc.scalar.activation(xprob[:, n, :], src[:, a * S:(a + 1) * S], ACT.Exp,
                                                       scale=HD ** -0.5, bias=xstat[:, 1, n:n + 1],
                                                       accum_out=xstat[:, 2, n:n + 1])
                            ins.then_inc(read_of("xs", t, j) if a else xexp, 1)
                if i in MIX_SLOT:
                    c = MIX_SLOT.index(i)
                    src = wait_full(act, "mix", c)
                    nc.scalar.copy(mixT[:, 2 * c:2 * c + 2, :], two(src[:, :])).then_inc(read_of("mix", c), 1)
                if i in POOL_SLOT:
                    c = POOL_SLOT.index(i)
                    src = bank[at("poolT", c)[0]]
                    act.wait_ge(cols_loaded, 16)
                    round_use(("poolT", c), *((poolT_hi[:, 2 * c + a, :], src[:, a * S:(a + 1) * S],
                                               cols[:, 10 + 2 * c + a:11 + 2 * c + a]) for a in range(2)))
                h = i - XPT_SLOT
                if 0 <= h < XHEADS:
                    src = wait_full(act, "xpT", h)
                    if h >= 2:
                        if h % 2 == 0:
                            act.wait_ge(even_x, h // 2)
                        else:
                            wait_full(act, "xoT", (h - 2) // 2)
                    nc.scalar.copy(xpT[:, h % 2, :], src[:, :]).then_inc(read_of("xpT", h), 1)
                h = i - XO_SLOT
                if 0 <= h < XHEADS and h % 2 == 1:
                    round_use(("xoT", h // 2), (xoT_hi[:, h // 2, :], bank[at("xoT", h // 2)[0]][:, 0:S], None))
                if name == "in2_x":
                    src = wait_full(act, "xq")
                    nc.scalar.copy(xqT[:, :, :], two(src[:, :])).then_inc(read_of("xq"), 1)
                elif name[-1] == "b":
                    for t in range(NT):
                        key = slot_key(name, t)
                        src = wait_full(act, *key)
                        if key[0] == "gate":
                            ins = nc.scalar.activation(gates[:, t, half(key[1])], src[:, :], ACT.Tanh, scale=0.5)
                        else:
                            ins = nc.scalar.copy((v3 if key[0] == "v2" else p_sb)[:, t, :], src[:, :])
                        ins.then_inc(read_of(*key), 1)
                split_ahead(name)
            split_to("out2_0b")
            for t in range(NT):
                for h in range(2):
                    round_tile("mergedT", nT_hi, t, h, scale=0.5)
            split_to("out2_1b")
            for n in range(2):
                for t in range(NT):
                    src = wait_full(act, "w_out2", n, t)
                    square(src[:, :], 4, t, row=n)
                if n == 0:
                    at_n = slice(8, 8 + NT)
                    all_written()
                    written(nc.scalar.activation(stat[:, 0, at_n], stat[:, 0, at_n], ACT.Identity,
                                                 bias=eps[:, 0:1], scale=1.0 / D))
            inverse_rms_halves(4)
            split_to("ff_in1")
            for t in range(NT):
                act.wait_ge(h_ready, 2 * t + 2)
                square(x_sb[:, t, :], 5, t)
            inverse_rms(5).then_inc(rms_ready, NT)
            for t in range(NT):
                for h in range(2):
                    round_tile("n2T", nT_hi, t, h)
            split_to("ff_in2")
            for j in range(FC + 1):
                if j < FC:
                    src = wait_full(act, "ff", j)
                    if j >= 2:
                        wait_read(act, "ff", j - 2)
                    nc.scalar.activation(silu[:, j % 2, :], src[:, 0:S], ACT.Silu).then_inc(silu_ready, 1)
                if j >= 1:
                    wait_read(act, "ff", j - 1)
                    nc.scalar.copy(hT_hi[:, j - 1, :], h32[:, (j - 1) % 2, :]).then_inc(product_rounded, 1)
                if j < FC:
                    split_ahead(f"ff_in{j}")
            split_to(BLOCKS[-1])
            for t in range(NT):
                for n in range(2):
                    src = wait_full(act, "ff_out", t, n)
                    square(src[:, :], 6, t, row=n)
                    if n == 0:
                        c = slice(12 + t, 13 + t)
                        all_written()
                        written(nc.scalar.activation(stat[:, 0, c], stat[:, 0, c], ACT.Identity,
                                                     bias=eps[:, 0:1], scale=1.0 / D))
            inverse_rms_halves(6)

        @block.vector
        def _(dve):
            steps = [0, 0]
            split = [0]

            def step(ins):
                steps[0] += 1
                ins.then_inc(dve_step, 1)
                dve.wait_ge(dve_step, steps[1] + steps[0])

            def step_apart(ins):
                step(ins)
                dve.sem_inc(dve_passed, 1)

            def norm(n, t, src, dst):
                dve.wait_ge(gain_loaded[n % 2], 16 * (n // 2 + 1))
                dve.wait_ge(rms_ready, NT * n + t + 1)
                nc.vector.scalar_tensor_tensor(out=dst, in0=src, scalar=stat[:, 2, 2 * n + t:2 * n + t + 1],
                                               in1=gain[:, n % 2, :], op0=ALU.mult, op1=ALU.mult).then_inc(norm_ready, 1)

            def gained(n, t, src, dst):
                dve.wait_ge(gain_loaded[n % 2], 16 * (n // 2 + 1))
                nc.vector.tensor_tensor(dst, src, gain[:, n % 2, :], ALU.mult).then_inc(norm_ready, 1)

            def copy_half_T(name, dst, t, h):
                src = wait_full(dve, name, t, h)
                nc.vector.tensor_copy(dst[:, 4 * h:4 * h + 4, tok(t)], four(src[:, :])).then_inc(read_of(name, t, h), 1)

            def split_to(name):
                while split[0] <= SPLIT_AT[name]:
                    s = split[0]
                    dve.wait_ge(w_rounded, s + 1)
                    nc.vector.tensor_tensor(w_lo[:, s % S_SLOTS, :], wraw[:, BLOCK_AT[SPLIT[s]] % R_SLOTS, :],
                                            w_hi[:, s % S_SLOTS, :].bitcast(F32), ALU.subtract).then_inc(w_split, 1)
                    split[0] += 1

            def split_ahead(name, ahead=S_SLOTS):
                split_to(SPLIT[min(SPLIT_AT[name] + ahead, len(SPLIT) - 1)])

            def rest(key, *parts):
                dve.wait_ge(act_rounded, rounded[key] + 1)
                for dst, src, hi, scale in parts:
                    if scale is None:
                        ins = nc.vector.tensor_tensor(dst, src, hi.bitcast(F32), ALU.subtract)
                    else:
                        ins = nc.vector.scalar_tensor_tensor(out=dst, in0=src, scalar=scale, in1=hi.bitcast(F32),
                                                             op0=ALU.mult, op1=ALU.subtract)
                ins.then_inc(read_of(*key), 1)

            def rest_tile(name, lo, hi, t, h, scale=None):
                where = (slice(None), slice(4 * h, 4 * h + 4), tok(t))
                rest((name, t, h), (lo[where], four(bank[at(name, t, h)[0]][:, :]), hi[where], scale))

            nc.vector.memset(eps[:, :], EPS).then_inc(eps_set, 1)
            nc.vector.memset(small[:, 227:228], 0.0).then_inc(u_used, RING)
            nc.vector.memset(small[:, 228:229], 0.0).then_inc(v_used, RING)
            for t in range(NT):
                dve.wait_ge(x_loaded[t], 16)
                gained(0, t, x_sb[:, t, :], xn[:, t, :])
            split_to("in1a")
            for t in range(NT):
                for h in range(2):
                    rest_tile("xT", aT_lo, aT_hi, t, h)
            split_to("in2a")
            dve.wait_ge(a_loaded, 64)
            nc.vector.memset(w_sT[CHUNK:P, :, 0:CHUNK], 0.0).then_inc(w_masked, 1)
            nc.vector.memset(bias0[0:CHUNK, :, CHUNK:P], NEG).then_inc(bias_masked, 1)
            nc.vector.memset(bias1[0:CHUNK, :, S - CHUNK:S], NEG).then_inc(bias_masked, 1)
            split_to("in3a")

            def head_sums(c):
                dve.wait_ge(qk_squared, c + 1)
                nc.vector.tensor_reduce(qk_stat[:, 0, c, :], sq[:, c, :].rearrange("p (h d) -> p h d", h=HEADS),
                                        AX_X, ALU.add).then_inc(qk_summed, 1)

            split_to("in3b")
            for t in range(NT):
                head_sums(t)
            split_to("in4b")
            for t in range(NT):
                head_sums(2 + t)
            dve.wait_ge(qk_rms, 1)
            for c in range(4):
                ins = nc.vector.tensor_scalar(qk_stat[:, 2, c, :], qk_stat[:, 2, c, :], stat[:, 2, c % NT:c % NT + 1], None,
                                              ALU.mult)
                if c == 3:
                    step(ins)
            for n, dst in ((0, q_sb), (1, k_sb)):
                for t in range(NT):
                    c = 2 * n + t
                    src = bank[at("proj", 2 + n, t)[0]]
                    nc.vector.tensor_tensor(dst[:, t, :].rearrange("p (h d) -> p h d", h=HEADS),
                                            src[:, :].rearrange("p (h d) -> p h d", h=HEADS),
                                            spread(qk_stat[:, 2, c, :], [[1, HEADS], [0, HD]]),
                                            ALU.mult).then_inc(read_of("proj", 2 + n, t), 1)
            dve.wait_ge(v_rms, 1)
            split_to("in0b")
            dve.wait_ge(cols_loaded, 16)
            for name, dst, col, scale in (("qT", qT, 0, HD ** -0.5), ("kT", kT, 1, 1.0)):
                for t in range(NT):
                    src = wait_full(dve, name, t)
                    nc.vector.tensor_scalar(dst[:, :, tok(t)], four(src[:, :]),
                                            cols[:, col:col + 1], scale, ALU.mult, ALU.mult).then_inc(read_of(name, t), 1)
            split_to("out0a")
            for t in range(NT):
                nc.vector.scalar_tensor_tensor(out=vg[:, t, :], in0=vg[:, t, :], scalar=stat[:, 2, 14 + t:15 + t],
                                               in1=gmlp_g[:, :], op0=ALU.mult, op1=ALU.mult).then_inc(v_normed, 1)

            def maxima(u):
                src = wait_full(dve, "score", u)
                heads = len(UNITS[u][1])
                step(nc.vector.tensor_reduce(attn_stat[:, 0, u, 0:heads], src[:, :].rearrange("p (a b) -> p a b", a=heads),
                                             AX_X, ALU.max))
                nc.vector.tensor_scalar(attn_stat[:, 1, u, 0:heads], attn_stat[:, 0, u, 0:heads], -1.0, None,
                                        ALU.mult).then_inc(row_max, 1)

            def normalise(u):
                wait_read(dve, "score", u)
                heads = len(UNITS[u][1])
                step(nc.vector.reciprocal(attn_stat[:, 3, u, 0:heads], attn_stat[:, 2, u, 0:heads]))
                p3d = prob[:, u % 3, :].rearrange("p (a b) -> p a b", a=heads)
                nc.vector.tensor_tensor(p3d, p3d, spread(attn_stat[:, 3, u, :], [[1, heads], [0, HALF // heads]]),
                                        ALU.mult).then_inc(prob_ready, 1)

            def spatial(t):
                src = wait_full(dve, "spatial", t)
                wait_read(dve, "proj", 0, t)
                v3d = vg[:, t, :].rearrange("p (g c) -> p g c", g=8)
                step(nc.vector.tensor_tensor(v3d, src[:, :].rearrange("p (g c) -> p g c", g=8),
                                             spread(cols[:, 2:10], [[1, 8], [0, GD]]), ALU.add))
                nc.vector.tensor_tensor(u_sb[:, t, :], u_sb[:, t, :], vg[:, t, :], ALU.mult).then_inc(read_of("spatial", t), 1)

            maxima(0)
            maxima(1)
            for u in range(len(UNITS)):
                normalise(u)
                if u + 2 < len(UNITS):
                    maxima(u + 2)
                if u < 2:
                    split_to(("out0b", "out1a")[u])
                if u in (2, 4):
                    spatial(u // 2 - 1)
            rest(("oT", 0), (aT_lo[:, 4:6, :], two(bank[at("oT", 0)[0]][:, :]), aT_hi[:, 4:6, :], None))
            for t in range(NT):
                rest(("aT", t), (aT_lo[:, 0:4, tok(t)], four(bank[at("aT", t)[0]][:, :]), aT_hi[:, 0:4, tok(t)], None))
            rest(("oT", 1), (aT_lo[:, 6:8, :], two(bank[at("oT", 1)[0]][:, :]), aT_hi[:, 6:8, :], None))
            split_to("out1b")
            mem = wait_loaded(dve, "mem")
            for t in range(NT):
                norm(1, t, mem[:, t * D:(t + 1) * D], mem_n[:, t, :])
            for n in range(2):
                for t in range(NT):
                    src = wait_full(dve, "w_out", n, t)
                    nc.vector.tensor_tensor(x_sb[:, t, half(n)], x_sb[:, t, half(n)], src[:, :],
                                            ALU.add).then_inc(read_of("w_out", n, t), 1)
            for t in range(NT):
                for n in range(2):
                    wait_read(dve, "w_out", n, t)
                gained(2, t, x_sb[:, t, :], xn[:, t, :])
            for t in range(NT):
                copy_half_T("xbT", bT, t, 1)
            dve.wait_ge(rms_ready, 3 * NT)
            for t in range(NT):
                for h in range(2):
                    wait_full(dve, "xbT", t, h)
                step(nc.vector.tensor_scalar(xn[:, t, :], xn[:, t, :], stat[:, 2, 2 * NT + t:2 * NT + t + 1], None, ALU.mult))

            def sixteen(values, spare, out, where):
                step_apart(nc.vector.max(out[:, 0:8], values))
                nc.vector.max_index(where[:, 0:8], out[:, 0:8], values)
                step_apart(nc.vector.match_replace(spare, out[:, 0:8], values, -3.0e38))
                step_apart(nc.vector.max(out[:, 8:16], spare))
                return nc.vector.max_index(where[:, 8:16], out[:, 8:16], spare)

            def choose(head, hh):
                step_apart(nc.vector.tensor_copy(head_sc[:, :, :].rearrange("p a b -> p (a b)"),
                                                 route[:, bass.ds(head * 2 * NKEYS, 2 * NKEYS)]))
                for p in range(2):
                    step_apart(sixteen(head_sc[:, p, :], head_sc2[:, p, :], top[:, p, :], rank[:, p, :]))
                nc.vector.tensor_copy(topi, rank[:, 0:2, :])
                step_apart(nc.vector.tensor_tensor(cand[:, :].rearrange("p (a b) -> p a b", a=TOPK),
                                                   spread(top[:, 0, :], [[1, TOPK], [0, TOPK]]),
                                                   spread(top[:, 1, :], [[0, TOPK], [1, TOPK]]), ALU.add))
                step(sixteen(cand[:, :], cand2[:, :], best, rank[:, 2, :]))
                nc.vector.tensor_scalar(nbest, best[:, 0:1], -1.0, None, ALU.mult).then_inc(best_ready, 1)
                step(nc.vector.tensor_scalar(rank[:, 3, :], rank[:, 2, :], 4, None, ALU.logical_shift_right))
                step(nc.vector.tensor_scalar(rank[:, 2, :], rank[:, 2, :], 15, None, ALU.bitwise_and))
                nc.vector.tensor_copy(ij[:, 0:TOPK], rank[:, 3, :])
                step(nc.vector.tensor_copy(ij[:, TOPK:2 * TOPK], rank[:, 2, :]))
                step(nc.vector.tensor_tensor(onehot[:, :, :, :].rearrange("p a b c -> p (a b) c"),
                                             spread(ij, [[1, 2 * TOPK], [0, TOPK]]),
                                             spread(iota, [[0, 2 * TOPK], [1, TOPK]]), ALU.is_equal))
                step(nc.vector.tensor_tensor(onehot[:, :, :, :], onehot[:, :, :, :],
                                             spread(topi, [[TOPK, 2], [0, TOPK], [1, TOPK]]), ALU.mult))
                step(nc.vector.tensor_reduce(picked, onehot[:, :, :, :].rearrange("p a b c -> p (a b) c"),
                                             AX_X, ALU.add))
                nc.vector.scalar_tensor_tensor(out=eidx[:, hh, :], in0=picked[:, 0:TOPK], scalar=float(NKEYS),
                                               in1=picked[:, TOPK:2 * TOPK], op0=ALU.mult,
                                               op1=ALU.add).then_inc(idx_ready, 1)

            def weigh(head, t):
                for k in range(TOPK):
                    dve.wait_ge(u_loaded[k % RING], head * 32 + 16 * (k // RING) + 16)
                    nc.vector.scalar_tensor_tensor(out=u_ring[:, k % RING, :], in0=u_ring[:, k % RING, :], scalar=1.0,
                                                   in1=xn[:, t, :], op0=ALU.mult, op1=ALU.mult,
                                                   accum_out=hdot[:, k:k + 1]).then_inc(u_used, 1)
                dve.wait_ge(u_used, head * TOPK + TOPK + RING)
                step(nc.vector.tensor_tensor(gq, hdot, hdot, ALU.mult))
                step(nc.vector.tensor_scalar(gq, gq, GELU_A, 1.0, ALU.mult, ALU.add))
                nc.vector.tensor_tensor(gq, gq, hdot, ALU.mult).then_inc(gq_ready, 1)
                dve.wait_ge(gexp_ready, head + 1)
                step(nc.vector.reciprocal(rsum, gsum))
                step(nc.vector.scalar_tensor_tensor(out=wexp, in0=hdot, scalar=rsum, in1=gexp,
                                                    op0=ALU.mult, op1=ALU.mult))
                dve.wait_ge(ge_ready, head + 1)
                step(nc.vector.tensor_scalar(ge, ge, 1.0, 0.5, ALU.add, ALU.mult))
                nc.vector.tensor_tensor(wexp, wexp, ge, ALU.mult).then_inc(w_ready, 1)

            def add_experts(t):
                for n in range(2):
                    src = wait_full(dve, "expert", t, n)
                    nc.vector.tensor_tensor(x_sb[:, t, half(n)], x_sb[:, t, half(n)], src[:, :],
                                            ALU.add).then_inc(read_of("expert", t, n), 1)

            def rest_input(t):
                for h in range(2):
                    rest_tile("nT", nT_lo, nT_hi, t, h)

            def weigh_and_choose(first, turns, t):
                before = steps[0]
                with dve.Fori(0, turns) as i:
                    steps[1] = i * LOOP_STEPS
                    for hh in range(2):
                        head = first + i * 2 + hh
                        weigh(head, t)
                        if t == 0:
                            dve.wait_ge(route_ready, head + 2)
                            dve.sem_inc(dve_passed, 1)
                        choose(head + 1, (hh + 1) % 2)
                    assert steps[0] - before == LOOP_STEPS, steps[0] - before
                steps[0] += LOOP_STEPS * (turns - 1)
                steps[1] = 0

            dve.wait_ge(iota_ready, 1)
            dve.wait_ge(route_ready, 1)
            choose(0, 0)
            weigh_and_choose(0, PEER_HEADS // 2, 0)
            add_experts(0)
            for j in range(PEER_HEADS):
                wait_read(dve, "route", j)
            weigh(PEER_HEADS, 1)
            norm(3, 0, x_sb[:, 0, :], xn[:, 0, :])
            choose(PEER_HEADS + 1, 1)
            weigh(PEER_HEADS + 1, 1)
            choose(PEER_HEADS + 2, 0)
            rest_input(0)
            weigh_and_choose(PEER_HEADS + 2, PEER_HEADS // 2 - 2, 1)
            last = NT * PEER_HEADS - 1
            weigh(last - 1, 1)
            choose(last, 1)
            weigh(last, 1)
            dve.wait_ge(w_ready, last + 1)
            for k in DVE_ROWS:
                dve.wait_ge(v_loaded[k % RING], last * 32 + 16 * (k // RING) + 16)
                step(nc.vector.scalar_tensor_tensor(out=x_sb[:, 1, :], in0=v_ring[:, k % RING, :], scalar=wexp[:, k:k + 1],
                                                    in1=x_sb[:, 1, :], op0=ALU.mult, op1=ALU.add))
            add_experts(1)
            split_to("in2_q0")
            norm(3, 1, x_sb[:, 1, :], xn[:, 1, :])
            split_to("in2_q1")
            rest_input(1)

            split_to("in2_k0")
            dve.wait_ge(const_loaded, 16)
            for c in range(2):
                src = wait_full(dve, "q2", c)
                nc.vector.tensor_scalar(q3T[:, 2 * c:2 * c + 2, :], two(src[:, :]),
                                        HD ** -0.5, None, ALU.mult).then_inc(read_of("q2", c), 1)
                split_ahead(f"in2_q{c}")
            for c in range(2):
                split_ahead(f"in2_k{c}")

            def z_softplus(p):
                dve.wait_ge(z_ln, p + 1)
                for a in range(2):
                    src = bank[at("z", 2 * p + a)[0]]
                    ins = nc.vector.scalar_tensor_tensor(out=sp_e[:, a, :], in0=src[:, 0:384], scalar=0.0,
                                                         in1=sp_e[:, a, :], op0=ALU.max, op1=ALU.add)
                    if a:
                        step(ins)
                nc.vector.tensor_tensor(sp_l[:, :, :], sp_e[:, :, :], spread(mask01, [[0, 2], [1, 384]]),
                                        ALU.mult).then_inc(l_ready, 1)

            def z_weight(p):
                dve.wait_ge(cumulated, p + 1)
                for a in range(2):
                    src = bank[at("z", 2 * p + a)[0]]
                    nc.vector.tensor_scalar(att[:, a, :], src[:, 0:384], 0.0, None,
                                            ALU.min).then_inc(read_of("z", 2 * p + a), 1)
                for a in range(2):
                    wait_read(dve, "z", 2 * p + a)
                nc.vector.tensor_tensor(att[:, :, :], att[:, :, :], spread(maskneg, [[0, 2], [1, 384]]),
                                        ALU.add).then_inc(att_in, 1)

            for i, name in enumerate(SLOT_BLOCKS):
                z, cum, attend = pair_at(i, Z_SLOT), pair_at(i, CUM_SLOT), pair_at(i, ATT_SLOT)
                if cum is not None:
                    z_weight(cum)
                if z is not None:
                    z_softplus(z)
                if attend is not None:
                    rest(("sbT", attend), (sbT_lo[:, attend, :], bank[at("sbT", attend)[0]][:, 0:S], sbT_hi[:, attend, :], None))
                if i in XS_SLOT:
                    t = XS_SLOT.index(i)
                    for j in range(2):
                        n = 4 * t + 2 * j
                        src = wait_full(dve, "xs", t, j)
                        step(nc.vector.tensor_reduce(xstat[:, 0, n:n + 2], two(src[:, :]), AX_X, ALU.max))
                        nc.vector.tensor_scalar(xstat[:, 1, n:n + 2], xstat[:, 0, n:n + 2], -HD ** -0.5, None,
                                                ALU.mult).then_inc(xmax, 1)
                if i - 1 in XS_SLOT:
                    t = XS_SLOT.index(i - 1)
                    n = 4 * t
                    for j in range(2):
                        wait_read(dve, "xs", t, j)
                    step(nc.vector.reciprocal(xstat[:, 3, n:n + 4], xstat[:, 2, n:n + 4]))
                    nc.vector.tensor_tensor(xprob[:, n:n + 4, :], xprob[:, n:n + 4, :],
                                            spread(xstat[:, 3, n:n + 4], [[1, 4], [0, S]]), ALU.mult).then_inc(xprob_ready, 1)
                if i in POOL_SLOT:
                    c = POOL_SLOT.index(i)
                    src = bank[at("poolT", c)[0]]
                    rest(("poolT", c), *((poolT_lo[:, 2 * c + a, :], src[:, a * S:(a + 1) * S], poolT_hi[:, 2 * c + a, :],
                                          cols[:, 10 + 2 * c + a:11 + 2 * c + a]) for a in range(2)))
                h = i - XO_SLOT
                if 0 <= h < XHEADS and h % 2 == 1:
                    c = h // 2
                    rest(("xoT", c), (xoT_lo[:, c, :], bank[at("xoT", c)[0]][:, 0:S], xoT_hi[:, c, :], None))
                split_ahead(name)
            def gated(key, b, t, n, dst):
                wait_read(dve, "gate", 2 * b + n, t)
                src = wait_full(dve, key, t, n)
                return nc.vector.scalar_tensor_tensor(out=dst, in0=gates[:, t, half(2 * b + n)], scalar=1.0, in1=src[:, :],
                                                      op0=ALU.add, op1=ALU.mult).then_inc(read_of(key, t, n), 1)

            def add_gated(key, b, t, n):
                gated(key, b, t, n, tmp[:, :])
                wait_read(dve, key, t, n)
                return nc.vector.tensor_tensor(xn[:, t, half(n)], xn[:, t, half(n)], tmp[:, :], ALU.add)

            split_ahead("x_o")
            for t in range(NT):
                for n in range(2):
                    gated("y_x", 2, t, n, xn[:, t, half(n)])
            split_ahead("pool_o0")
            for t in range(NT):
                for n in range(2):
                    wait_read(dve, "y_x", t, n)
                    step(add_gated("y_pool", 0, t, n))
            split_ahead("pool_o1")
            for t in range(NT):
                for n in range(2):
                    add_gated("y_sb", 1, t, n).then_inc(merged_ready, 1)
                    dve.wait_ge(merged_ready, 2 * t + n + 1)
            for t in range(NT):
                for h in range(2):
                    rest_tile("mergedT", nT_lo, nT_hi, t, h, scale=0.5)
            split_to("out2_1b")

            def add_normed(n, key, slot):
                dve.wait_ge(gain_loaded[n % 2], 16 * (n // 2 + 1))
                dve.wait_ge(rms_ready, NT * (n + 1))
                for t in range(NT):
                    for m in range(2):
                        src = bank[at(*key(t, m))[0]]
                        dst = z_sb[:, t, half(m)]
                        nc.vector.scalar_tensor_tensor(out=dst, in0=src[:, :], scalar=stat[:, 2, 2 * n + t:2 * n + t + 1],
                                                       in1=gain[:, n % 2, half(m)], op0=ALU.mult,
                                                       op1=ALU.mult).then_inc(read_of(*key(t, m)), 1)
                        wait_read(dve, *key(t, m))
                        nc.vector.tensor_tensor(x_sb[:, t, half(m)], x_sb[:, t, half(m)], dst, ALU.add).then_inc(h_ready, 1)

            add_normed(4, lambda t, m: ("w_out2", m, t), 0)
            nc.vector.memset(small[:, 229:230], 0.0).then_inc(norm_ready, NT)
            split_to("ff_in1")
            for t in range(NT):
                norm(5, t, x_sb[:, t, :], xn[:, t, :])
            for t in range(NT):
                for h in range(2):
                    rest_tile("n2T", nT_lo, nT_hi, t, h)
            split_to("ff_in2")
            for j in range(FC + 1):
                if j < FC:
                    dve.wait_ge(silu_ready, j + 1)
                    if j >= 2:
                        dve.wait_ge(ffT_ready, j - 1)
                    src = bank[at("ff", j)[0]]
                    nc.vector.tensor_tensor(h32[:, j % 2, :], silu[:, j % 2, :], src[:, S:2 * S],
                                            ALU.mult).then_inc(read_of("ff", j), 1)
                if j >= 1:
                    dve.wait_ge(product_rounded, j)
                    nc.vector.tensor_tensor(hT_lo[:, j - 1, :], h32[:, (j - 1) % 2, :], hT_hi[:, j - 1, :].bitcast(F32),
                                            ALU.subtract).then_inc(ffT_ready, 1)
                if j < FC:
                    split_ahead(f"ff_in{j}")
            split_to(BLOCKS[-1])
            add_normed(6, lambda t, m: ("ff_out", t, m), 0)

        @block.tensor
        def _(pe):
            def open_bank(*key):
                b, u = at(*key)
                if u:
                    pe.wait_ge(bank_read[b], u)
                return bank[b]

            def transposes(src, *key):
                dst = open_bank(*key)
                for c in range(src.shape[1] // P):
                    mm = nc.tensor.transpose(dst[:, c * P:(c + 1) * P], src[:, c * P:(c + 1) * P], ident)
                mm.then_inc(full_of(*key), 1)

            def tile_T(n, name, src, t):
                pe.wait_ge(norm_ready, NT * n + t + 1)
                for h in range(2):
                    transposes(src[:, t, half(h)], name, t, h)

            def T_ready(name):
                for t in range(NT):
                    for h in range(2):
                        wait_read(pe, name, t, h)

            def split_block(name):
                s = SPLIT_AT[name]
                pe.wait_ge(w_split, s + 1)
                return w_hi[:, s % S_SLOTS, :], w_lo[:, s % S_SLOTS, :]

            def product(dst, a, b, start, stop):
                (a_hi, a_lo), (b_hi, b_lo) = a, b
                nc.tensor.matmul(dst, a_hi, b_hi, start=start, stop=False)
                nc.tensor.matmul(dst, a_hi, b_lo, start=False, stop=False)
                return nc.tensor.matmul(dst, a_lo, b_hi, start=False, stop=stop)

            def parts(pair, *index):
                return tuple(p[index] for p in pair)

            ALL = slice(None)

            def tokens_out(name, aT, key):
                w = split_block(name)
                first = name[-1] == "a"
                for t in range(NT):
                    dst = open_bank(*key(t)) if first else bank[at(*key(t))[0]]
                    for c in range(KC // 2):
                        mm = product(dst[:, :], parts(aT, ALL, c + (0 if first else KC // 2), tok(t)),
                                     parts(w, ALL, half(c)), start=first and c == 0, stop=not first and c == KC // 2 - 1)
                    if not first:
                        mm.then_inc(full_of(*key(t)), 1)
                if first:
                    mm.then_inc(w_part, 1)

            def rows_out(name, aT, first, last, chunk, key):
                w = split_block(name)
                for t in range(NT):
                    for n in range(2):
                        dst = open_bank(*key(t, n)) if first else bank[at(*key(t, n))[0]]
                        for c in range(2):
                            mm = product(dst[:, :], parts(aT, ALL, chunk + c, tok(t)),
                                         parts(w, ALL, slice(c * D + n * HALF, c * D + (n + 1) * HALF)),
                                         start=first and c == 0, stop=last and c == 1)
                        if last:
                            mm.then_inc(full_of(*key(t, n)), 1)
                if not last:
                    mm.then_inc(w_part, 1)

            def channels_out(name, aT, *key):
                w = split_block(name)
                dst = open_bank(*key)
                for a in range(2):
                    for c in range(KC):
                        mm = product(dst[:, a * S:(a + 1) * S], parts(w, ALL, slice(c * S + a * P, c * S + (a + 1) * P)),
                                     parts(aT, ALL, c, ALL), start=(c == 0), stop=(c == KC - 1))
                mm.then_inc(full_of(*key), 1)

            def plain_channels_out(w, aT, *key):
                dst = open_bank(*key)
                for a in range(2):
                    for c in range(KC):
                        mm = nc.tensor.matmul(dst[:, a * S:(a + 1) * S], w[:, c * S + a * P:c * S + (a + 1) * P],
                                              aT[:, c, :], start=(c == 0), stop=(c == KC - 1))
                mm.then_inc(full_of(*key), 1)

            aT = aT_hi, aT_lo
            nT = nT_hi, nT_lo

            pe.wait_ge(ident_loaded, 16)
            for t in range(NT):
                tile_T(0, "xT", xn, t)
            T_ready("xT")
            for n in (1, 2, 3, 4):
                for p in "ab":
                    tokens_out(f"in{n}{p}", aT, lambda t, n=n: ("proj", n, t))
            for name, n, src in (("qT", 2, q_sb), ("kT", 3, k_sb)):
                for t in range(NT):
                    wait_read(pe, "proj", n, t)
                    transposes(src[:, t, :], name, t)

            def scores(u):
                dst = open_bank("score", u)
                t, heads = UNITS[u]
                w = HALF // len(heads)
                first = BIAS_HEADS.index(heads[0])
                bias = (bias1 if t else bias0)[:, first:first + len(heads), :].rearrange("p h s -> p (h s)")
                nc.tensor.matmul(dst[:, :], ident, bias, start=True, stop=False)
                for a, h in enumerate(heads):
                    r, c = slice(HD * (h % 2), HD * (h % 2) + HD), h // 2
                    mm = nc.tensor.matmul(dst[:, a * w:(a + 1) * w], qT[r, c, tok(t)], kT[r, c, 0:w], start=False,
                                          stop=(a == len(heads) - 1))
                mm.then_inc(full_of("score", u), 1)

            pe.wait_ge(bias_masked, 2)
            for name in ("qT", "kT"):
                for t in range(NT):
                    wait_read(pe, name, t)
            scores(0)
            scores(1)
            for p in "ab":
                tokens_out(f"in0{p}", aT, lambda t: ("proj", 0, t))
            for t in range(NT):
                wait_read(pe, "proj", 4, t)
            pe.wait_ge(w_masked, 1)
            for u in range(len(UNITS)):
                t, heads = UNITS[u]
                if u + 2 < len(UNITS):
                    scores(u + 2)
                pe.wait_ge(prob_ready, u + 1)
                transposes(prob[:, u % 3, :], "pT", u)
                if u == 0:
                    both_oT = [open_bank("oT", c) for c in range(2)]
                if u in (1, 3):
                    m = u // 2
                    pe.wait_ge(v_normed, m + 1)
                    dst = open_bank("spatial", m)
                    for g in range(8):
                        mm = nc.tensor.matmul(dst[:, g * GD:(g + 1) * GD], w_sT[:, g, :], vg[:, m, g * GD:(g + 1) * GD],
                                              start=True, stop=True)
                    mm.then_inc(full_of("spatial", m), 1)
                wait_read(pe, "pT", u)
                for a, h in enumerate(heads):
                    r, off = slice(HD * (h % 2), HD * (h % 2) + HD), S * (h // 2 % 2) + t * P
                    for kt in range(t + 1):
                        piece = a * (t + 1) + kt
                        mm = nc.tensor.matmul(both_oT[h // 4][r, off:off + P], v_sb[:, kt, h * HD:(h + 1) * HD],
                                              probT[:, u % 2, piece * P:(piece + 1) * P], start=(kt == 0), stop=(kt == t))
                mm.then_inc(full_of("oT", HEADS_DONE.index(u)) if u in HEADS_DONE else unit_part, 1)
                if u in (4, 5):
                    m = u - 4
                    wait_read(pe, "spatial", m)
                    transposes(u_sb[:, m, :], "aT", m)
            for c in range(2):
                wait_read(pe, "oT", c)
                wait_read(pe, "aT", c)
            for n in range(2):
                for p in "ab":
                    tokens_out(f"out{n}{p}", aT, lambda t, n=n: ("w_out", n, t))
            for t in range(NT):
                tile_T(2, "xbT", xn, t)
            T_ready("xbT")
            pe.wait_ge(subk_loaded, 16)

            def router(j):
                plain_channels_out(wait_loaded(pe, f"query{j}"), bT, "query", j)
                dst = open_bank("route", j)
                wait_read(pe, "query", j)
                for t in range(NT):
                    for p in range(2):
                        o = t * S + p * NKEYS
                        mm = nc.tensor.matmul(dst[:, o:o + NKEYS], q2T[:, j % 2, p, tok(t)], sub_kT[:, 2 * j + p, :],
                                              start=True, stop=True)
                mm.then_inc(full_of("route", j), 1)

            def beside(n):
                if n < PEER_HEADS - 4:
                    router(4 + n)
                if n == 4:
                    for t in range(NT):
                        tile_T(1, "memT", mem_n, t)
                if n == 5:
                    T_ready("memT")
                    plain_channels_out(wait_loaded(pe, "mem_k"), bT, "mk")
                if n == 6:
                    w = wait_loaded(pe, "mem_v")
                    dst = open_bank("mv")
                    for t in range(NT):
                        for c in range(KC):
                            mm = nc.tensor.matmul(dst[:, t * S:(t + 1) * S], bT[:, c, tok(t)], w[:, c * S:(c + 1) * S],
                                                  start=(c == 0), stop=(c == KC - 1))
                    mm.then_inc(full_of("mv"), 1)

            for j in range(4):
                router(j)

            def add_rows(acc, t, head, ks, start=False, stop=False):
                for n_row, k in enumerate(ks):
                    pe.wait_ge(v_loaded[k % RING], head * 32 + 16 * (k // RING) + 16)
                    pe.wait_ge(diag_ready, head * TOPK + (n_row if stop else k) + 1)
                    ends = stop and k == ks[-1]
                    for n in range(2):
                        mm = nc.tensor.matmul(acc[n][:, :], diag[:, k % RING, :], v_ring[:, k % RING, half(n)],
                                              start=start and n_row == 0, stop=ends)
                        if ends:
                            mm.then_inc(full_of("expert", t, n), 1)
                    if not ends:
                        mm.then_inc(v_used, 1)

            acc = [open_bank("expert", 0, n) for n in range(2)]
            for head in range(PEELED):
                for n in range(2):
                    add_rows(acc, 0, head, range(n * RING, (n + 1) * RING), start=(head == 0 and n == 0))
                    beside(2 * head + n)
            with pe.Fori(0, (PEER_HEADS - PEELED) // 2) as i:
                for hh in range(2):
                    add_rows(acc, 0, PEELED + i * 2 + hh, range(TOPK))
            pe.wait_ge(const_loaded, 16)
            for n in range(2):
                nc.tensor.matmul(acc[n][:, :], zeros, const[:, 0:HALF], start=False,
                                 stop=True).then_inc(full_of("expert", 0, n), 1)
            acc = [open_bank("expert", 1, n) for n in range(2)]
            add_rows(acc, 1, PEER_HEADS, range(TOPK), start=True)
            tile_T(3, "nT", xn, 0)
            add_rows(acc, 1, PEER_HEADS + 1, range(TOPK))
            with pe.Fori(0, PEER_HEADS // 2 - 2) as i:
                for hh in range(2):
                    add_rows(acc, 1, PEER_HEADS + 2 + i * 2 + hh, range(TOPK))
            last = NT * PEER_HEADS - 1
            add_rows(acc, 1, last - 1, range(TOPK))
            add_rows(acc, 1, last, PE_ROWS, stop=True)
            tile_T(3, "nT", xn, 1)

            T_ready("nT")
            for key in ("q2", "k2"):
                for c in range(2):
                    channels_out(f"in2_{key[0]}{c}", nT, key, c)
            for key in ("q2", "k2"):
                for c in range(2):
                    wait_read(pe, key, c)
            for i, name in enumerate(SLOT_BLOCKS):
                z, cum, attend = pair_at(i, Z_SLOT), pair_at(i, CUM_SLOT), pair_at(i, ATT_SLOT)
                if attend is not None:
                    dst = open_bank("sbT", attend)
                    if attend == 0:
                        for t in range(NT):
                            wait_read(pe, "v2", t)
                    pe.wait_ge(att_ready, attend + 1)
                    for a in range(2):
                        g, r = 2 * attend + a, slice(HD * a, HD * a + HD)
                        nc.tensor.matmul(dst[r, 0:S], v3[:, 0, g * HD:(g + 1) * HD], att[:, a, 0:S], start=True, stop=False)
                        mm = nc.tensor.matmul(dst[r, P:S], v3[:, 1, g * HD:(g + 1) * HD], att[:, a, S:384],
                                              start=False, stop=True)
                    mm.then_inc(full_of("sbT", attend), 1)
                if cum is not None:
                    pe.wait_ge(l_ready, cum + 1)
                    for a in range(2):
                        dst = bank[at("z", 2 * cum + a)[0]]
                        nc.tensor.matmul(dst[:, 0:S], negtri, sp_l[:, a, 0:S], start=False, stop=False,
                                         skip_group_check=True)
                        nc.tensor.matmul(dst[:, P:S], negones, sp_l[:, a, S:384], start=False, stop=False,
                                         skip_group_check=True)
                        mm = nc.tensor.matmul(dst[:, S:384], negtri, sp_l[:, a, S:384], start=False, stop=True,
                                              skip_group_check=True)
                    mm.then_inc(cumulated, 1)
                if z is not None:
                    for a in range(2):
                        dst = open_bank("z", 2 * z + a)
                        r = slice(HD * a, HD * a + HD)
                        nc.tensor.matmul(dst[:, 0:S], k3T[r, z, 0:P], q3T[r, z, 0:S], start=True, stop=False)
                        nc.tensor.matmul(dst[:, S:384], k3T[r, z, P:S], q3T[r, z, P:S], start=False,
                                         stop=True).then_inc(full_of("z", 2 * z + a), 1)
                if i in XS_SLOT:
                    t = XS_SLOT.index(i)
                    wait_read(pe, "xq")
                    wait_read(pe, "mk")
                    for j in range(2):
                        dst = open_bank("xs", t, j)
                        r = slice(HD * j, HD * j + HD)
                        for a in range(2):
                            mm = nc.tensor.matmul(dst[:, a * S:(a + 1) * S], xqT[r, a, tok(t)], mkT[r, a, :],
                                                  start=True, stop=True)
                        mm.then_inc(full_of("xs", t, j), 1)
                if i in MIX_SLOT:
                    c = MIX_SLOT.index(i)
                    pe.wait_ge(pool_loaded, 32)
                    for t in range(NT):
                        wait_read(pe, "pool_in", t)
                    dst = open_bank("mix", c)
                    for a in range(2):
                        g = 2 * c + a
                        nc.tensor.matmul(dst[:, a * S:(a + 1) * S], p_sb[:, 0, g * P:(g + 1) * P], band[:, g, 0:S],
                                         start=True, stop=False)
                        mm = nc.tensor.matmul(dst[:, a * S + P:(a + 1) * S], p_sb[:, 1, g * P:(g + 1) * P],
                                              band[:, g, S:384], start=False, stop=True)
                    mm.then_inc(full_of("mix", c), 1)
                if i in POOL_SLOT:
                    c = POOL_SLOT.index(i)
                    dst = open_bank("poolT", c)
                    wait_read(pe, "mix", c)
                    for a in range(2):
                        g = 2 * c + a
                        mm = nc.tensor.matmul(dst[:, a * S:(a + 1) * S], w_mix[:, g, :], mixT[:, g, :],
                                              start=True, stop=True)
                    mm.then_inc(full_of("poolT", c), 1)
                h = i - XO_SLOT
                if 0 <= h < XHEADS:
                    c, a = h // 2, h % 2
                    dst_x = bank[at("xoT", c)[0]] if a else open_bank("xoT", c)
                    wait_read(pe, "xpT", h)
                    wait_read(pe, "mv")
                    for m in range(2):
                        mm = nc.tensor.matmul(dst_x[HD * a:HD * a + HD, 0:S], mv[:, m, h * HD:(h + 1) * HD],
                                              xpT[:, h % 2, m * S:(m + 1) * S], start=(m == 0), stop=(m == 1))
                    mm.then_inc(full_of("xoT", c) if a else even_x, 1)
                h = i - XPT_SLOT
                if 0 <= h < XHEADS:
                    if h == 0:
                        pe.wait_ge(xprob_ready, NT)
                    dst = open_bank("xpT", h)
                    for c in range(2):
                        for t in range(NT):
                            src = xprob[:, 4 * t + 2 * (h % 2) + h // 2, c * P:(c + 1) * P]
                            mm = nc.tensor.transpose(dst[:, c * S + t * P:c * S + (t + 1) * P], src, ident)
                    mm.then_inc(full_of("xpT", h), 1)
                if name == "in2_x":
                    channels_out(name, nT, "xq")
                else:
                    tokens_out(name, nT, lambda t: slot_key(name, t))
            for key, name, src, n_blocks, ready in (
                    ("y_x", "x_o", (xoT_hi, xoT_lo), 1, "xoT"), ("y_pool", "pool_o", (poolT_hi, poolT_lo), 2, "poolT"),
                    ("y_sb", "sb_o", (sbT_hi, sbT_lo), 2, "sbT")):
                for c in range(4 if ready == "sbT" else 2):
                    wait_read(pe, ready, c)
                for b in range(n_blocks):
                    rows_out(f"{name}{b}" if n_blocks > 1 else name, src, b == 0, b == n_blocks - 1, 2 * b,
                             lambda t, n: (key, t, n))
            for t in range(NT):
                pe.wait_ge(merged_ready, 2 * t + 2)
                for h in range(2):
                    transposes(xn[:, t, half(h)], "mergedT", t, h)
            for n in range(2):
                for p in "ab":
                    if n == 0:
                        for t in range(NT):
                            wait_read(pe, "mergedT", t, "ab".index(p))
                    tokens_out(f"out2_{n}{p}", nT, lambda t: ("w_out2", n, t))
            for t in range(NT):
                tile_T(5, "n2T", xn, t)
            T_ready("n2T")
            for j in range(FC):
                channels_out(f"ff_in{j}", nT, "ff", j)
            for j in range(FC // 2):
                pe.wait_ge(ffT_ready, 2 * j + 2)
                rows_out(f"ff_out{j}", (hT_hi, hT_lo), j == 0, j == FC // 2 - 1, 2 * j, lambda t, n: ("ff_out", t, n))


def position_constants():
    import numpy as np

    key, query = np.arange(P)[:, None], np.arange(P)[None, :]
    before = (key < query).astype(np.float32)
    mask = np.concatenate([before, np.ones((P, P), np.float32), before], 1)
    const = np.concatenate([np.eye(P), -(key >= query).astype(np.float32), -np.ones((P, P)),
                            mask, np.where(mask > 0, 0.0, NEG), np.zeros((P, P))], 1)
    band = np.zeros((2 * P, 4, S), np.float32)
    s, t = np.arange(S)[:, None], np.arange(S)[None, :]
    for g, w in enumerate((2, 4, 8, 16)):
        inside = (s <= t) & (s > t - w)
        band[:, g] = inside / np.minimum(t + 1, w).astype(np.float32) - (s == t)
    band = np.concatenate([band[0:P], band[P:, :, P:]], 2)
    return const.astype(np.float32), band.astype(np.float32)


def lay_out(inputs):
    import numpy as np

    a = {k: np.asarray(v) for k, v in inputs.items()}
    a = {k: (v if k in ("x", "mem_2") else v[0]) for k, v in a.items()}
    io = {}

    def blocks(w, names, width=HALF):
        k = w.shape[0] // P
        for n, name in enumerate(names):
            part = w[:, n * width:(n + 1) * width].reshape(k, P, width)
            io[name] = part.transpose(1, 0, 2).reshape(P, k * width)

    def halves(w, name):
        for n, part in enumerate("ab"):
            blocks(w[n * HALF:(n + 1) * HALF], [name + part])

    def rows(w, names):
        for n, name in enumerate(names):
            blocks(w[n * S:(n + 1) * S], [name], D)

    io["x"] = a["x"][0]
    for n in range(5):
        halves(a["w_in"][:, n * HALF:(n + 1) * HALF], f"in{n}")
    for n in range(2):
        halves(a["w_out"][:, n * HALF:(n + 1) * HALF], f"out{n}")
        halves(a["w_out_2"][:, n * HALF:(n + 1) * HALF], f"out2_{n}")
    blocks(a["peer_w_query"], [f"query{j}" for j in range(PEER_HEADS)], S)
    io["mem"] = a["mem_2"][0].reshape(NT, P, D).transpose(1, 0, 2).reshape(P, NT * D)
    blocks(a["w_mem_kv_2"], ["mem_k", "mem_v"], S)
    w = a["w_in_2"]
    halves(w[:, 0:512], "in2_p")
    blocks(w[:, 512:1536], ["in2_q0", "in2_q1", "in2_k0", "in2_k1"], S)
    halves(w[:, 1536:2048], "in2_v")
    blocks(w[:, 2048:2304], ["in2_x"], S)
    for n in range(N_GATES):
        halves(w[:, 2304 + n * HALF:2304 + (n + 1) * HALF], f"in2_g{n}")
    rows(a["w_pool_o_2"], ["pool_o0", "pool_o1"])
    rows(a["w_sb_o_2"], ["sb_o0", "sb_o1"])
    rows(a["w_x_o_2"], ["x_o"])
    w = a["w_ffn_in_2"].reshape(D, 2, FC, P).transpose(0, 2, 1, 3).reshape(D, 2 * DFF)
    blocks(w, [f"ff_in{j}" for j in range(FC)], S)
    rows(a["w_ffn_out_2"], [f"ff_out{j}" for j in range(FC // 2)])
    io["w_sT"] = a["gmlp_w_s"].transpose(2, 0, 1)
    rel = np.clip(P + np.arange(P)[:, None] - np.arange(S)[None, :], -P, P) + P
    io["rel"] = a["rel_bias"][list(BIAS_HEADS)][:, rel].transpose(1, 0, 2)
    io["sub_kT"] = a["peer_sub_keys"].reshape(HP, NKEYS, P).transpose(2, 0, 1)
    io["w_mix"] = a["w_pool_mix_2"].transpose(1, 0, 2)
    cols = np.zeros((P, 16), np.float32)
    cols[:, 0] = np.tile(a["q_norm_g"], 2)
    cols[:, 1] = np.tile(a["k_norm_g"], 2)
    cols[:, 2:10] = a["gmlp_b_s"].T
    cols[:, 10:14] = a["pool_scale_2"].reshape(4, P).T
    io["cols"] = cols
    for name in ("ln_mix_g", "gmlp_norm_g", "ln_ffn_g", "norm_mix_pre_2", "norm_mem_2", "norm_mix_post_2",
                 "norm_ffn_pre_2", "norm_ffn_post_2", "peer_u", "peer_v"):
        io[name] = a[name]
    io["const"], io["band"] = position_constants()
    return {k: np.ascontiguousarray(v) for k, v in io.items()}


def kernel(**inputs):
    import concourse.bacc as bacc
    from concourse.bass_utils import run_bass_kernel_spmd

    nc = bacc.Bacc("TRN2", target_bir_lowering=False, num_devices=1)
    arrays = lay_out(inputs)
    io = {k: nc.dram_tensor("in_" + k, v.shape, mybir.dt.from_np(v.dtype), kind="ExternalInput").ap() for k, v in arrays.items()}
    out = nc.dram_tensor("out_y", (S, D), F32, kind="ExternalOutput").ap()
    two_block_kernel(nc, io, out)
    r = run_bass_kernel_spmd(nc, [{"in_" + k: v for k, v in arrays.items()}], core_ids=[0])
    return r.results[0]["out_y"].reshape(1, S, D)
```

```python
from contextlib import ExitStack

import concourse.bass as bass
from concourse import mybir

F32 = mybir.dt.float32
F32R = mybir.dt.float32r
BF16 = mybir.dt.bfloat16
U32 = mybir.dt.uint32
ALU = mybir.AluOpType
ACT = mybir.ActivationFunctionType
AX_X = mybir.AxisListType.X

P = 128
D = 1024
S = 256
NT = S // P
KC = D // P
HALF = 512
EPS = 1e-6
NEG = -1e30
CHUNK = 64
GD = 64
HD = 64
HEADS = 8
PAIRS = HEADS // 2
XHEADS = 4
PEER_HEADS = 8
TOPK = 16
NKEYS = 128
HP = 2 * PEER_HEADS
DFF = 2816
FC = DFF // P
GELU_C = 0.7978845608028654
GELU_A = 0.044715
WB = 2048
R_SLOTS = 4
S_SLOTS = 3
RING = 8
N_GATES = 3 * D // HALF
AHEAD = 3
PEELED = PEER_HEADS - AHEAD + 1
LOOP_STEPS = 42
MIXED = RING + 3
DVE_ROWS = range(RING + 1, TOPK, 2)
PE_ROWS = [k for k in range(TOPK) if k not in DVE_ROWS]

SLOT_BLOCKS = (["in2_va", "in2_vb", "in2_pa", "in2_pb", "in2_x"]
               + [f"in2_g{n}{p}" for n in range(N_GATES) for p in "ab"])
BLOCKS = ([f"in{n}{p}" for n in (1, 2, 3, 4, 0) for p in "ab"]
          + [f"out{n}{p}" for n in range(2) for p in "ab"] + ["mem"] + [f"query{j}" for j in range(PEER_HEADS)]
          + ["mem_k", "mem_v", "in2_q0", "in2_q1", "in2_k0", "in2_k1"] + SLOT_BLOCKS
          + ["x_o", "pool_o0", "pool_o1", "sb_o0", "sb_o1"] + [f"out2_{n}{p}" for n in range(2) for p in "ab"]
          + [f"ff_in{j}" for j in range(FC)] + [f"ff_out{j}" for j in range(FC // 2)])
APART = ("query1", "query2", "query3", "query7", "mem_k")
BLOCK_AT = {name: n for n, name in enumerate(name for name in BLOCKS if name not in APART)}
IN_SLOTS = list(BLOCK_AT)
SPLIT = [name for name in BLOCKS if not name.startswith(("query", "mem"))]
SPLIT_AT = {name: n for n, name in enumerate(SPLIT)}
RAW_USE = {f"query{j}": ("query", j) for j in range(PEER_HEADS)} | {"mem_k": ("mk",), "mem_v": ("mv",)}


def last_product(name):
    base, part = name[:-1], name[-1]
    if name in ("in2_x", "x_o"):
        return ("xq",) if name == "in2_x" else ("y_x", NT - 1, 1)
    if name.startswith(("in2_q", "in2_k")):
        return (name[4:5] + "2", int(part))
    if name.startswith("ff_in"):
        return ("ff", int(name[5:]))
    if name.startswith("ff_out"):
        return ("ff_out", NT - 1, 1) if name == f"ff_out{FC // 2 - 1}" else None
    if name.startswith(("pool_o", "sb_o")):
        return ("y_" + base[:-2], NT - 1, 1) if part == "1" else None
    if part == "a":
        return None
    if name.startswith("in2_g"):
        return ("gate", int(name[5:-1]), NT - 1)
    if name in ("in2_vb", "in2_pb"):
        return (("v2", NT - 1) if name == "in2_vb" else ("pool_in", NT - 1))
    if name.startswith("out2_"):
        return ("w_out2", int(name[5:-1]), NT - 1)
    return ("proj" if name.startswith("in") else "w_out", int(name[-2]), NT - 1)


PART_AT = {}
for _name in SPLIT:
    if last_product(_name) is None:
        PART_AT[_name] = len(PART_AT) + 1

UNITS = [(0, (0, 2, 4, 6)), (0, (1, 3, 5, 7)), (1, (0, 2)), (1, (1, 3)), (1, (4, 6)), (1, (5, 7))]
BIAS_HEADS = (0, 2, 4, 6, 1, 3, 5, 7)
HEADS_DONE = (3, 5)

Z_SLOT, CUM_SLOT, ATT_SLOT = 0, 2, 4
MIX_SLOT, POOL_SLOT = (9, 11), (12, 13)
XS_SLOT = (8, 10)
XPT_SLOT, XO_SLOT = 12, 13


def pair_at(i, first):
    p = (i - first) // 2
    return p if (i - first) % 2 == 0 and 0 <= p < PAIRS else None


def psum_uses():
    uses, count, turn, held = {}, [0] * 8, {}, set()

    def use(*key, among=tuple(range(8))):
        free = [b for b in among if b not in held]
        n = turn.get(among, 0)
        while among[n % len(among)] not in free:
            n += 1
        b = among[n % len(among)]
        turn[among] = n + 1
        uses[key] = (b, count[b])
        count[b] += 1
        return b

    def both(name):
        for t in range(NT):
            for h in range(2):
                use(name, t, h)

    both("xT")
    for n in (1, 2, 3, 4):
        for t in range(NT):
            use("proj", n, t)
    for name in ("qT", "kT"):
        for t in range(NT):
            use(name, t)
    use("score", 0)
    use("score", 1)
    use("score", 2)
    for t in range(NT):
        use("proj", 0, t)
    for u in range(len(UNITS)):
        if 3 <= u + 2 < len(UNITS):
            use("score", u + 2)
        use("pT", u)
        if u == 0:
            held.add(use("oT", 0))
            held.add(use("oT", 1))
        if u in (1, 3):
            use("spatial", u // 2)
        if u in (4, 5):
            use("aT", u - 4)
    held.clear()
    for key in (("w_out", 0, 0), ("w_out", 1, 0), ("w_out", 0, 1), ("xbT", 0, 0), ("xbT", 0, 1), ("query0",), ("route0",),
                ("w_out", 1, 1), ("xbT", 1, 0), ("xbT", 1, 1)):
        use(*key)
    for j in range(AHEAD):
        use("query", j)
        use("route", j)
    for n in range(2):
        held.add(use("expert", 0, n))
    for j in range(AHEAD, PEER_HEADS):
        use("query", j)
        use("route", j)
    both("memT")
    use("mk")
    use("mv")
    held.clear()
    for n in range(2):
        held.add(use("expert", 1, n))
    both("nT")
    held.clear()
    for key in ("q2", "k2"):
        for c in range(2):
            use(key, c)
    z_banks, sum_banks, one = (0, 1, 2, 3), (4, 5, 6), (7,)
    for i, name in enumerate(SLOT_BLOCKS):
        if pair_at(i, ATT_SLOT) is not None:
            use("sbT", pair_at(i, ATT_SLOT), among=one)
        if pair_at(i, Z_SLOT) is not None:
            for a in range(2):
                use("z", 2 * pair_at(i, Z_SLOT) + a, among=z_banks)
        if i in XS_SLOT:
            for j in range(2):
                use("xs", XS_SLOT.index(i), j, among=z_banks)
        if i in MIX_SLOT:
            use("mix", MIX_SLOT.index(i), among=one)
        if i in POOL_SLOT:
            use("poolT", POOL_SLOT.index(i), among=one)
        if 0 <= i - XPT_SLOT < XHEADS:
            use("xpT", i - XPT_SLOT, among=z_banks)
        if 0 <= i - XO_SLOT < XHEADS and (i - XO_SLOT) % 2 == 0:
            use("xoT", (i - XO_SLOT) // 2, among=z_banks)
        if name == "in2_x":
            use("xq", among=sum_banks)
        elif name[-1] == "a":
            for t in range(NT):
                use(*slot_key(name, t), among=sum_banks)
    for key in ("y_x", "y_pool", "y_sb"):
        for t in range(NT):
            for n in range(2):
                use(key, t, n)
    both("mergedT")
    for n in range(2):
        for t in range(NT):
            use("w_out2", n, t)
    both("n2T")
    for j in range(FC):
        use("ff", j)
    for t in range(NT):
        for n in range(2):
            use("ff_out", t, n)
    return uses


def slot_key(name, t):
    if name.startswith("in2_g"):
        return ("gate", int(name[5:-1]), t)
    return ("v2", t) if name.startswith("in2_v") else ("pool_in", t)


def rounded_order():
    keys = [("xT", t, h) for h in range(2) for t in range(NT)]
    keys += [("oT", 0), ("aT", 0), ("oT", 1), ("aT", 1)]
    keys += [("nT", t, h) for t in range(NT) for h in range(2)]
    for i in range(len(SLOT_BLOCKS)):
        if pair_at(i, ATT_SLOT) is not None:
            keys.append(("sbT", pair_at(i, ATT_SLOT)))
        if i in POOL_SLOT:
            keys.append(("poolT", POOL_SLOT.index(i)))
        if 0 <= i - XO_SLOT < XHEADS and (i - XO_SLOT) % 2 == 1:
            keys.append(("xoT", (i - XO_SLOT) // 2))
    keys += [("mergedT", t, h) for t in range(NT) for h in range(2)]
    keys += [("n2T", t, h) for h in range(2) for t in range(NT)]
    return {key: n for n, key in enumerate(keys)}


def two_block_kernel(nc, io, out):
    bank_use = psum_uses()
    rounded = rounded_order()

    def at(*key):
        return bank_use[key]

    with ExitStack() as ctx:
        def sb(name, shape, dt=F32):
            return ctx.enter_context(nc.sbuf_tensor(name, shape, dt))

        def sem(name):
            return ctx.enter_context(nc.semaphore(name))

        bank = [ctx.enter_context(nc.psum_tensor(f"bank{b}", [P, HALF], F32)) for b in range(8)]

        x_sb = sb("x_sb", [P, NT, D])
        xn = sb("xn", [P, NT, D])
        wraw = sb("wraw", [P, R_SLOTS, WB])
        gain = sb("gain", [P, 2, D])
        const = sb("const", [P, 4 * P + 2 * 384])
        cols = sb("cols", [P, 16])
        mkT = sb("mkT", [P, 2, S])
        mv = sb("mv", [P, NT, 256])
        stat = sb("stat", [P, 3, 16])
        junk = sb("junk", [P, D], BF16)
        eps = sb("eps", [P, 1])
        small = sb("small", [P, 256])
        rank = sb("rank", [P, 4, TOPK], U32)
        eidx = sb("eidx", [P, 2, TOPK], U32)
        attn_stat = sb("attn_stat", [P, 4, len(UNITS), 4])
        qk_stat = sb("qk_stat", [P, 3, 4, HEADS])
        xstat = sb("xstat", [P, 4, 8])

        arena_bytes = 141312
        arena = sb("arena", [P, arena_bytes // 4])
        first_byte = nc.sbuf_base - arena_bytes

        def place(name, off, shape, dt=F32):
            size = 4
            for n in shape[1:]:
                size *= n
            assert off + size <= arena_bytes, name
            return nc.alloc_sbuf_tensor_at(name, shape, dt, offset=first_byte + off)

        KB = 1024
        w_hi = place("w_hi", 0, [P, S_SLOTS, WB], F32R)
        w_lo = place("w_lo", 24 * KB, [P, S_SLOTS, WB], F32R)
        w_hi_last = place("w_hi_last", 102 * KB, [P, WB], F32R)
        w_lo_last = place("w_lo_last", 110 * KB, [P, WB], F32R)
        aT_hi = place("aT_hi", 48 * KB, [P, KC, S], F32R)
        aT_lo = place("aT_lo", 56 * KB, [P, KC, S], F32R)
        u_sb = place("u_sb", 64 * KB, [P, NT, HALF])
        vg = place("vg", 68 * KB, [P, NT, HALF])
        q_sb = place("q_sb", 72 * KB, [P, NT, HALF])
        k_sb = place("k_sb", 76 * KB, [P, NT, HALF])
        v_sb = place("v_sb", 80 * KB, [P, NT, HALF])
        w_sT = place("w_sT", 84 * KB, [P, 8, P])
        bias0 = place("bias0", 88 * KB, [P, HEADS, P])
        bias1 = place("bias1", 92 * KB, [P, HEADS, S])
        qT = place("qT", 100 * KB, [P, 4, S])
        kT = place("kT", 104 * KB, [P, 4, S])
        sq = place("sq", 108 * KB, [P, 4, HALF])
        prob = place("prob", 108 * KB, [P, 3, HALF])
        probT = place("probT", 116 * KB, [P, 2, HALF])
        gmlp_g = place("gmlp_g", 120 * KB, [P, HALF])
        mem_n = place("mem_n", 122 * KB, [P, NT, D])
        sub_kT = place("sub_kT", 130 * KB, [P, HP, NKEYS])
        u_ring = place("u_ring", 0, [P, RING, D])
        v_ring = place("v_ring", 32 * KB, [P, RING, D])
        diag = place("diag", 64 * KB, [P, RING, P])
        route = place("route", 68 * KB, [P, NT * PEER_HEADS * 2 * NKEYS])
        head_sc = place("head_sc", 84 * KB, [P, 2, NKEYS])
        head_sc2 = place("head_sc2", 85 * KB, [P, 2, NKEYS])
        cand = place("cand", 86 * KB, [P, TOPK * TOPK])
        cand2 = place("cand2", 87 * KB, [P, TOPK * TOPK])
        onehot = place("onehot", 88 * KB, [P, 2, TOPK, TOPK])
        q2T = place("q2T", 90 * KB, [P, 2, 2, S])
        bT = place("bT", 94 * KB, [P, KC, S])
        apart_v = place("apart_v", 32 * KB, [P, 2, WB // 2])
        apart_diag = place("apart_diag", 64 * KB, [P, WB // 2])
        apart_probT = place("apart_probT", 118 * KB, [P, WB // 2])
        apart_route0 = place("apart_route0", 72 * KB, [P, WB // 2])
        apart_route1 = place("apart_route1", 80 * KB, [P, WB // 2])
        apart_last = place("apart_last", 102 * KB, [P, 4, WB // 2])
        w_apart = {"query1": (apart_v[:, 0, :], apart_v[:, 1, :]), "query2": (apart_diag[:, :], apart_probT[:, :]),
                   "query3": (apart_route0[:, :], apart_route1[:, :]), "query7": (apart_last[:, 0, :], apart_last[:, 1, :]),
                   "mem_k": (apart_last[:, 2, :], apart_last[:, 3, :])}
        nT_hi = place("nT_hi", 102 * KB, [P, KC, S], F32R)
        nT_lo = place("nT_lo", 110 * KB, [P, KC, S], F32R)
        gates = place("gates", 48 * KB, [P, NT, 3 * D])
        xqT = place("xqT", 70 * KB, [P, 2, S])
        sbT_hi = place("sbT_hi", 72 * KB, [P, 4, S], F32R)
        sbT_lo = place("sbT_lo", 76 * KB, [P, 4, S], F32R)
        poolT_hi = place("poolT_hi", 80 * KB, [P, 4, S], F32R)
        poolT_lo = place("poolT_lo", 84 * KB, [P, 4, S], F32R)
        p_sb = place("p_sb", 88 * KB, [P, NT, HALF])
        k3T = place("k3T", 92 * KB, [P, 4, S])
        v3 = place("v3", 96 * KB, [P, NT, HALF])
        w_mix = place("w_mix", 100 * KB, [P, 4, P])
        q3T = place("q3T", 118 * KB, [P, 4, S])
        mixT = place("mixT", 118 * KB, [P, 4, S])
        sp_e = place("sp_e", 122 * KB, [P, 2, 384])
        sp_l = place("sp_l", 125 * KB, [P, 2, 384])
        att = place("att", 128 * KB, [P, 2, 384])
        band = place("band", 131 * KB, [P, 4, 384])
        xprob = place("xprob", 92 * KB, [P, 8, S])
        xpT = place("xpT", 122 * KB, [P, 2, HALF])
        xoT_hi = place("xoT_hi", 128 * KB, [P, 2, S], F32R)
        xoT_lo = place("xoT_lo", 130 * KB, [P, 2, S], F32R)
        tmp = place("tmp", 132 * KB, [P, HALF])
        hT_hi = place("hT_hi", 48 * KB, [P, FC, S], F32R)
        hT_lo = place("hT_lo", 70 * KB, [P, FC, S], F32R)
        z_sb = place("z_sb", 92 * KB, [P, NT, D])
        silu = place("silu", 118 * KB, [P, 2, S])
        h32 = place("h32", 120 * KB, [P, 2, S])

        ident = const[:, 0:P]
        negtri = const[:, P:2 * P]
        negones = const[:, 2 * P:3 * P]
        mask01 = const[:, 3 * P:3 * P + 384]
        maskneg = const[:, 3 * P + 384:3 * P + 768]
        zeros = const[:, 3 * P + 768:4 * P + 768]
        top = small[:, 0:32].rearrange("p (a b) -> p a b", a=2)
        topi = small[:, 32:64].rearrange("p (a b) -> p a b", a=2)
        best = small[:, 64:80]
        ij = small[:, 80:112]
        picked = small[:, 112:144]
        hdot = small[:, 144:160]
        gexp = small[:, 160:176]
        gq = small[:, 176:192]
        ge = small[:, 192:208]
        wexp = small[:, 208:224]
        nbest = small[:, 224:225]
        gsum = small[:, 225:226]
        rsum = small[:, 226:227]
        iota = small[:, 240:256]
        unread = small[:, 229:240]

        bank_full = [sem(f"bank_full{b}") for b in range(8)]
        bank_read = [sem(f"bank_read{b}") for b in range(8)]
        w_loaded = [sem(f"w_loaded{i}") for i in range(R_SLOTS)]
        apart_loaded = [sem(f"apart_loaded{i}") for i in range(len(APART))]
        w_rounded = sem("w_rounded")
        w_split = sem("w_split")
        w_part = sem("w_part")
        act_rounded = sem("act_rounded")
        x_loaded = [sem(f"x_loaded{t}") for t in range(NT)]
        ident_loaded = sem("ident_loaded")
        const_loaded = sem("const_loaded")
        cols_loaded = sem("cols_loaded")
        gain_loaded = [sem(f"gain_loaded{i}") for i in range(2)]
        a_loaded = sem("a_loaded")
        subk_loaded = sem("subk_loaded")
        pool_loaded = sem("pool_loaded")
        u_loaded = [sem(f"u_loaded{i}") for i in range(RING)]
        v_loaded = [sem(f"v_loaded{i}") for i in range(RING)]
        stored = sem("stored")
        dve_step = sem("dve_step")
        dve_passed = sem("dve_passed")
        act_step = sem("act_step")
        eps_set = sem("eps_set")
        root_ready = sem("root_ready")
        rms_ready = sem("rms_ready")
        norm_ready = sem("norm_ready")
        w_masked = sem("w_masked")
        bias_masked = sem("bias_masked")
        iota_ready = sem("iota_ready")
        v_rms = sem("v_rms")
        v_normed = sem("v_normed")
        qk_squared = sem("qk_squared")
        qk_summed = sem("qk_summed")
        qk_rms = sem("qk_rms")
        row_max = sem("row_max")
        row_exp = sem("row_exp")
        prob_ready = sem("prob_ready")
        unit_part = sem("unit_part")
        route_ready = sem("route_ready")
        idx_ready = sem("idx_ready")
        u_used = sem("u_used")
        v_used = sem("v_used")
        best_ready = sem("best_ready")
        gexp_ready = sem("gexp_ready")
        gq_ready = sem("gq_ready")
        ge_ready = sem("ge_ready")
        w_ready = sem("w_ready")
        diag_ready = sem("diag_ready")
        pool_passed = sem("pool_passed")
        z_ln = sem("z_ln")
        l_ready = sem("l_ready")
        cumulated = sem("cumulated")
        att_in = sem("att_in")
        att_ready = sem("att_ready")
        xmax = sem("xmax")
        xprob_ready = sem("xprob_ready")
        even_x = sem("even_x")
        merged_ready = sem("merged_ready")
        h_ready = sem("h_ready")
        silu_ready = sem("silu_ready")
        product_rounded = sem("product_rounded")
        ffT_ready = sem("ffT_ready")

        def spread(ap, dims):
            return bass.AP(tensor=ap.tensor, offset=ap.offset, ap=[ap.ap[0]] + dims)

        def tok(t):
            return slice(t * P, (t + 1) * P)

        def half(n):
            return slice(n * HALF, (n + 1) * HALF)

        def four(ap):
            return ap.rearrange("p (c k) -> p c k", c=4)

        def two(ap):
            return ap.rearrange("p (c k) -> p c k", c=2)

        def wait_loaded(eng, name):
            b = BLOCK_AT[name]
            eng.wait_ge(w_loaded[b % R_SLOTS], 16 * (b // R_SLOTS + 1))
            return wraw[:, b % R_SLOTS, :]

        def wait_halves(eng, name):
            if name in APART:
                eng.wait_ge(apart_loaded[APART.index(name)], 32)
                return w_apart[name]
            w = wait_loaded(eng, name)
            return w[:, 0:WB // 2], w[:, WB // 2:WB]

        def split_slot(name):
            if name == "out1b":
                return w_hi_last[:, :], w_lo_last[:, :]
            s = SPLIT_AT[name] % S_SLOTS
            return w_hi[:, s, :], w_lo[:, s, :]

        def wait_full(eng, *key):
            b, u = at(*key)
            eng.wait_ge(bank_full[b], u + 1)
            return bank[b]

        def wait_read(eng, *key):
            b, u = at(*key)
            eng.wait_ge(bank_read[b], u + 1)

        def read_of(*key):
            return bank_read[at(*key)[0]]

        def full_of(*key):
            return bank_full[at(*key)[0]]

        block = ctx.enter_context(nc.Block())

        @block.sync
        def _(sp):
            def load_block(name):
                b = BLOCK_AT[name]
                if b >= R_SLOTS:
                    freed = IN_SLOTS[b - R_SLOTS]
                    if freed in SPLIT_AT:
                        sp.wait_ge(w_split, SPLIT_AT[freed] + 1)
                    elif freed == "mem":
                        sp.wait_ge(norm_ready, 2 * NT)
                    else:
                        wait_full(sp, *RAW_USE[freed])
                sp.dma_start(wraw[:, b % R_SLOTS, :], io[name]).then_inc(w_loaded[b % R_SLOTS], 16)

            def load_blocks(first, last):
                for name in IN_SLOTS[BLOCK_AT[first]:BLOCK_AT[last] + 1]:
                    load_block(name)

            def load_apart(name):
                for n, dst in enumerate(w_apart[name]):
                    sp.dma_start(dst, io[name][:, n * WB // 2:(n + 1) * WB // 2]).then_inc(apart_loaded[APART.index(name)], 16)

            def load_gain(n, name):
                if n >= 2:
                    sp.wait_ge(norm_ready, NT * (n - 1))
                g = io[name]
                src = bass.AP(tensor=g.tensor, offset=g.offset, ap=[[0, P], [1, D]])
                sp.dma_start(gain[:, n % 2, :], src).then_inc(gain_loaded[n % 2], 16)

            for t in range(NT):
                sp.dma_start(x_sb[:, t, :], io["x"][tok(t), :]).then_inc(x_loaded[t], 16)
            sp.dma_start(ident, io["const"][:, 0:P]).then_inc(ident_loaded, 16)
            load_gain(0, "ln_mix_g")
            load_blocks("in1a", "in2b")
            sp.dma_start(const[:, P:4 * P + 768], io["const"][:, P:4 * P + 768]).then_inc(const_loaded, 16)
            sp.dma_start(cols[:, :], io["cols"]).then_inc(cols_loaded, 16)
            g = io["gmlp_norm_g"]
            sp.dma_start(gmlp_g[:, :], bass.AP(tensor=g.tensor, offset=g.offset, ap=[[0, P], [1, HALF]])).then_inc(a_loaded, 16)
            sp.dma_start(w_sT[:, :, :], io["w_sT"]).then_inc(a_loaded, 16)
            sp.dma_start(bias0[:, :, :], io["rel"][:, :, P:S]).then_inc(a_loaded, 16)
            sp.dma_start(bias1[:, :, :], io["rel"]).then_inc(a_loaded, 16)
            load_gain(1, "norm_mem_2")
            load_blocks("in3a", "in0b")
            load_gain(2, "ln_ffn_g")
            sp.dma_start(sub_kT[:, :, :], io["sub_kT"]).then_inc(subk_loaded, 16)
            load_blocks("out0a", "query0")
            wait_full(sp, "aT", 1)
            wait_full(sp, "oT", 1)
            load_apart("query2")
            load_apart("query3")
            load_blocks("query4", "query6")
            load_gain(3, "norm_mix_pre_2")
            sp.wait_ge(w_part, PART_AT["out0a"])
            load_apart("query1")
            wait_full(sp, "w_out", 1, 1)
            load_apart("query7")
            load_apart("mem_k")
            load_block("mem_v")
            sp.wait_ge(v_loaded[(TOPK - 1) % RING], NT * PEER_HEADS * 16 * (TOPK // RING))
            load_blocks("in2_q0", "in2_k1")
            load_gain(4, "norm_mix_post_2")
            sp.dma_start(band[:, :, :], io["band"]).then_inc(pool_loaded, 16)
            sp.dma_start(w_mix[:, :, :], io["w_mix"]).then_inc(pool_loaded, 16)
            load_blocks("in2_va", "in2_g0a")
            load_gain(5, "norm_ffn_pre_2")
            load_blocks("in2_g0b", "ff_in5")
            load_gain(6, "norm_ffn_post_2")
            load_blocks("ff_in6", BLOCKS[-1])
            for t in range(NT):
                for n in range(2):
                    sp.wait_ge(h_ready, 2 * NT + 2 * t + n + 1)
                    sp.dma_start(out[tok(t), half(n)], x_sb[:, t, half(n)]).then_inc(stored, 16)
            sp.wait_ge(stored, 2 * 16 * NT)

        @block.gpsimd
        def _(pool):
            pool.iota(iota, [[1, TOPK]], base=0, channel_multiplier=0,
                      allow_small_or_imprecise_dtypes=True).then_inc(iota_ready, 1)
            def gather(table, ring, used, loaded, head, hh, ks):
                for k in ks:
                    pool.wait_ge(used, head * TOPK + k + 1)
                    pool.sem_inc(pool_passed, 1)
                    pool.indirect_dma_start(
                        out=ring[:, k % RING, :], out_offset=None, in_=io[table],
                        in_offset=bass.IndirectOffsetOnAxis(ap=eidx[:, hh, k:k + 1], axis=0),
                    ).then_inc(loaded[k % RING], 16)

            def u_rows(head, hh, ks):
                gather("peer_u", u_ring, u_used, u_loaded, head, hh, ks)

            def v_rows(head, hh, ks):
                gather("peer_v", v_ring, v_used, v_loaded, head, hh, ks)

            def chosen(head):
                pool.wait_ge(idx_ready, head + 1)
                pool.sem_inc(pool_passed, 1)

            def rows(head, hh):
                u_rows(head, hh, range(RING, TOPK))
                v_rows(head, hh, range(MIXED))
                chosen(head + 1)
                for k in range(MIXED, TOPK):
                    u_rows(head + 1, 1 - hh, (k - MIXED,))
                    v_rows(head, hh, (k,))
                u_rows(head + 1, 1 - hh, range(TOPK - MIXED, RING))

            wait_full(pool, "w_out", 1, 1)
            chosen(0)
            u_rows(0, 0, range(RING))
            last = NT * PEER_HEADS - 1
            with pool.Fori(0, (last - 1) // 2) as i:
                for hh in range(2):
                    rows(i * 2 + hh, hh)
            rows(last - 1, 0)
            u_rows(last, 1, range(RING, TOPK))
            v_rows(last, 1, range(TOPK))

        @block.scalar
        def _(act):
            steps = [0]
            split = [0]
            turned = [0]
            tables = [0]

            def written(ins):
                steps[0] += 1
                return ins.then_inc(act_step, 1)

            def all_written():
                act.wait_ge(act_step, steps[0])

            def square(src, n, t, row=0):
                if steps[0]:
                    all_written()
                written(nc.scalar.activation(junk[:, 0:src.shape[1]], src, ACT.Square,
                                             accum_out=stat[:, row, 2 * n + t:2 * n + t + 1]))

            def root(n, t, width=D):
                c = slice(2 * n + t, 2 * n + t + 1)
                all_written()
                nc.scalar.activation(stat[:, 1, c], stat[:, 0, c], ACT.Sqrt,
                                     bias=eps[:, 0:1], scale=1.0 / width).then_inc(root_ready, 1)

            def half_square(src, n, t, m):
                c = slice(2 * n + t, 2 * n + t + 1)
                square(src, n, t, row=m)
                all_written()
                if m == 0:
                    written(nc.scalar.activation(stat[:, 0, c], stat[:, 0, c], ACT.Identity,
                                                 bias=eps[:, 0:1], scale=1.0 / D))
                else:
                    nc.scalar.activation(stat[:, 1, c], stat[:, 1, c], ACT.Sqrt, bias=stat[:, 0, c],
                                         scale=1.0 / D).then_inc(root_ready, 1)

            def load_table(function):
                tables[0] += 1
                nc.scalar.activation(unread[:, tables[0]:tables[0] + 1], eps[:, 0:1], function)

            def split_to(name):
                while split[0] <= SPLIT_AT[name]:
                    s = split[0]
                    raw = wait_loaded(act, SPLIT[s])
                    if s >= S_SLOTS and SPLIT[s] != "out1b":
                        done = last_product(SPLIT[s - S_SLOTS])
                        if done:
                            wait_full(act, *done)
                        else:
                            act.wait_ge(w_part, PART_AT[SPLIT[s - S_SLOTS]])
                    nc.scalar.copy(split_slot(SPLIT[s])[0], raw).then_inc(w_rounded, 1)
                    split[0] += 1

            def split_ahead(name, ahead=S_SLOTS):
                split_to(SPLIT[min(SPLIT_AT[name] + ahead, len(SPLIT) - 1)])

            def round_use(key, *copies):
                assert rounded[key] == turned[0], key
                turned[0] += 1
                wait_full(act, *key)
                for dst, src, scale in copies:
                    if scale is None:
                        ins = nc.scalar.copy(dst, src)
                    else:
                        ins = nc.scalar.activation(dst, src, ACT.Copy, scale=scale)
                ins.then_inc(act_rounded, 1)

            def round_tile(name, dst, t, h, scale=None):
                round_use((name, t, h), (dst[:, 4 * h:4 * h + 4, tok(t)], four(bank[at(name, t, h)[0]][:, :]), scale))

            def copy_half_T(name, dst, t, h):
                src = wait_full(act, name, t, h)
                nc.scalar.copy(dst[:, 4 * h:4 * h + 4, tok(t)], four(src[:, :])).then_inc(read_of(name, t, h), 1)

            act.wait_ge(eps_set, 1)
            load_table(ACT.Sqrt)
            split_to("in1a")
            for h in range(2):
                for t in range(NT):
                    round_tile("xT", aT_hi, t, h)
            split_to("in2a")
            for t in range(NT):
                act.wait_ge(x_loaded[t], 16)
                square(x_sb[:, t, :], 0, t)
                root(0, t)
            load_table(ACT.Gelu_apprx_tanh)
            act.wait_ge(rms_ready, NT)
            row_scale = [stat[:, 2, t:t + 1] for t in range(NT)]
            split_to("in2b")
            for t in range(NT):
                src = wait_full(act, "proj", 1, t)
                nc.scalar.activation(vg[:, t, :], src[:, :], ACT.Gelu_apprx_tanh,
                                     scale=row_scale[t]).then_inc(read_of("proj", 1, t), 1)
            for t in range(NT):
                wait_read(act, "proj", 1, t)
                square(vg[:, t, :], 7, t)
            load_table(ACT.Sqrt)
            split_to("in3a")
            for n in (2, 3):
                split_to(f"in{n + 1}b")
                for t in range(NT):
                    src = wait_full(act, "proj", n, t)
                    nc.scalar.activation(sq[:, 2 * (n - 2) + t, :], src[:, :], ACT.Square,
                                         scale=row_scale[t]).then_inc(qk_squared, 1)
                if n == 2:
                    split_to("in4a")
            sums, roots = (qk_stat[:, n, :, :].rearrange("p a b -> p (a b)") for n in range(2))
            all_written()
            nc.scalar.activation(stat[:, 1, 14:16], stat[:, 0, 14:16], ACT.Sqrt, bias=eps[:, 0:1],
                                 scale=1.0 / HALF).then_inc(v_rms, 1)
            act.wait_ge(qk_summed, 4)
            nc.scalar.activation(roots, sums, ACT.Sqrt, bias=eps[:, 0:1], scale=1.0 / HD).then_inc(qk_rms, 1)
            load_table(ACT.Exp)
            split_to("in0b")
            for t in range(NT):
                src = wait_full(act, "proj", 4, t)
                nc.scalar.activation(v_sb[:, t, :], src[:, :], ACT.Copy,
                                     scale=row_scale[t]).then_inc(read_of("proj", 4, t), 1)
            split_to("out0a")

            def exps(u):
                act.wait_ge(row_max, u + 1)
                heads = len(UNITS[u][1])
                w = HALF // heads
                for a in range(heads):
                    ins = nc.scalar.activation(prob[:, u % 3, a * w:(a + 1) * w], prob[:, u % 3, a * w:(a + 1) * w], ACT.Exp,
                                               bias=attn_stat[:, 1, u, a:a + 1], accum_out=attn_stat[:, 2, u, a:a + 1])
                ins.then_inc(row_exp, 1)

            exps(0)
            exps(1)
            exps(2)
            split_to("out0b")
            for t in range(NT):
                src = wait_full(act, "proj", 0, t)
                nc.scalar.activation(u_sb[:, t, :], src[:, :], ACT.Gelu_apprx_tanh,
                                     scale=row_scale[t]).then_inc(read_of("proj", 0, t), 1)
            for u in range(len(UNITS)):
                src = wait_full(act, "pT", u)
                if u >= 2:
                    if u - 2 in HEADS_DONE:
                        wait_full(act, "oT", HEADS_DONE.index(u - 2))
                    else:
                        act.wait_ge(unit_part, u - 1)
                nc.scalar.copy(probT[:, u % 2, :], src[:, :]).then_inc(read_of("pT", u), 1)
                if 3 <= u + 2 < len(UNITS):
                    exps(u + 2)
                if u == 4:
                    round_use(("oT", 0), (aT_hi[:, 4:6, :], two(bank[at("oT", 0)[0]][:, :]), None))
            for t in range(NT):
                round_use(("aT", t), (aT_hi[:, 0:4, tok(t)], four(bank[at("aT", t)[0]][:, :]), None))
                if t == 0:
                    round_use(("oT", 1), (aT_hi[:, 6:8, :], two(bank[at("oT", 1)[0]][:, :]), None))
            split_to("out1b")
            mem = wait_loaded(act, "mem")
            for t in range(NT):
                square(mem[:, t * D:(t + 1) * D], 1, t)
                root(1, t)

            def router_input(t):
                for n in range(2):
                    wait_read(act, "w_out", n, t)
                square(x_sb[:, t, :], 2, t)
                root(2, t)
                copy_half_T("xbT", bT, t, 0)

            def router(j, tiles=(0, 1)):
                q_key, r_key = (("query0",), ("route0",)) if tiles == (0,) else (("query", j), ("route", j))
                first, width = tiles[0] * P, len(tiles) * P
                src = wait_full(act, *q_key)
                if j >= 2:
                    wait_full(act, "route", j - 2)
                nc.scalar.copy(q2T[:, j % 2, :, first:first + width],
                               two(src[:, 0:2 * width])).then_inc(read_of(*q_key), 1)
                src = wait_full(act, *r_key)
                act.wait_ge(rms_ready, 2 * NT + tiles[-1] + 1)
                for i, t in enumerate(tiles):
                    ins = nc.scalar.activation(route[:, (t * PEER_HEADS + j) * S:(t * PEER_HEADS + j + 1) * S],
                                               src[:, i * S:(i + 1) * S], ACT.Copy, scale=stat[:, 2, 2 * NT + t:2 * NT + t + 1])
                    if t == tiles[-1]:
                        ins.then_inc(read_of(*r_key), 1)
                    else:
                        ins.then_inc(route_ready, 2 if j == PEER_HEADS - 1 else 1)

            router_input(0)
            router(0, (0,))
            router_input(1)
            router(0, (1,))

            def after(head):
                if AHEAD + head < PEER_HEADS:
                    router(AHEAD + head)
                else:
                    for t in range(NT):
                        for h in range(2):
                            copy_half_T("memT", bT, t, h)
                    src = wait_full(act, "mk")
                    nc.scalar.copy(mkT[:, :, :], two(src[:, :])).then_inc(read_of("mk"), 1)
                    src = wait_full(act, "mv")
                    nc.scalar.copy(mv[:, :, :], two(src[:, :])).then_inc(read_of("mv"), 1)

            for j in range(1, AHEAD):
                router(j)
                if j == 1:
                    nc.scalar.activation(small[:, 228:229], eps[:, 0:1], ACT.Copy).then_inc(v_used, RING)

            def weights(head):
                act.wait_ge(best_ready, head + 1)
                nc.scalar.activation(gexp, best, ACT.Exp, bias=nbest, accum_out=gsum).then_inc(gexp_ready, 1)
                act.wait_ge(gq_ready, head + 1)
                nc.scalar.activation(ge, gq, ACT.Tanh, scale=GELU_C).then_inc(ge_ready, 1)
                act.wait_ge(w_ready, head + 1)

            def diagonals(head, ks):
                for k in ks:
                    act.wait_ge(v_used, head * TOPK + k + 1)
                    nc.scalar.activation(diag[:, k % RING, :], ident, ACT.Copy,
                                         scale=wexp[:, k:k + 1]).then_inc(diag_ready, 1)

            for head in range(PEELED):
                weights(head)
                diagonals(head, range(TOPK))
                after(head)

            def block_2_input(t):
                for n in range(2):
                    wait_read(act, "expert", t, n)
                square(x_sb[:, t, :], 3, t)
                root(3, t)

            def round_input(t):
                for h in range(2):
                    round_tile("nT", nT_hi, t, h)

            with act.Fori(0, (PEER_HEADS - PEELED) // 2) as i:
                for hh in range(2):
                    head = PEELED + i * 2 + hh
                    weights(head)
                    diagonals(head, range(TOPK))
            for head in (PEER_HEADS, PEER_HEADS + 1):
                weights(head)
                diagonals(head, range(RING))
                if head == PEER_HEADS:
                    block_2_input(0)
                diagonals(head, range(RING, TOPK))
                if head == PEER_HEADS:
                    round_input(0)
            with act.Fori(0, PEER_HEADS // 2 - 2) as i:
                for hh in range(2):
                    head = PEER_HEADS + 2 + i * 2 + hh
                    weights(head)
                    diagonals(head, range(TOPK))
            for head, rows in ((NT * PEER_HEADS - 2, range(TOPK)), (NT * PEER_HEADS - 1, PE_ROWS)):
                weights(head)
                if rows is PE_ROWS:
                    load_table(ACT.Sqrt)
                diagonals(head, rows)
            block_2_input(1)
            split_to("in2_q0")
            round_input(1)
            split_to("in2_q1")

            split_to("in2_k0")
            split_to("in2_k1")
            split_to("in2_va")
            for c in range(2):
                src = wait_full(act, "k2", c)
                nc.scalar.copy(k3T[:, 2 * c:2 * c + 2, :], two(src[:, :])).then_inc(read_of("k2", c), 1)
                split_ahead(f"in2_k{c}")
            e_pair, att_pair = (b[:, :, :].rearrange("p a b -> p (a b)") for b in (sp_e, att))
            for i, name in enumerate(SLOT_BLOCKS):
                z, cum, attend = pair_at(i, Z_SLOT), pair_at(i, CUM_SLOT), pair_at(i, ATT_SLOT)
                if z is not None:
                    for a in range(2):
                        src = wait_full(act, "z", 2 * z + a)
                        if z:
                            act.wait_ge(l_ready, z)
                        written(nc.scalar.activation(sp_e[:, a, :], src[:, 0:384], ACT.Abs))
                    all_written()
                    written(nc.scalar.activation(e_pair, e_pair, ACT.Exp, scale=-1.0))
                if cum is not None:
                    act.wait_ge(att_in, cum + 1)
                    nc.scalar.activation(att_pair, att_pair, ACT.Exp).then_inc(att_ready, 1)
                if z is not None:
                    all_written()
                    nc.scalar.activation(e_pair, e_pair, ACT.Ln, bias=1.0).then_inc(z_ln, 1)
                if attend is not None:
                    round_use(("sbT", attend), (sbT_hi[:, attend, :], bank[at("sbT", attend)[0]][:, 0:S], None))
                if i in XS_SLOT:
                    t = XS_SLOT.index(i)
                    for j in range(2):
                        act.wait_ge(xmax, 2 * t + j + 1)
                        src = bank[at("xs", t, j)[0]]
                        for a in range(2):
                            n = 4 * t + 2 * j + a
                            ins = nc.scalar.activation(xprob[:, n, :], src[:, a * S:(a + 1) * S], ACT.Exp,
                                                       scale=HD ** -0.5, bias=xstat[:, 1, n:n + 1],
                                                       accum_out=xstat[:, 2, n:n + 1])
                        ins.then_inc(read_of("xs", t, j), 1)
                if i in MIX_SLOT:
                    c = MIX_SLOT.index(i)
                    src = wait_full(act, "mix", c)
                    nc.scalar.copy(mixT[:, 2 * c:2 * c + 2, :], two(src[:, :])).then_inc(read_of("mix", c), 1)
                if i in POOL_SLOT:
                    c = POOL_SLOT.index(i)
                    src = bank[at("poolT", c)[0]]
                    act.wait_ge(cols_loaded, 16)
                    round_use(("poolT", c), *((poolT_hi[:, 2 * c + a, :], src[:, a * S:(a + 1) * S],
                                               cols[:, 10 + 2 * c + a:11 + 2 * c + a]) for a in range(2)))
                h = i - XPT_SLOT
                if 0 <= h < XHEADS:
                    src = wait_full(act, "xpT", h)
                    if h >= 2:
                        if h % 2 == 0:
                            act.wait_ge(even_x, h // 2)
                        else:
                            wait_full(act, "xoT", (h - 2) // 2)
                    nc.scalar.copy(xpT[:, h % 2, :], src[:, :]).then_inc(read_of("xpT", h), 1)
                h = i - XO_SLOT
                if 0 <= h < XHEADS and h % 2 == 1:
                    round_use(("xoT", h // 2), (xoT_hi[:, h // 2, :], bank[at("xoT", h // 2)[0]][:, 0:S], None))
                if name == "in2_x":
                    src = wait_full(act, "xq")
                    nc.scalar.copy(xqT[:, :, :], two(src[:, :])).then_inc(read_of("xq"), 1)
                elif name[-1] == "b":
                    for t in range(NT):
                        key = slot_key(name, t)
                        src = wait_full(act, *key)
                        if key[0] == "gate":
                            ins = nc.scalar.activation(gates[:, t, half(key[1])], src[:, :], ACT.Tanh, scale=0.5)
                        else:
                            ins = nc.scalar.copy((v3 if key[0] == "v2" else p_sb)[:, t, :], src[:, :])
                        ins.then_inc(read_of(*key), 1)
                split_ahead(name)
            load_table(ACT.Sqrt)
            split_to("out2_0b")
            for t in range(NT):
                for h in range(2):
                    round_tile("mergedT", nT_hi, t, h, scale=0.5)
            split_to("out2_1b")
            for m in range(2):
                for t in range(NT):
                    src = wait_full(act, "w_out2", m, t)
                    half_square(src[:, :], 4, t, m)
                if m == 0:
                    split_to("ff_in1")
            for t in range(NT):
                act.wait_ge(h_ready, 2 * t + 2)
                square(x_sb[:, t, :], 5, t)
                root(5, t)
            load_table(ACT.Silu)
            for h in range(2):
                for t in range(NT):
                    round_tile("n2T", nT_hi, t, h)
            split_to("ff_in2")
            for j in range(FC + 1):
                if j < FC:
                    src = wait_full(act, "ff", j)
                    if j >= 2:
                        wait_read(act, "ff", j - 2)
                    nc.scalar.activation(silu[:, j % 2, :], src[:, 0:S], ACT.Silu).then_inc(silu_ready, 1)
                if j >= 1:
                    wait_read(act, "ff", j - 1)
                    nc.scalar.copy(hT_hi[:, j - 1, :], h32[:, (j - 1) % 2, :]).then_inc(product_rounded, 1)
                if j < FC:
                    split_ahead(f"ff_in{j}")
            load_table(ACT.Sqrt)
            split_to(BLOCKS[-1])
            for t in range(NT):
                for m in range(2):
                    src = wait_full(act, "ff_out", t, m)
                    half_square(src[:, :], 6, t, m)

        @block.vector
        def _(dve):
            steps = [0, 0]
            split = [0]

            def step(ins):
                steps[0] += 1
                ins.then_inc(dve_step, 1)
                dve.wait_ge(dve_step, steps[1] + steps[0])

            def step_apart(ins):
                step(ins)
                dve.sem_inc(dve_passed, 1)

            def invert(n, t):
                c = slice(2 * n + t, 2 * n + t + 1)
                dve.wait_ge(root_ready, NT * n + t + 1)
                nc.vector.reciprocal(stat[:, 2, c], stat[:, 1, c]).then_inc(rms_ready, 1)
                dve.wait_ge(rms_ready, NT * n + t + 1)

            def norm(n, t, src, dst):
                dve.wait_ge(gain_loaded[n % 2], 16 * (n // 2 + 1))
                invert(n, t)
                nc.vector.scalar_tensor_tensor(out=dst, in0=src, scalar=stat[:, 2, 2 * n + t:2 * n + t + 1],
                                               in1=gain[:, n % 2, :], op0=ALU.mult, op1=ALU.mult).then_inc(norm_ready, 1)

            def gained(n, src, dst):
                dve.wait_ge(gain_loaded[n % 2], 16 * (n // 2 + 1))
                nc.vector.tensor_tensor(dst, src, gain[:, n % 2, :], ALU.mult).then_inc(norm_ready, 1)

            def copy_half_T(name, dst, t, h):
                src = wait_full(dve, name, t, h)
                nc.vector.tensor_copy(dst[:, 4 * h:4 * h + 4, tok(t)], four(src[:, :])).then_inc(read_of(name, t, h), 1)

            def split_to(name):
                while split[0] <= SPLIT_AT[name]:
                    s = split[0]
                    dve.wait_ge(w_rounded, s + 1)
                    hi, lo = split_slot(SPLIT[s])
                    nc.vector.tensor_tensor(lo, wraw[:, BLOCK_AT[SPLIT[s]] % R_SLOTS, :], hi.bitcast(F32),
                                            ALU.subtract).then_inc(w_split, 1)
                    split[0] += 1

            def split_ahead(name, ahead=S_SLOTS):
                split_to(SPLIT[min(SPLIT_AT[name] + ahead, len(SPLIT) - 1)])

            def rest(key, *parts):
                dve.wait_ge(act_rounded, rounded[key] + 1)
                for dst, src, hi, scale in parts:
                    if scale is None:
                        ins = nc.vector.tensor_tensor(dst, src, hi.bitcast(F32), ALU.subtract)
                    else:
                        ins = nc.vector.scalar_tensor_tensor(out=dst, in0=src, scalar=scale, in1=hi.bitcast(F32),
                                                             op0=ALU.mult, op1=ALU.subtract)
                ins.then_inc(read_of(*key), 1)

            def rest_tile(name, lo, hi, t, h, scale=None):
                where = (slice(None), slice(4 * h, 4 * h + 4), tok(t))
                rest((name, t, h), (lo[where], four(bank[at(name, t, h)[0]][:, :]), hi[where], scale))

            nc.vector.memset(eps[:, :], EPS).then_inc(eps_set, 1)
            nc.vector.memset(small[:, 227:228], 0.0).then_inc(u_used, RING)
            for t in range(NT):
                dve.wait_ge(x_loaded[t], 16)
                gained(0, x_sb[:, t, :], xn[:, t, :])
            split_to("in1a")
            for h in range(2):
                for t in range(NT):
                    rest_tile("xT", aT_lo, aT_hi, t, h)
            split_to("in2a")
            for t in range(NT):
                invert(0, t)
            dve.wait_ge(a_loaded, 64)
            nc.vector.memset(w_sT[CHUNK:P, :, 0:CHUNK], 0.0).then_inc(w_masked, 1)
            nc.vector.memset(bias0[0:CHUNK, :, CHUNK:P], NEG).then_inc(bias_masked, 1)
            nc.vector.memset(bias1[0:CHUNK, :, S - CHUNK:S], NEG).then_inc(bias_masked, 1)
            split_to("in3a")

            def head_sums(c):
                dve.wait_ge(qk_squared, c + 1)
                nc.vector.tensor_reduce(qk_stat[:, 0, c, :], sq[:, c, :].rearrange("p (h d) -> p h d", h=HEADS),
                                        AX_X, ALU.add).then_inc(qk_summed, 1)

            split_to("in3b")
            for t in range(NT):
                head_sums(t)
            split_to("in4b")
            for t in range(NT):
                head_sums(2 + t)
            dve.wait_ge(v_rms, 1)
            nc.vector.reciprocal(stat[:, 2, 14:16], stat[:, 1, 14:16])
            dve.wait_ge(qk_rms, 1)
            step(nc.vector.reciprocal(qk_stat[:, 2, :, :], qk_stat[:, 1, :, :]))
            for c in range(4):
                ins = nc.vector.tensor_scalar(qk_stat[:, 2, c, :], qk_stat[:, 2, c, :], stat[:, 2, c % NT:c % NT + 1], None,
                                              ALU.mult)
                if c == 3:
                    step(ins)
            for n, dst in ((0, q_sb), (1, k_sb)):
                for t in range(NT):
                    c = 2 * n + t
                    src = bank[at("proj", 2 + n, t)[0]]
                    nc.vector.tensor_tensor(dst[:, t, :].rearrange("p (h d) -> p h d", h=HEADS),
                                            src[:, :].rearrange("p (h d) -> p h d", h=HEADS),
                                            spread(qk_stat[:, 2, c, :], [[1, HEADS], [0, HD]]),
                                            ALU.mult).then_inc(read_of("proj", 2 + n, t), 1)
            split_to("in0b")
            dve.wait_ge(cols_loaded, 16)
            for name, dst, col, scale in (("qT", qT, 0, HD ** -0.5), ("kT", kT, 1, 1.0)):
                for t in range(NT):
                    src = wait_full(dve, name, t)
                    nc.vector.tensor_scalar(dst[:, :, tok(t)], four(src[:, :]),
                                            cols[:, col:col + 1], scale, ALU.mult, ALU.mult).then_inc(read_of(name, t), 1)
            split_to("out0a")
            for t in range(NT):
                nc.vector.scalar_tensor_tensor(out=vg[:, t, :], in0=vg[:, t, :], scalar=stat[:, 2, 14 + t:15 + t],
                                               in1=gmlp_g[:, :], op0=ALU.mult, op1=ALU.mult).then_inc(v_normed, 1)

            def maxima(u):
                src = wait_full(dve, "score", u)
                if u >= 3:
                    wait_full(dve, "pT", u - 3)
                t, heads = UNITS[u][0], len(UNITS[u][1])
                first = BIAS_HEADS.index(UNITS[u][1][0])
                p3d = prob[:, u % 3, :].rearrange("p (a b) -> p a b", a=heads)
                nc.vector.tensor_tensor(p3d, src[:, :].rearrange("p (a b) -> p a b", a=heads),
                                        (bias1 if t else bias0)[:, first:first + heads, :],
                                        ALU.add).then_inc(read_of("score", u), 1)
                wait_read(dve, "score", u)
                step(nc.vector.tensor_reduce(attn_stat[:, 0, u, 0:heads], p3d, AX_X, ALU.max))
                nc.vector.tensor_scalar(attn_stat[:, 1, u, 0:heads], attn_stat[:, 0, u, 0:heads], -1.0, None,
                                        ALU.mult).then_inc(row_max, 1)

            def normalise(u):
                dve.wait_ge(row_exp, u + 1)
                heads = len(UNITS[u][1])
                step(nc.vector.reciprocal(attn_stat[:, 3, u, 0:heads], attn_stat[:, 2, u, 0:heads]))
                p3d = prob[:, u % 3, :].rearrange("p (a b) -> p a b", a=heads)
                nc.vector.tensor_tensor(p3d, p3d, spread(attn_stat[:, 3, u, :], [[1, heads], [0, HALF // heads]]),
                                        ALU.mult).then_inc(prob_ready, 1)

            def spatial(t):
                src = wait_full(dve, "spatial", t)
                wait_read(dve, "proj", 0, t)
                v3d = vg[:, t, :].rearrange("p (g c) -> p g c", g=8)
                step(nc.vector.tensor_tensor(v3d, src[:, :].rearrange("p (g c) -> p g c", g=8),
                                             spread(cols[:, 2:10], [[1, 8], [0, GD]]), ALU.add))
                nc.vector.tensor_tensor(u_sb[:, t, :], u_sb[:, t, :], vg[:, t, :], ALU.mult).then_inc(read_of("spatial", t), 1)

            dve.wait_ge(bias_masked, 2)
            maxima(0)
            maxima(1)
            maxima(2)
            normalise(0)
            split_to("out0b")
            for u in range(len(UNITS)):
                if u >= 1:
                    normalise(u)
                if 3 <= u + 2 < len(UNITS):
                    maxima(u + 2)
                if u in (2, 4):
                    spatial(u // 2 - 1)
            rest(("oT", 0), (aT_lo[:, 4:6, :], two(bank[at("oT", 0)[0]][:, :]), aT_hi[:, 4:6, :], None))
            for t in range(NT):
                rest(("aT", t), (aT_lo[:, 0:4, tok(t)], four(bank[at("aT", t)[0]][:, :]), aT_hi[:, 0:4, tok(t)], None))
                if t == 0:
                    rest(("oT", 1), (aT_lo[:, 6:8, :], two(bank[at("oT", 1)[0]][:, :]), aT_hi[:, 6:8, :], None))
            split_to("out1b")
            mem = wait_loaded(dve, "mem")
            for t in range(NT):
                norm(1, t, mem[:, t * D:(t + 1) * D], mem_n[:, t, :])

            def add_mixed(t, n):
                src = wait_full(dve, "w_out", n, t)
                nc.vector.tensor_tensor(x_sb[:, t, half(n)], x_sb[:, t, half(n)], src[:, :],
                                        ALU.add).then_inc(read_of("w_out", n, t), 1)

            def router_input(t):
                for n in range(2):
                    wait_read(dve, "w_out", n, t)
                gained(2, x_sb[:, t, :], xn[:, t, :])
                copy_half_T("xbT", bT, t, 1)
                invert(2, t)
                for h in range(2):
                    wait_full(dve, "xbT", t, h)
                step(nc.vector.tensor_scalar(xn[:, t, :], xn[:, t, :], stat[:, 2, 2 * NT + t:2 * NT + t + 1], None, ALU.mult))

            add_mixed(0, 0)
            add_mixed(0, 1)
            router_input(0)

            def sixteen(*lists):
                for values, spare, out, where in lists:
                    ins = nc.vector.max(out[:, 0:8], values)
                step_apart(ins)
                for values, spare, out, where in lists:
                    nc.vector.max_index(where[:, 0:8], out[:, 0:8], values)
                    ins = nc.vector.match_replace(spare, out[:, 0:8], values, -3.0e38)
                step_apart(ins)
                for values, spare, out, where in lists:
                    ins = nc.vector.max(out[:, 8:16], spare)
                step_apart(ins)
                for values, spare, out, where in lists:
                    ins = nc.vector.max_index(where[:, 8:16], out[:, 8:16], spare)
                step_apart(ins)

            def choose(head, hh):
                scores = head_sc
                if isinstance(head, int) and head == 0:
                    scores = two(route[:, 0:2 * NKEYS])
                else:
                    step_apart(nc.vector.tensor_copy(head_sc[:, :, :].rearrange("p a b -> p (a b)"),
                                                     route[:, bass.ds(head * 2 * NKEYS, 2 * NKEYS)]))
                sixteen(*((scores[:, p, :], head_sc2[:, p, :], top[:, p, :], rank[:, p, :]) for p in range(2)))
                nc.vector.tensor_copy(topi, rank[:, 0:2, :])
                step_apart(nc.vector.tensor_tensor(cand[:, :].rearrange("p (a b) -> p a b", a=TOPK),
                                                   spread(top[:, 0, :], [[1, TOPK], [0, TOPK]]),
                                                   spread(top[:, 1, :], [[0, TOPK], [1, TOPK]]), ALU.add))
                sixteen((cand[:, :], cand2[:, :], best, rank[:, 2, :]))
                nc.vector.tensor_scalar(nbest, best[:, 0:1], -1.0, None, ALU.mult).then_inc(best_ready, 1)
                step(nc.vector.tensor_scalar(rank[:, 3, :], rank[:, 2, :], 4, None, ALU.logical_shift_right))
                step(nc.vector.tensor_scalar(rank[:, 2, :], rank[:, 2, :], 15, None, ALU.bitwise_and))
                nc.vector.tensor_copy(ij[:, 0:TOPK], rank[:, 3, :])
                step(nc.vector.tensor_copy(ij[:, TOPK:2 * TOPK], rank[:, 2, :]))
                step(nc.vector.tensor_tensor(onehot[:, :, :, :].rearrange("p a b c -> p (a b) c"),
                                             spread(ij, [[1, 2 * TOPK], [0, TOPK]]),
                                             spread(iota, [[0, 2 * TOPK], [1, TOPK]]), ALU.is_equal))
                step(nc.vector.tensor_tensor(onehot[:, :, :, :], onehot[:, :, :, :],
                                             spread(topi, [[TOPK, 2], [0, TOPK], [1, TOPK]]), ALU.mult))
                step(nc.vector.tensor_reduce(picked, onehot[:, :, :, :].rearrange("p a b c -> p (a b) c"),
                                             AX_X, ALU.add))
                nc.vector.scalar_tensor_tensor(out=eidx[:, hh, :], in0=picked[:, 0:TOPK], scalar=float(NKEYS),
                                               in1=picked[:, TOPK:2 * TOPK], op0=ALU.mult,
                                               op1=ALU.add).then_inc(idx_ready, 1)

            def weigh(head, t):
                for k in range(TOPK):
                    dve.wait_ge(u_loaded[k % RING], head * 32 + 16 * (k // RING) + 16)
                    nc.vector.scalar_tensor_tensor(out=u_ring[:, k % RING, :], in0=u_ring[:, k % RING, :], scalar=1.0,
                                                   in1=xn[:, t, :], op0=ALU.mult, op1=ALU.mult,
                                                   accum_out=hdot[:, k:k + 1]).then_inc(u_used, 1)
                dve.wait_ge(u_used, head * TOPK + TOPK + RING)
                step(nc.vector.tensor_tensor(gq, hdot, hdot, ALU.mult))
                step(nc.vector.tensor_scalar(gq, gq, GELU_A, 1.0, ALU.mult, ALU.add))
                nc.vector.tensor_tensor(gq, gq, hdot, ALU.mult).then_inc(gq_ready, 1)
                dve.wait_ge(gexp_ready, head + 1)
                step(nc.vector.reciprocal(rsum, gsum))
                step(nc.vector.scalar_tensor_tensor(out=wexp, in0=hdot, scalar=rsum, in1=gexp,
                                                    op0=ALU.mult, op1=ALU.mult))
                dve.wait_ge(ge_ready, head + 1)
                step(nc.vector.tensor_scalar(ge, ge, 1.0, 0.5, ALU.add, ALU.mult))
                nc.vector.tensor_tensor(wexp, wexp, ge, ALU.mult).then_inc(w_ready, 1)

            def add_experts(t):
                for n in range(2):
                    src = wait_full(dve, "expert", t, n)
                    nc.vector.tensor_tensor(x_sb[:, t, half(n)], x_sb[:, t, half(n)], src[:, :],
                                            ALU.add).then_inc(read_of("expert", t, n), 1)

            def rest_input(t):
                for h in range(2):
                    rest_tile("nT", nT_lo, nT_hi, t, h)

            def weigh_and_choose(first, turns, t):
                before = steps[0]
                with dve.Fori(0, turns) as i:
                    steps[1] = i * LOOP_STEPS
                    for hh in range(2):
                        head = first + i * 2 + hh
                        weigh(head, t)
                        if t == 0:
                            dve.wait_ge(route_ready, head + 1)
                            dve.sem_inc(dve_passed, 1)
                        choose(head + 1, (hh + 1) % 2)
                    assert steps[0] - before == LOOP_STEPS, steps[0] - before
                steps[0] += LOOP_STEPS * (turns - 1)
                steps[1] = 0

            dve.wait_ge(iota_ready, 1)
            wait_read(dve, "route0")
            choose(0, 0)
            add_mixed(1, 0)
            add_mixed(1, 1)
            router_input(1)
            weigh_and_choose(0, PEER_HEADS // 2, 0)
            for j in range(PEER_HEADS):
                wait_read(dve, "route", j)
            weigh(PEER_HEADS, 1)
            add_experts(0)
            choose(PEER_HEADS + 1, 1)
            norm(3, 0, x_sb[:, 0, :], xn[:, 0, :])
            weigh(PEER_HEADS + 1, 1)
            choose(PEER_HEADS + 2, 0)
            rest_input(0)
            weigh_and_choose(PEER_HEADS + 2, PEER_HEADS // 2 - 2, 1)
            last = NT * PEER_HEADS - 1
            weigh(last - 1, 1)
            choose(last, 1)
            weigh(last, 1)
            dve.wait_ge(w_ready, last + 1)
            for k in DVE_ROWS:
                dve.wait_ge(v_loaded[k % RING], last * 32 + 16 * (k // RING) + 16)
                step(nc.vector.scalar_tensor_tensor(out=x_sb[:, 1, :], in0=v_ring[:, k % RING, :], scalar=wexp[:, k:k + 1],
                                                    in1=x_sb[:, 1, :], op0=ALU.mult, op1=ALU.add))
            add_experts(1)
            norm(3, 1, x_sb[:, 1, :], xn[:, 1, :])
            split_to("in2_q0")
            rest_input(1)
            split_to("in2_q1")

            split_to("in2_k0")
            dve.wait_ge(const_loaded, 16)
            for c in range(2):
                src = wait_full(dve, "q2", c)
                nc.vector.tensor_scalar(q3T[:, 2 * c:2 * c + 2, :], two(src[:, :]),
                                        HD ** -0.5, None, ALU.mult).then_inc(read_of("q2", c), 1)
                split_ahead(f"in2_q{c}")
            for c in range(2):
                split_ahead(f"in2_k{c}")

            def z_softplus(p):
                dve.wait_ge(z_ln, p + 1)
                for a in range(2):
                    src = bank[at("z", 2 * p + a)[0]]
                    ins = nc.vector.scalar_tensor_tensor(out=sp_e[:, a, :], in0=src[:, 0:384], scalar=0.0,
                                                         in1=sp_e[:, a, :], op0=ALU.max, op1=ALU.add)
                    if a:
                        step(ins)
                nc.vector.tensor_tensor(sp_l[:, :, :], sp_e[:, :, :], spread(mask01, [[0, 2], [1, 384]]),
                                        ALU.mult).then_inc(l_ready, 1)

            def z_weight(p):
                dve.wait_ge(cumulated, p + 1)
                for a in range(2):
                    src = bank[at("z", 2 * p + a)[0]]
                    nc.vector.tensor_scalar(att[:, a, :], src[:, 0:384], 0.0, None,
                                            ALU.min).then_inc(read_of("z", 2 * p + a), 1)
                for a in range(2):
                    wait_read(dve, "z", 2 * p + a)
                nc.vector.tensor_tensor(att[:, :, :], att[:, :, :], spread(maskneg, [[0, 2], [1, 384]]),
                                        ALU.add).then_inc(att_in, 1)

            for i, name in enumerate(SLOT_BLOCKS):
                z, cum, attend = pair_at(i, Z_SLOT), pair_at(i, CUM_SLOT), pair_at(i, ATT_SLOT)
                if cum is not None:
                    z_weight(cum)
                if z is not None:
                    z_softplus(z)
                if attend is not None:
                    rest(("sbT", attend), (sbT_lo[:, attend, :], bank[at("sbT", attend)[0]][:, 0:S], sbT_hi[:, attend, :], None))
                if i in XS_SLOT:
                    t = XS_SLOT.index(i)
                    for j in range(2):
                        n = 4 * t + 2 * j
                        src = wait_full(dve, "xs", t, j)
                        step(nc.vector.tensor_reduce(xstat[:, 0, n:n + 2], two(src[:, :]), AX_X, ALU.max))
                        nc.vector.tensor_scalar(xstat[:, 1, n:n + 2], xstat[:, 0, n:n + 2], -HD ** -0.5, None,
                                                ALU.mult).then_inc(xmax, 1)
                if i - 1 in XS_SLOT:
                    t = XS_SLOT.index(i - 1)
                    n = 4 * t
                    for j in range(2):
                        wait_read(dve, "xs", t, j)
                    step(nc.vector.reciprocal(xstat[:, 3, n:n + 4], xstat[:, 2, n:n + 4]))
                    nc.vector.tensor_tensor(xprob[:, n:n + 4, :], xprob[:, n:n + 4, :],
                                            spread(xstat[:, 3, n:n + 4], [[1, 4], [0, S]]), ALU.mult).then_inc(xprob_ready, 1)
                if i in POOL_SLOT:
                    c = POOL_SLOT.index(i)
                    src = bank[at("poolT", c)[0]]
                    rest(("poolT", c), *((poolT_lo[:, 2 * c + a, :], src[:, a * S:(a + 1) * S], poolT_hi[:, 2 * c + a, :],
                                          cols[:, 10 + 2 * c + a:11 + 2 * c + a]) for a in range(2)))
                h = i - XO_SLOT
                if 0 <= h < XHEADS and h % 2 == 1:
                    c = h // 2
                    rest(("xoT", c), (xoT_lo[:, c, :], bank[at("xoT", c)[0]][:, 0:S], xoT_hi[:, c, :], None))
                split_ahead(name)
            def gated(key, b, t, n, dst):
                wait_read(dve, "gate", 2 * b + n, t)
                src = wait_full(dve, key, t, n)
                return nc.vector.scalar_tensor_tensor(out=dst, in0=gates[:, t, half(2 * b + n)], scalar=1.0, in1=src[:, :],
                                                      op0=ALU.add, op1=ALU.mult).then_inc(read_of(key, t, n), 1)

            def add_gated(key, b, t, n):
                gated(key, b, t, n, tmp[:, :])
                wait_read(dve, key, t, n)
                return nc.vector.tensor_tensor(xn[:, t, half(n)], xn[:, t, half(n)], tmp[:, :], ALU.add)

            split_ahead("x_o")
            for t in range(NT):
                for n in range(2):
                    gated("y_x", 2, t, n, xn[:, t, half(n)])
            split_ahead("pool_o0")
            for t in range(NT):
                for n in range(2):
                    wait_read(dve, "y_x", t, n)
                    step(add_gated("y_pool", 0, t, n))
            split_ahead("pool_o1")
            for t in range(NT):
                for n in range(2):
                    add_gated("y_sb", 1, t, n).then_inc(merged_ready, 1)
                    dve.wait_ge(merged_ready, 2 * t + n + 1)
            for t in range(NT):
                for h in range(2):
                    rest_tile("mergedT", nT_lo, nT_hi, t, h, scale=0.5)
            split_to("out2_1b")

            def add_normed(n, t, key):
                dve.wait_ge(gain_loaded[n % 2], 16 * (n // 2 + 1))
                invert(n, t)
                for m in range(2):
                    src = bank[at(*key(m))[0]]
                    nc.vector.scalar_tensor_tensor(out=z_sb[:, t, half(m)], in0=src[:, :],
                                                   scalar=stat[:, 2, 2 * n + t:2 * n + t + 1],
                                                   in1=gain[:, n % 2, half(m)], op0=ALU.mult,
                                                   op1=ALU.mult).then_inc(read_of(*key(m)), 1)
                for m in range(2):
                    wait_read(dve, *key(m))
                    nc.vector.tensor_tensor(x_sb[:, t, half(m)], x_sb[:, t, half(m)], z_sb[:, t, half(m)],
                                            ALU.add).then_inc(h_ready, 1)

            split_to("ff_in1")
            for t in range(NT):
                add_normed(4, t, lambda m: ("w_out2", m, t))
            nc.vector.memset(unread[:, 0:1], 0.0).then_inc(norm_ready, NT)
            for t in range(NT):
                norm(5, t, x_sb[:, t, :], xn[:, t, :])
            for h in range(2):
                for t in range(NT):
                    rest_tile("n2T", nT_lo, nT_hi, t, h)
            split_to("ff_in2")
            for j in range(FC + 1):
                if j < FC:
                    dve.wait_ge(silu_ready, j + 1)
                    if j >= 2:
                        dve.wait_ge(ffT_ready, j - 1)
                    src = bank[at("ff", j)[0]]
                    nc.vector.tensor_tensor(h32[:, j % 2, :], silu[:, j % 2, :], src[:, S:2 * S],
                                            ALU.mult).then_inc(read_of("ff", j), 1)
                if j >= 1:
                    dve.wait_ge(product_rounded, j)
                    nc.vector.tensor_tensor(hT_lo[:, j - 1, :], h32[:, (j - 1) % 2, :], hT_hi[:, j - 1, :].bitcast(F32),
                                            ALU.subtract).then_inc(ffT_ready, 1)
                if j < FC:
                    split_ahead(f"ff_in{j}")
            split_to(BLOCKS[-1])
            for t in range(NT):
                add_normed(6, t, lambda m: ("ff_out", t, m))

        @block.tensor
        def _(pe):
            def open_bank(*key):
                b, u = at(*key)
                if u:
                    pe.wait_ge(bank_read[b], u)
                return bank[b]

            def transposes(src, *key):
                dst = open_bank(*key)
                for c in range(src.shape[1] // P):
                    mm = nc.tensor.transpose(dst[:, c * P:(c + 1) * P], src[:, c * P:(c + 1) * P], ident)
                mm.then_inc(full_of(*key), 1)

            def keep_warm(turns, *key):
                dst = open_bank(*key)
                for _ in range(turns):
                    nc.tensor.matmul(dst[:, 0:P], ident, ident, start=True, stop=True)

            def tile_T(n, name, src, t):
                pe.wait_ge(norm_ready, NT * n + t + 1)
                for h in range(2):
                    transposes(src[:, t, half(h)], name, t, h)

            def T_ready(name):
                for t in range(NT):
                    for h in range(2):
                        wait_read(pe, name, t, h)

            def split_block(name):
                pe.wait_ge(w_split, SPLIT_AT[name] + 1)
                return split_slot(name)

            def product(dst, a, b, start, stop):
                (a_hi, a_lo), (b_hi, b_lo) = a, b
                nc.tensor.matmul(dst, a_hi, b_hi, start=start, stop=False)
                nc.tensor.matmul(dst, a_hi, b_lo, start=False, stop=False)
                return nc.tensor.matmul(dst, a_lo, b_hi, start=False, stop=stop)

            def parts(pair, *index):
                return tuple(p[index] for p in pair)

            ALL = slice(None)

            def half_ready(name, h):
                for t in range(NT):
                    wait_read(pe, name, t, h)

            def tokens_out(name, aT, key, turned=None, tiles=(0, 1)):
                w = split_block(name)
                first = name[-1] == "a"
                if turned:
                    half_ready(turned, 0 if first else 1)
                for t in tiles:
                    dst = open_bank(*key(t)) if first else bank[at(*key(t))[0]]
                    for c in range(KC // 2):
                        mm = product(dst[:, :], parts(aT, ALL, c + (0 if first else KC // 2), tok(t)),
                                     parts(w, ALL, half(c)), start=first and c == 0, stop=not first and c == KC // 2 - 1)
                    if not first:
                        mm.then_inc(full_of(*key(t)), 1)
                if first and tiles[-1] == NT - 1:
                    mm.then_inc(w_part, 1)

            def rows_out(name, aT, first, last, chunk, key):
                w = split_block(name)
                for t in range(NT):
                    for n in range(2):
                        dst = open_bank(*key(t, n)) if first else bank[at(*key(t, n))[0]]
                        for c in range(2):
                            mm = product(dst[:, :], parts(aT, ALL, chunk + c, tok(t)),
                                         parts(w, ALL, slice(c * D + n * HALF, c * D + (n + 1) * HALF)),
                                         start=first and c == 0, stop=last and c == 1)
                        if last:
                            mm.then_inc(full_of(*key(t, n)), 1)
                if not last:
                    mm.then_inc(w_part, 1)

            def channels_out(name, aT, *key, turned=None):
                w = split_block(name)
                dst = open_bank(*key)
                for a in range(2):
                    for c in range(KC):
                        if turned and a == 0 and c % (KC // 2) == 0:
                            half_ready(turned, c // (KC // 2))
                        mm = product(dst[:, a * S:(a + 1) * S], parts(w, ALL, slice(c * S + a * P, c * S + (a + 1) * P)),
                                     parts(aT, ALL, c, ALL), start=(c == 0), stop=(c == KC - 1))
                mm.then_inc(full_of(*key), 1)

            def plain_channels_out(halves, aT, *key, first=0, width=S):
                dst = open_bank(*key)
                for a in range(2):
                    for c in range(KC):
                        w, o = halves[c // (KC // 2)], c % (KC // 2) * S + a * P
                        mm = nc.tensor.matmul(dst[:, a * width:(a + 1) * width], w[:, o:o + P],
                                              aT[:, c, first:first + width], start=(c == 0), stop=(c == KC - 1))
                mm.then_inc(full_of(*key), 1)

            aT = aT_hi, aT_lo
            nT = nT_hi, nT_lo

            pe.wait_ge(ident_loaded, 16)
            keep_warm(9, "xT", 0, 0)
            for t in range(NT):
                tile_T(0, "xT", xn, t)
            for n in (1, 2, 3, 4):
                for p in "ab":
                    tokens_out(f"in{n}{p}", aT, lambda t, n=n: ("proj", n, t), turned="xT" if n == 1 else None)
            for name, n, src in (("qT", 2, q_sb), ("kT", 3, k_sb)):
                for t in range(NT):
                    wait_read(pe, "proj", n, t)
                    transposes(src[:, t, :], name, t)

            def scores(u):
                dst = open_bank("score", u)
                t, heads = UNITS[u]
                w = HALF // len(heads)
                for a, h in enumerate(heads):
                    r, c = slice(HD * (h % 2), HD * (h % 2) + HD), h // 2
                    mm = nc.tensor.matmul(dst[:, a * w:(a + 1) * w], qT[r, c, tok(t)], kT[r, c, 0:w], start=True, stop=True)
                mm.then_inc(full_of("score", u), 1)

            for name in ("qT", "kT"):
                for t in range(NT):
                    wait_read(pe, name, t)
            scores(0)
            scores(1)
            scores(2)
            for p in "ab":
                tokens_out(f"in0{p}", aT, lambda t: ("proj", 0, t))
            for t in range(NT):
                wait_read(pe, "proj", 4, t)
            pe.wait_ge(w_masked, 1)
            for u in range(len(UNITS)):
                t, heads = UNITS[u]
                if 3 <= u + 2 < len(UNITS):
                    scores(u + 2)
                pe.wait_ge(prob_ready, u + 1)
                transposes(prob[:, u % 3, :], "pT", u)
                if u == 0:
                    both_oT = [open_bank("oT", c) for c in range(2)]
                if u in (1, 3):
                    m = u // 2
                    pe.wait_ge(v_normed, m + 1)
                    dst = open_bank("spatial", m)
                    for g in range(8):
                        mm = nc.tensor.matmul(dst[:, g * GD:(g + 1) * GD], w_sT[:, g, :], vg[:, m, g * GD:(g + 1) * GD],
                                              start=True, stop=True)
                    mm.then_inc(full_of("spatial", m), 1)
                wait_read(pe, "pT", u)
                for a, h in enumerate(heads):
                    r, off = slice(HD * (h % 2), HD * (h % 2) + HD), S * (h // 2 % 2) + t * P
                    for kt in range(t + 1):
                        piece = a * (t + 1) + kt
                        mm = nc.tensor.matmul(both_oT[h // 4][r, off:off + P], v_sb[:, kt, h * HD:(h + 1) * HD],
                                              probT[:, u % 2, piece * P:(piece + 1) * P], start=(kt == 0), stop=(kt == t))
                mm.then_inc(full_of("oT", HEADS_DONE.index(u)) if u in HEADS_DONE else unit_part, 1)
                if u in (4, 5):
                    m = u - 4
                    wait_read(pe, "spatial", m)
                    transposes(u_sb[:, m, :], "aT", m)
            def mix(n, p, t):
                tokens_out(f"out{n}{p}", aT, lambda t: ("w_out", n, t), tiles=(t,))

            def router(j, tiles=(0, 1)):
                q_key, r_key = (("query0",), ("route0",)) if tiles == (0,) else (("query", j), ("route", j))
                plain_channels_out(wait_halves(pe, f"query{j}"), bT, *q_key, first=tiles[0] * P, width=len(tiles) * P)
                dst = open_bank(*r_key)
                wait_read(pe, *q_key)
                for i, t in enumerate(tiles):
                    for p in range(2):
                        o = i * S + p * NKEYS
                        mm = nc.tensor.matmul(dst[:, o:o + NKEYS], q2T[:, j % 2, p, tok(t)], sub_kT[:, 2 * j + p, :],
                                              start=True, stop=True)
                mm.then_inc(full_of(*r_key), 1)

            def router_input(t):
                tile_T(2, "xbT", xn, t)

            wait_read(pe, "aT", 0)
            mix(0, "a", 0)
            for c in range(2):
                wait_read(pe, "oT", c)
            mix(0, "b", 0)
            for p in "ab":
                mix(1, p, 0)
            wait_read(pe, "aT", 1)
            mix(0, "a", 1)
            router_input(0)
            pe.wait_ge(subk_loaded, 16)
            for h in range(2):
                wait_read(pe, "xbT", 0, h)
            router(0, (0,))
            mix(0, "b", 1)
            for p in "ab":
                mix(1, p, 1)
            router_input(1)
            for h in range(2):
                wait_read(pe, "xbT", 1, h)
            router(0, (1,))

            def after(head):
                if AHEAD + head < PEER_HEADS:
                    router(AHEAD + head)
                else:
                    for t in range(NT):
                        tile_T(1, "memT", mem_n, t)
                    T_ready("memT")
                    plain_channels_out(wait_halves(pe, "mem_k"), bT, "mk")
                    w = wait_loaded(pe, "mem_v")
                    dst = open_bank("mv")
                    for t in range(NT):
                        for c in range(KC):
                            mm = nc.tensor.matmul(dst[:, t * S:(t + 1) * S], bT[:, c, tok(t)], w[:, c * S:(c + 1) * S],
                                                  start=(c == 0), stop=(c == KC - 1))
                    mm.then_inc(full_of("mv"), 1)

            for j in range(1, AHEAD):
                router(j)

            def add_rows(acc, t, head, ks, start=False, stop=False):
                for n_row, k in enumerate(ks):
                    pe.wait_ge(v_loaded[k % RING], head * 32 + 16 * (k // RING) + 16)
                    pe.wait_ge(diag_ready, head * TOPK + (n_row if stop else k) + 1)
                    ends = stop and k == ks[-1]
                    for n in range(2):
                        mm = nc.tensor.matmul(acc[n][:, :], diag[:, k % RING, :], v_ring[:, k % RING, half(n)],
                                              start=start and n_row == 0, stop=ends)
                        if ends:
                            mm.then_inc(full_of("expert", t, n), 1)
                    if not ends:
                        mm.then_inc(v_used, 1)

            acc = [open_bank("expert", 0, n) for n in range(2)]
            for head in range(PEELED):
                add_rows(acc, 0, head, range(TOPK), start=(head == 0))
                after(head)
            with pe.Fori(0, (PEER_HEADS - PEELED) // 2) as i:
                for hh in range(2):
                    add_rows(acc, 0, PEELED + i * 2 + hh, range(TOPK))
            pe.wait_ge(const_loaded, 16)
            for n in range(2):
                nc.tensor.matmul(acc[n][:, :], zeros, const[:, 0:HALF], start=False,
                                 stop=True).then_inc(full_of("expert", 0, n), 1)
            acc = [open_bank("expert", 1, n) for n in range(2)]
            add_rows(acc, 1, PEER_HEADS, range(TOPK), start=True)
            tile_T(3, "nT", xn, 0)
            add_rows(acc, 1, PEER_HEADS + 1, range(TOPK))
            with pe.Fori(0, PEER_HEADS // 2 - 2) as i:
                for hh in range(2):
                    add_rows(acc, 1, PEER_HEADS + 2 + i * 2 + hh, range(TOPK))
            last = NT * PEER_HEADS - 1
            add_rows(acc, 1, last - 1, range(TOPK))
            add_rows(acc, 1, last, PE_ROWS, stop=True)
            keep_warm(14, "nT", 1, 0)
            tile_T(3, "nT", xn, 1)

            for key in ("q2", "k2"):
                for c in range(2):
                    channels_out(f"in2_{key[0]}{c}", nT, key, c, turned="nT" if (key, c) == ("q2", 0) else None)
            for key in ("q2", "k2"):
                for c in range(2):
                    wait_read(pe, key, c)
            for i, name in enumerate(SLOT_BLOCKS):
                z, cum, attend = pair_at(i, Z_SLOT), pair_at(i, CUM_SLOT), pair_at(i, ATT_SLOT)
                if attend is not None:
                    dst = open_bank("sbT", attend)
                    if attend == 0:
                        for t in range(NT):
                            wait_read(pe, "v2", t)
                    pe.wait_ge(att_ready, attend + 1)
                    for a in range(2):
                        g, r = 2 * attend + a, slice(HD * a, HD * a + HD)
                        nc.tensor.matmul(dst[r, 0:S], v3[:, 0, g * HD:(g + 1) * HD], att[:, a, 0:S], start=True, stop=False)
                        mm = nc.tensor.matmul(dst[r, P:S], v3[:, 1, g * HD:(g + 1) * HD], att[:, a, S:384],
                                              start=False, stop=True)
                    mm.then_inc(full_of("sbT", attend), 1)
                if cum is not None:
                    pe.wait_ge(l_ready, cum + 1)
                    for a in range(2):
                        dst = bank[at("z", 2 * cum + a)[0]]
                        nc.tensor.matmul(dst[:, 0:S], negtri, sp_l[:, a, 0:S], start=False, stop=False,
                                         skip_group_check=True)
                        nc.tensor.matmul(dst[:, P:S], negones, sp_l[:, a, S:384], start=False, stop=False,
                                         skip_group_check=True)
                        mm = nc.tensor.matmul(dst[:, S:384], negtri, sp_l[:, a, S:384], start=False, stop=True,
                                              skip_group_check=True)
                    mm.then_inc(cumulated, 1)
                if z is not None:
                    for a in range(2):
                        dst = open_bank("z", 2 * z + a)
                        r = slice(HD * a, HD * a + HD)
                        nc.tensor.matmul(dst[:, 0:S], k3T[r, z, 0:P], q3T[r, z, 0:S], start=True, stop=False)
                        nc.tensor.matmul(dst[:, S:384], k3T[r, z, P:S], q3T[r, z, P:S], start=False,
                                         stop=True).then_inc(full_of("z", 2 * z + a), 1)
                if i in XS_SLOT:
                    t = XS_SLOT.index(i)
                    wait_read(pe, "xq")
                    wait_read(pe, "mk")
                    for j in range(2):
                        dst = open_bank("xs", t, j)
                        r = slice(HD * j, HD * j + HD)
                        for a in range(2):
                            mm = nc.tensor.matmul(dst[:, a * S:(a + 1) * S], xqT[r, a, tok(t)], mkT[r, a, :],
                                                  start=True, stop=True)
                        mm.then_inc(full_of("xs", t, j), 1)
                if i in MIX_SLOT:
                    c = MIX_SLOT.index(i)
                    pe.wait_ge(pool_loaded, 32)
                    for t in range(NT):
                        wait_read(pe, "pool_in", t)
                    dst = open_bank("mix", c)
                    for a in range(2):
                        g = 2 * c + a
                        nc.tensor.matmul(dst[:, a * S:(a + 1) * S], p_sb[:, 0, g * P:(g + 1) * P], band[:, g, 0:S],
                                         start=True, stop=False)
                        mm = nc.tensor.matmul(dst[:, a * S + P:(a + 1) * S], p_sb[:, 1, g * P:(g + 1) * P],
                                              band[:, g, S:384], start=False, stop=True)
                    mm.then_inc(full_of("mix", c), 1)
                if i in POOL_SLOT:
                    c = POOL_SLOT.index(i)
                    dst = open_bank("poolT", c)
                    wait_read(pe, "mix", c)
                    for a in range(2):
                        g = 2 * c + a
                        mm = nc.tensor.matmul(dst[:, a * S:(a + 1) * S], w_mix[:, g, :], mixT[:, g, :],
                                              start=True, stop=True)
                    mm.then_inc(full_of("poolT", c), 1)
                h = i - XO_SLOT
                if 0 <= h < XHEADS:
                    c, a = h // 2, h % 2
                    dst_x = bank[at("xoT", c)[0]] if a else open_bank("xoT", c)
                    wait_read(pe, "xpT", h)
                    wait_read(pe, "mv")
                    for m in range(2):
                        mm = nc.tensor.matmul(dst_x[HD * a:HD * a + HD, 0:S], mv[:, m, h * HD:(h + 1) * HD],
                                              xpT[:, h % 2, m * S:(m + 1) * S], start=(m == 0), stop=(m == 1))
                    mm.then_inc(full_of("xoT", c) if a else even_x, 1)
                h = i - XPT_SLOT
                if 0 <= h < XHEADS:
                    if h == 0:
                        pe.wait_ge(xprob_ready, NT)
                    dst = open_bank("xpT", h)
                    for c in range(2):
                        for t in range(NT):
                            src = xprob[:, 4 * t + 2 * (h % 2) + h // 2, c * P:(c + 1) * P]
                            mm = nc.tensor.transpose(dst[:, c * S + t * P:c * S + (t + 1) * P], src, ident)
                    mm.then_inc(full_of("xpT", h), 1)
                if name == "in2_x":
                    channels_out(name, nT, "xq")
                else:
                    tokens_out(name, nT, lambda t: slot_key(name, t))
            for key, name, src, n_blocks, ready in (
                    ("y_x", "x_o", (xoT_hi, xoT_lo), 1, "xoT"), ("y_pool", "pool_o", (poolT_hi, poolT_lo), 2, "poolT"),
                    ("y_sb", "sb_o", (sbT_hi, sbT_lo), 2, "sbT")):
                for c in range(4 if ready == "sbT" else 2):
                    wait_read(pe, ready, c)
                for b in range(n_blocks):
                    rows_out(f"{name}{b}" if n_blocks > 1 else name, src, b == 0, b == n_blocks - 1, 2 * b,
                             lambda t, n: (key, t, n))
            for t in range(NT):
                pe.wait_ge(merged_ready, 2 * t + 2)
                for h in range(2):
                    transposes(xn[:, t, half(h)], "mergedT", t, h)
            for n in range(2):
                for p in "ab":
                    tokens_out(f"out2_{n}{p}", nT, lambda t: ("w_out2", n, t), turned="mergedT" if n == 0 else None)
            keep_warm(22, "n2T", 0, 0)
            for t in range(NT):
                tile_T(5, "n2T", xn, t)
            for j in range(FC):
                channels_out(f"ff_in{j}", nT, "ff", j, turned="n2T" if j == 0 else None)
            for j in range(FC // 2):
                pe.wait_ge(ffT_ready, 2 * j + 2)
                rows_out(f"ff_out{j}", (hT_hi, hT_lo), j == 0, j == FC // 2 - 1, 2 * j, lambda t, n: ("ff_out", t, n))


def position_constants():
    import numpy as np

    key, query = np.arange(P)[:, None], np.arange(P)[None, :]
    before = (key < query).astype(np.float32)
    mask = np.concatenate([before, np.ones((P, P), np.float32), before], 1)
    const = np.concatenate([np.eye(P), -(key >= query).astype(np.float32), -np.ones((P, P)),
                            mask, np.where(mask > 0, 0.0, NEG), np.zeros((P, P))], 1)
    band = np.zeros((2 * P, 4, S), np.float32)
    s, t = np.arange(S)[:, None], np.arange(S)[None, :]
    for g, w in enumerate((2, 4, 8, 16)):
        inside = (s <= t) & (s > t - w)
        band[:, g] = inside / np.minimum(t + 1, w).astype(np.float32) - (s == t)
    band = np.concatenate([band[0:P], band[P:, :, P:]], 2)
    return const.astype(np.float32), band.astype(np.float32)


def lay_out(inputs):
    import numpy as np

    a = {k: np.asarray(v) for k, v in inputs.items()}
    a = {k: (v if k in ("x", "mem_2") else v[0]) for k, v in a.items()}
    io = {}

    def blocks(w, names, width=HALF):
        k = w.shape[0] // P
        for n, name in enumerate(names):
            part = w[:, n * width:(n + 1) * width].reshape(k, P, width)
            io[name] = part.transpose(1, 0, 2).reshape(P, k * width)

    def halves(w, name):
        for n, part in enumerate("ab"):
            blocks(w[n * HALF:(n + 1) * HALF], [name + part])

    def rows(w, names):
        for n, name in enumerate(names):
            blocks(w[n * S:(n + 1) * S], [name], D)

    io["x"] = a["x"][0]
    for n in range(5):
        halves(a["w_in"][:, n * HALF:(n + 1) * HALF], f"in{n}")
    for n in range(2):
        halves(a["w_out"][:, n * HALF:(n + 1) * HALF], f"out{n}")
        halves(a["w_out_2"][:, n * HALF:(n + 1) * HALF], f"out2_{n}")
    blocks(a["peer_w_query"], [f"query{j}" for j in range(PEER_HEADS)], S)
    io["mem"] = a["mem_2"][0].reshape(NT, P, D).transpose(1, 0, 2).reshape(P, NT * D)
    blocks(a["w_mem_kv_2"], ["mem_k", "mem_v"], S)
    w = a["w_in_2"]
    halves(w[:, 0:512], "in2_p")
    blocks(w[:, 512:1536], ["in2_q0", "in2_q1", "in2_k0", "in2_k1"], S)
    halves(w[:, 1536:2048], "in2_v")
    blocks(w[:, 2048:2304], ["in2_x"], S)
    for n in range(N_GATES):
        halves(w[:, 2304 + n * HALF:2304 + (n + 1) * HALF], f"in2_g{n}")
    rows(a["w_pool_o_2"], ["pool_o0", "pool_o1"])
    rows(a["w_sb_o_2"], ["sb_o0", "sb_o1"])
    rows(a["w_x_o_2"], ["x_o"])
    w = a["w_ffn_in_2"].reshape(D, 2, FC, P).transpose(0, 2, 1, 3).reshape(D, 2 * DFF)
    blocks(w, [f"ff_in{j}" for j in range(FC)], S)
    rows(a["w_ffn_out_2"], [f"ff_out{j}" for j in range(FC // 2)])
    io["w_sT"] = a["gmlp_w_s"].transpose(2, 0, 1)
    rel = np.clip(P + np.arange(P)[:, None] - np.arange(S)[None, :], -P, P) + P
    io["rel"] = a["rel_bias"][list(BIAS_HEADS)][:, rel].transpose(1, 0, 2)
    io["sub_kT"] = a["peer_sub_keys"].reshape(HP, NKEYS, P).transpose(2, 0, 1)
    io["w_mix"] = a["w_pool_mix_2"].transpose(1, 0, 2)
    cols = np.zeros((P, 16), np.float32)
    cols[:, 0] = np.tile(a["q_norm_g"], 2)
    cols[:, 1] = np.tile(a["k_norm_g"], 2)
    cols[:, 2:10] = a["gmlp_b_s"].T
    cols[:, 10:14] = a["pool_scale_2"].reshape(4, P).T
    io["cols"] = cols
    for name in ("ln_mix_g", "gmlp_norm_g", "ln_ffn_g", "norm_mix_pre_2", "norm_mem_2", "norm_mix_post_2",
                 "norm_ffn_pre_2", "norm_ffn_post_2", "peer_u", "peer_v"):
        io[name] = a[name]
    io["const"], io["band"] = position_constants()
    return {k: np.ascontiguousarray(v) for k, v in io.items()}


def kernel(**inputs):
    import concourse.bacc as bacc
    from concourse.bass_utils import run_bass_kernel_spmd

    nc = bacc.Bacc("TRN2", target_bir_lowering=False, num_devices=1)
    arrays = lay_out(inputs)
    io = {k: nc.dram_tensor("in_" + k, v.shape, mybir.dt.from_np(v.dtype), kind="ExternalInput").ap() for k, v in arrays.items()}
    out = nc.dram_tensor("out_y", (S, D), F32, kind="ExternalOutput").ap()
    two_block_kernel(nc, io, out)
    r = run_bass_kernel_spmd(nc, [{"in_" + k: v for k, v in arrays.items()}], core_ids=[0])
    return r.results[0]["out_y"].reshape(1, S, D)
```
